# Optimizing a Trainium2 kernel written in Bass

```python
import math
import jax, jax.numpy as jnp
from jax import lax
import numpy as np

D_MODEL = 1024
BATCH = 1
SEQ = 512
DEPTH = 1

ATTN_HEADS = 8
ATTN_HEAD_DIM = 64
ATTN_WIDTH = ATTN_HEADS * ATTN_HEAD_DIM
KV_RANK = 256
IDX_HEADS = 8
IDX_DIM = 64
TOPK_MAX = 256
ATTN_QBLOCK = 64
N_BUCKETS = 32
MAX_DISTANCE = 128
SSM_HEADS = 16
SSM_HEAD_DIM = 64
SSM_INNER = SSM_HEADS * SSM_HEAD_DIM
SSM_GROUPS = 2
SSM_STATE = 128
CONV_WIDTH = 4
CONV_CH = SSM_INNER + 2 * SSM_GROUPS * SSM_STATE
SSD_CHUNK = 128
N_EXPERTS = 32
TOP_K = 4
D_EXPERT = D_MODEL
SWIGLU_LIMIT = 7.0
SWIGLU_ALPHA = 1.702
MOE_BLOCK = 128
EPS = 1e-6

SPLIT_SIZES = (ATTN_WIDTH, KV_RANK, IDX_HEADS * IDX_DIM, IDX_DIM, IDX_HEADS, SSM_INNER, CONV_CH, SSM_HEADS, 2 * D_MODEL)
D_IN = sum(SPLIT_SIZES)


def _rms(x, g, eps=EPS):
    xf = x.astype(jnp.float32)
    y = xf * lax.rsqrt(jnp.mean(xf * xf, axis=-1, keepdims=True) + eps)
    return (y * g.astype(jnp.float32)).astype(x.dtype)

def _layernorm(x, g, b, eps=EPS):
    xf = x.astype(jnp.float32)
    mu = jnp.mean(xf, axis=-1, keepdims=True)
    var = jnp.mean(jnp.square(xf - mu), axis=-1, keepdims=True)
    y = (xf - mu) * lax.rsqrt(var + eps) * g.astype(jnp.float32) + b.astype(jnp.float32)
    return y.astype(x.dtype)

def _t5_bucket(dist):
    n = jnp.maximum(dist, 0)
    max_exact = N_BUCKETS // 2
    nf = jnp.maximum(n, 1).astype(jnp.float32)
    large = max_exact + (jnp.log(nf / max_exact) / math.log(MAX_DISTANCE / max_exact) * (N_BUCKETS - max_exact)).astype(jnp.int32)
    large = jnp.minimum(large, N_BUCKETS - 1)
    return jnp.where(n < max_exact, n, large)

def _split(proj):
    idx = [int(i) for i in np.cumsum(SPLIT_SIZES)[:-1]]
    return jnp.split(proj, idx, axis=-1)

def _dsa_attention(q, k, v, q_idx, w_idx, k_idx, rel_bias):
    Bsz, L = q.shape[0], q.shape[1]
    topk = min(TOPK_MAX, L // 4)
    nblk = L // ATTN_QBLOCK
    scale = ATTN_HEAD_DIM ** -0.5
    key_pos = jnp.arange(L, dtype=jnp.int32)

    def to_blocks(a):
        return jnp.moveaxis(a.reshape(Bsz, nblk, ATTN_QBLOCK, *a.shape[2:]), 1, 0)

    def block(args):
        qb, qib, wib, start = args
        t = start + jnp.arange(ATTN_QBLOCK, dtype=jnp.int32)
        dots = jnp.einsum('bqhd,bsd->bqhs', qib, k_idx)
        score = jnp.einsum('bqh,bqhs->bqs', wib, jax.nn.relu(dots)).astype(jnp.float32)
        causal = key_pos[None, :] <= t[:, None]
        score = jnp.where(causal[None], score, -jnp.inf)
        _, sel = lax.top_k(score, topk)
        kg = jax.vmap(lambda kk, ii: kk[ii])(k, sel)
        vg = jax.vmap(lambda vv, ii: vv[ii])(v, sel)
        dist = t[None, :, None] - sel
        bias = jnp.moveaxis(rel_bias[_t5_bucket(dist)], -1, 2).astype(jnp.float32)
        logits = jnp.einsum('bqhd,bqkhd->bqhk', qb, kg).astype(jnp.float32) * scale + bias
        logits = jnp.where((dist >= 0)[:, :, None, :], logits, -jnp.inf)
        p = jax.nn.softmax(logits, axis=-1).astype(vg.dtype)
        return jnp.einsum('bqhk,bqkhd->bqhd', p, vg)

    starts = jnp.arange(nblk, dtype=jnp.int32) * ATTN_QBLOCK
    out = lax.map(block, (to_blocks(q), to_blocks(q_idx), to_blocks(w_idx), starts))
    return jnp.moveaxis(out, 0, 1).reshape(Bsz, L, ATTN_WIDTH)

def _mamba2_ssd(z, xbc, dt_raw, conv_w, conv_b, dt_bias, a_log, d_skip, norm_w):
    Bsz, L = xbc.shape[0], xbc.shape[1]
    nc = L // SSD_CHUNK
    hg = SSM_HEADS // SSM_GROUPS
    xbc = lax.conv_general_dilated(xbc, conv_w[:, None, :].astype(xbc.dtype), window_strides=(1,),
                                   padding=[(CONV_WIDTH - 1, 0)], dimension_numbers=('NWC', 'WIO', 'NWC'),
                                   feature_group_count=CONV_CH) + conv_b
    xbc = jax.nn.silu(xbc).astype(jnp.float32)
    xs, bm, cm = jnp.split(xbc, [SSM_INNER, SSM_INNER + SSM_GROUPS * SSM_STATE], axis=-1)
    dt = jax.nn.softplus(dt_raw.astype(jnp.float32) + dt_bias.astype(jnp.float32))
    a = -jnp.exp(a_log.astype(jnp.float32)).reshape(SSM_GROUPS, hg)

    def chunks(arr, *tail):
        return jnp.moveaxis(arr.reshape(Bsz, nc, SSD_CHUNK, *tail), 1, 0)

    x_c = chunks(xs, SSM_GROUPS, hg, SSM_HEAD_DIM)
    dt_c = chunks(dt, SSM_GROUPS, hg)
    b_c = chunks(bm, SSM_GROUPS, SSM_STATE)
    c_c = chunks(cm, SSM_GROUPS, SSM_STATE)
    causal = jnp.tril(jnp.ones((SSD_CHUNK, SSD_CHUNK), dtype=bool))[None, :, :, None, None]

    def step(state, inp):
        xc, dtc, bc, cc = inp
        acum = jnp.cumsum(dtc * a, axis=1)
        seg = acum[:, :, None] - acum[:, None, :]
        lmat = jnp.exp(jnp.where(causal, seg, -jnp.inf))
        cb = jnp.einsum('bign,bjgn->bijg', cc, bc)
        wmat = cb[..., None] * lmat * dtc[:, None]
        y = jnp.einsum('bijgh,bjghp->bighp', wmat, xc)
        y = y + jnp.einsum('bign,bghpn->bighp', cc, state) * jnp.exp(acum)[..., None]
        decay = jnp.exp(acum[:, -1:] - acum) * dtc
        state = state * jnp.exp(acum[:, -1])[..., None, None] + jnp.einsum('bjgn,bjgh,bjghp->bghpn', bc, decay, xc)
        return state, y

    h0 = jnp.zeros((Bsz, SSM_GROUPS, hg, SSM_HEAD_DIM, SSM_STATE), jnp.float32)
    _, ys = lax.scan(step, h0, (x_c, dt_c, b_c, c_c))
    y = jnp.moveaxis(ys, 0, 1).reshape(Bsz, L, SSM_HEADS, SSM_HEAD_DIM)
    y = y + d_skip.astype(jnp.float32)[:, None] * xs.reshape(Bsz, L, SSM_HEADS, SSM_HEAD_DIM)
    y = y.reshape(Bsz, L, SSM_INNER) * jax.nn.silu(z.astype(jnp.float32))
    yg = y.reshape(Bsz, L, SSM_GROUPS, SSM_INNER // SSM_GROUPS)
    yg = yg * lax.rsqrt(jnp.mean(yg * yg, axis=-1, keepdims=True) + EPS)
    y = yg.reshape(Bsz, L, SSM_INNER) * norm_w.astype(jnp.float32)
    return y.astype(z.dtype)

def _moe(h, w_router, b_router, w_gu, b_gu, w_dn, b_dn):
    Bsz, L, D = h.shape
    T = Bsz * L
    hf = h.reshape(T, D)
    logits = (hf @ w_router + b_router).astype(jnp.float32)
    top_val, top_idx = lax.top_k(logits, TOP_K)
    gates = jax.nn.softmax(top_val, axis=-1)
    n_assign = T * TOP_K
    e_flat = top_idx.reshape(n_assign)
    g_flat = gates.reshape(n_assign)
    tok_flat = jnp.arange(n_assign, dtype=jnp.int32) // TOP_K
    order = jnp.argsort(e_flat)
    e_sorted = e_flat[order]
    counts = jnp.bincount(e_flat, length=N_EXPERTS)
    padded = (counts + MOE_BLOCK - 1) // MOE_BLOCK * MOE_BLOCK
    pad_end = jnp.cumsum(padded)
    pad_start = pad_end - padded
    start = jnp.cumsum(counts) - counts
    rank = jnp.arange(n_assign, dtype=jnp.int32) - start[e_sorted]
    dest = pad_start[e_sorted] + rank
    n_rows = n_assign + N_EXPERTS * MOE_BLOCK
    row_tok = jnp.full((n_rows,), T, dtype=jnp.int32).at[dest].set(tok_flat[order])
    row_gate = jnp.zeros((n_rows,), jnp.float32).at[dest].set(g_flat[order])
    n_blk = n_rows // MOE_BLOCK
    blk_start = jnp.arange(n_blk, dtype=jnp.int32) * MOE_BLOCK
    blk_exp = jnp.minimum(jnp.sum(blk_start[:, None] >= pad_end[None, :], axis=1), N_EXPERTS - 1)
    h_pad = jnp.concatenate([hf, jnp.zeros((1, D), hf.dtype)], axis=0)

    def run_block(args):
        toks, e = args
        xb = h_pad[toks]
        gu = xb @ w_gu[e] + b_gu[e]
        g, u = gu[:, :D_EXPERT], gu[:, D_EXPERT:]
        g = jnp.minimum(g, SWIGLU_LIMIT)
        u = jnp.clip(u, -SWIGLU_LIMIT, SWIGLU_LIMIT)
        act = (u + 1.0) * (g * jax.nn.sigmoid(SWIGLU_ALPHA * g))
        return act @ w_dn[e] + b_dn[e]

    out = lax.map(run_block, (row_tok.reshape(n_blk, MOE_BLOCK), blk_exp))
    out = out.reshape(n_rows, D) * row_gate[:, None].astype(out.dtype)
    y = jax.ops.segment_sum(out, row_tok, num_segments=T + 1)[:T]
    return y.reshape(Bsz, L, D)

def first_inputs(seed: int = 0) -> dict:
    key = jax.random.key(seed)
    ks = jax.random.split(key, 32)
    f32 = jnp.float32

    def nrm(k, shape, scale):
        return jax.random.normal(k, shape, f32) * scale

    def gain(k, shape):
        return 1.0 + 0.05 * jax.random.normal(k, shape, f32)

    dt = jnp.exp(jax.random.uniform(ks[17], (DEPTH, SSM_HEADS), f32, math.log(1e-3), math.log(1e-1)))
    return {
        'x': nrm(ks[0], (BATCH, SEQ, D_MODEL), 1.0),
        'c': nrm(ks[1], (BATCH, D_MODEL), 1.0),
        'rel_bias': nrm(ks[2], (N_BUCKETS, ATTN_HEADS), 0.5),
        'w_ada': nrm(ks[3], (DEPTH, D_MODEL, 6 * D_MODEL), 0.5 * D_MODEL ** -0.5),
        'b_ada': nrm(ks[4], (DEPTH, 6 * D_MODEL), 0.02),
        'norm_mix': gain(ks[5], (DEPTH, D_MODEL)),
        'norm_ffn': gain(ks[6], (DEPTH, D_MODEL)),
        'w_in': nrm(ks[7], (DEPTH, D_MODEL, D_IN), D_MODEL ** -0.5),
        'kv_norm': gain(ks[8], (DEPTH, KV_RANK)),
        'w_kv_up': nrm(ks[9], (DEPTH, KV_RANK, 2 * ATTN_WIDTH), KV_RANK ** -0.5),
        'q_norm': gain(ks[10], (DEPTH, ATTN_HEAD_DIM)),
        'k_norm': gain(ks[11], (DEPTH, ATTN_HEAD_DIM)),
        'idx_k_ln_w': gain(ks[12], (DEPTH, IDX_DIM)),
        'idx_k_ln_b': nrm(ks[13], (DEPTH, IDX_DIM), 0.02),
        'w_attn_o': nrm(ks[14], (DEPTH, ATTN_WIDTH, D_MODEL), ATTN_WIDTH ** -0.5),
        'conv_w': nrm(ks[15], (DEPTH, CONV_WIDTH, CONV_CH), CONV_WIDTH ** -0.5),
        'conv_b': nrm(ks[16], (DEPTH, CONV_CH), 0.02),
        'dt_bias': dt + jnp.log(-jnp.expm1(-dt)),
        'a_log': jnp.log(jax.random.uniform(ks[18], (DEPTH, SSM_HEADS), f32, 1.0, 16.0)),
        'd_skip': gain(ks[19], (DEPTH, SSM_HEADS)),
        'ssm_norm': gain(ks[20], (DEPTH, SSM_INNER)),
        'w_ssm_o': nrm(ks[21], (DEPTH, SSM_INNER, D_MODEL), SSM_INNER ** -0.5),
        'w_out': nrm(ks[22], (DEPTH, D_MODEL, D_MODEL), D_MODEL ** -0.5),
        'w_router': nrm(ks[23], (DEPTH, D_MODEL, N_EXPERTS), D_MODEL ** -0.5),
        'b_router': nrm(ks[24], (DEPTH, N_EXPERTS), 0.01),
        'w_gu': nrm(ks[25], (DEPTH, N_EXPERTS, D_MODEL, 2 * D_EXPERT), D_MODEL ** -0.5),
        'b_gu': nrm(ks[26], (DEPTH, N_EXPERTS, 2 * D_EXPERT), 0.02),
        'w_dn': nrm(ks[27], (DEPTH, N_EXPERTS, D_EXPERT, D_MODEL), D_EXPERT ** -0.5),
        'b_dn': nrm(ks[28], (DEPTH, N_EXPERTS, D_MODEL), 0.02),
    }

def first_block(x, c, rel_bias, w_ada, b_ada, norm_mix, norm_ffn, w_in, kv_norm, w_kv_up, q_norm, k_norm,
              idx_k_ln_w, idx_k_ln_b, w_attn_o, conv_w, conv_b, dt_bias, a_log, d_skip, ssm_norm, w_ssm_o,
              w_out, w_router, b_router, w_gu, b_gu, w_dn, b_dn):
    Bsz, L, _ = x.shape
    cond = jax.nn.silu(c)
    for l in range(DEPTH):
        mod = cond @ w_ada[l] + b_ada[l]
        sh_m, sc_m, g_m, sh_f, sc_f, g_f = jnp.split(mod[:, None, :], 6, axis=-1)
        h = _rms(x, norm_mix[l]) * (1.0 + sc_m) + sh_m
        proj = h @ w_in[l]
        q, kv_lat, q_i, k_i, w_i, z, xbc, dt_raw, gate_logits = _split(proj)
        q = _rms(q.reshape(Bsz, L, ATTN_HEADS, ATTN_HEAD_DIM), q_norm[l])
        kv = _rms(kv_lat, kv_norm[l]) @ w_kv_up[l]
        k, v = jnp.split(kv, 2, axis=-1)
        k = _rms(k.reshape(Bsz, L, ATTN_HEADS, ATTN_HEAD_DIM), k_norm[l])
        v = v.reshape(Bsz, L, ATTN_HEADS, ATTN_HEAD_DIM)
        q_i = q_i.reshape(Bsz, L, IDX_HEADS, IDX_DIM) * (IDX_DIM ** -0.5)
        w_i = w_i * (IDX_HEADS ** -0.5)
        k_i = _layernorm(k_i, idx_k_ln_w[l], idx_k_ln_b[l])
        y_attn = _dsa_attention(q, k, v, q_i, w_i, k_i, rel_bias) @ w_attn_o[l]
        y_ssd = _mamba2_ssd(z, xbc, dt_raw, conv_w[l], conv_b[l], dt_bias[l], a_log[l], d_skip[l], ssm_norm[l]) @ w_ssm_o[l]
        g_attn, g_ssd = jnp.split(gate_logits, 2, axis=-1)
        mixed = jax.nn.sigmoid(g_attn) * y_attn + jax.nn.sigmoid(g_ssd) * y_ssd
        x = x + g_m * (mixed @ w_out[l])
        h = _rms(x, norm_ffn[l]) * (1.0 + sc_f) + sh_f
        x = x + g_f * _moe(h, w_router[l], b_router[l], w_gu[l], b_gu[l], w_dn[l], b_dn[l])
    return x


DEPTH_2 = 2

N_MIXERS = 2
RMS_EPS = 1e-6
LN_EPS = 1e-5
CHUNK = 128
A_WIDTH = 2 * D_MODEL
A_GROUPS = 8
A_GROUP_DIM = A_WIDTH // A_GROUPS
B_WIDTH = 3 * D_MODEL // 2
B_HEADS = 12
B_HEAD_DIM = B_WIDTH // B_HEADS
RG_C = 8.0

N_A_LAYERS = (DEPTH_2 + 1) // 2
N_B_LAYERS = DEPTH_2 // 2


def rms_norm(x, w):
    xf = x.astype(jnp.float32)
    y = xf * lax.rsqrt(jnp.mean(xf * xf, axis=-1, keepdims=True) + RMS_EPS)
    return (y * w.astype(jnp.float32)).astype(x.dtype)

def layer_norm(x, w, b):
    xf = x.astype(jnp.float32)
    mu = jnp.mean(xf, axis=-1, keepdims=True)
    var = jnp.mean(jnp.square(xf - mu), axis=-1, keepdims=True)
    y = (xf - mu) * lax.rsqrt(var + LN_EPS)
    return (y * w.astype(jnp.float32) + b.astype(jnp.float32)).astype(x.dtype)

def chunked_sgu_mixer(h, w_in, ln_w, ln_b, w_s, b_s, w_out):
    B, S, _ = h.shape
    z = h @ w_in
    u, v, g = jnp.split(z, 3, axis=-1)
    u = jax.nn.gelu(u)
    v = layer_norm(jax.nn.gelu(v), ln_w, ln_b)
    v = v.reshape(B, S // CHUNK, CHUNK, A_GROUPS, A_GROUP_DIM)
    causal = jnp.tril(jnp.ones((CHUNK, CHUNK), dtype=w_s.dtype))
    w_causal = w_s * causal[None]
    s = jnp.einsum('gts,bnsgc->bntgc', w_causal, v) + b_s.T[None, None, :, :, None]
    y = u * s.reshape(B, S, A_WIDTH) * jax.nn.silu(g)
    return y @ w_out

def _linear_combine(left, right):
    a_l, b_l = left
    a_r, b_r = right
    return a_l * a_r, a_r * b_l + b_r

def rglru_mixer(h, w_in, conv_w, conv_b, gate_a_w, gate_a_b, gate_x_w, gate_x_b, lam, w_out):
    B, S, _ = h.shape
    xb, g = jnp.split(h @ w_in, 2, axis=-1)
    xp = jnp.pad(xb, ((0, 0), (CONV_WIDTH - 1, 0), (0, 0)))
    xc = conv_b + conv_w[CONV_WIDTH - 1] * xp[:, CONV_WIDTH - 1:CONV_WIDTH - 1 + S]
    for k in range(CONV_WIDTH - 1):
        xc = xc + conv_w[k] * xp[:, k:k + S]
    xh = xc.reshape(B, S, B_HEADS, B_HEAD_DIM)
    r = jax.nn.sigmoid(jnp.einsum('bshi,hij->bshj', xh, gate_a_w).reshape(B, S, B_WIDTH) + gate_a_b)
    i = jax.nn.sigmoid(jnp.einsum('bshi,hij->bshj', xh, gate_x_w).reshape(B, S, B_WIDTH) + gate_x_b)
    log_a = -RG_C * r.astype(jnp.float32) * jax.nn.softplus(-lam.astype(jnp.float32))
    a = jnp.exp(log_a)
    mult = jnp.sqrt(-jnp.expm1(2.0 * log_a))
    bterm = mult * (i * xc).astype(jnp.float32)
    _, hseq = lax.associative_scan(_linear_combine, (a, bterm), axis=1)
    y = hseq.astype(h.dtype) * jax.nn.silu(g)
    return y @ w_out

def second_inputs(seed: int = 0) -> dict:
    key = jax.random.key(seed)
    ks = jax.random.split(key, 20)
    f32 = jnp.float32
    x = jax.random.normal(ks[0], (BATCH, SEQ, D_MODEL), f32)
    norm_w = 1.0 + 0.05 * jax.random.normal(ks[1], (DEPTH_2, D_MODEL), f32)
    a_w_in = jax.random.normal(ks[2], (N_A_LAYERS, D_MODEL, 3 * A_WIDTH), f32) * D_MODEL ** -0.5
    a_ln_w = 1.0 + 0.05 * jax.random.normal(ks[3], (N_A_LAYERS, A_WIDTH), f32)
    a_ln_b = 0.02 * jax.random.normal(ks[4], (N_A_LAYERS, A_WIDTH), f32)
    a_w_s = jax.random.normal(ks[5], (N_A_LAYERS, A_GROUPS, CHUNK, CHUNK), f32) * CHUNK ** -0.5
    a_b_s = 1.0 + 0.05 * jax.random.normal(ks[6], (N_A_LAYERS, A_GROUPS, CHUNK), f32)
    a_w_out = jax.random.normal(ks[7], (N_A_LAYERS, A_WIDTH, D_MODEL), f32) * A_WIDTH ** -0.5
    b_w_in = jax.random.normal(ks[8], (N_B_LAYERS, D_MODEL, 2 * B_WIDTH), f32) * D_MODEL ** -0.5
    b_conv_w = jax.random.normal(ks[9], (N_B_LAYERS, CONV_WIDTH, B_WIDTH), f32) * CONV_WIDTH ** -0.5
    b_conv_b = 0.02 * jax.random.normal(ks[10], (N_B_LAYERS, B_WIDTH), f32)
    b_gate_a_w = jax.random.normal(ks[11], (N_B_LAYERS, B_HEADS, B_HEAD_DIM, B_HEAD_DIM), f32) * B_HEAD_DIM ** -0.5
    b_gate_a_b = 0.02 * jax.random.normal(ks[12], (N_B_LAYERS, B_WIDTH), f32)
    b_gate_x_w = jax.random.normal(ks[13], (N_B_LAYERS, B_HEADS, B_HEAD_DIM, B_HEAD_DIM), f32) * B_HEAD_DIM ** -0.5
    b_gate_x_b = 0.02 * jax.random.normal(ks[14], (N_B_LAYERS, B_WIDTH), f32)
    a_c = jax.random.uniform(ks[15], (N_B_LAYERS, B_WIDTH), f32, minval=0.9, maxval=0.999)
    a0 = a_c ** (1.0 / RG_C)
    b_lambda = jnp.log(a0) - jnp.log1p(-a0)
    b_w_out = jax.random.normal(ks[16], (N_B_LAYERS, B_WIDTH, D_MODEL), f32) * B_WIDTH ** -0.5
    norm_f_w = 1.0 + 0.05 * jax.random.normal(ks[17], (D_MODEL,), f32)
    return {
        "x": x, "norm_w": norm_w,
        "a_w_in": a_w_in, "a_ln_w": a_ln_w, "a_ln_b": a_ln_b,
        "a_w_s": a_w_s, "a_b_s": a_b_s, "a_w_out": a_w_out,
        "b_w_in": b_w_in, "b_conv_w": b_conv_w, "b_conv_b": b_conv_b,
        "b_gate_a_w": b_gate_a_w, "b_gate_a_b": b_gate_a_b,
        "b_gate_x_w": b_gate_x_w, "b_gate_x_b": b_gate_x_b,
        "b_lambda": b_lambda, "b_w_out": b_w_out,
        "norm_f_w": norm_f_w,
    }

def second_block(x, norm_w, a_w_in, a_ln_w, a_ln_b, a_w_s, a_b_s, a_w_out,
              b_w_in, b_conv_w, b_conv_b, b_gate_a_w, b_gate_a_b,
              b_gate_x_w, b_gate_x_b, b_lambda, b_w_out, norm_f_w):
    for layer in range(DEPTH_2):
        h = rms_norm(x, norm_w[layer])
        j = layer // N_MIXERS
        if layer % N_MIXERS == 0:
            y = chunked_sgu_mixer(h, a_w_in[j], a_ln_w[j], a_ln_b[j], a_w_s[j], a_b_s[j], a_w_out[j])
        else:
            y = rglru_mixer(h, b_w_in[j], b_conv_w[j], b_conv_b[j], b_gate_a_w[j], b_gate_a_b[j],
                            b_gate_x_w[j], b_gate_x_b[j], b_lambda[j], b_w_out[j])
        x = x + y
    return rms_norm(x, norm_f_w)


def setup_inputs(seed=0):
    out = dict(first_inputs(seed))
    for name, value in second_inputs(seed + 1).items():
        if name != "x":
            out[name + "_2"] = value
    return out


def reference(
    x, c, rel_bias, w_ada, b_ada, norm_mix, norm_ffn, w_in, kv_norm, w_kv_up, q_norm, k_norm,
    idx_k_ln_w, idx_k_ln_b, w_attn_o, conv_w, conv_b, dt_bias, a_log, d_skip, ssm_norm, w_ssm_o,
    w_out, w_router, b_router, w_gu, b_gu, w_dn, b_dn, norm_w_2, a_w_in_2, a_ln_w_2, a_ln_b_2,
    a_w_s_2, a_b_s_2, a_w_out_2, b_w_in_2, b_conv_w_2, b_conv_b_2, b_gate_a_w_2, b_gate_a_b_2,
    b_gate_x_w_2, b_gate_x_b_2, b_lambda_2, b_w_out_2, norm_f_w_2,
):
    x = first_block(
        x, c, rel_bias, w_ada, b_ada, norm_mix, norm_ffn, w_in, kv_norm, w_kv_up, q_norm,
        k_norm, idx_k_ln_w, idx_k_ln_b, w_attn_o, conv_w, conv_b, dt_bias, a_log, d_skip,
        ssm_norm, w_ssm_o, w_out, w_router, b_router, w_gu, b_gu, w_dn, b_dn,
    )
    return second_block(
        x, norm_w_2, a_w_in_2, a_ln_w_2, a_ln_b_2, a_w_s_2, a_b_s_2, a_w_out_2, b_w_in_2,
        b_conv_w_2, b_conv_b_2, b_gate_a_w_2, b_gate_a_b_2, b_gate_x_w_2, b_gate_x_b_2,
        b_lambda_2, b_w_out_2, norm_f_w_2,
    )


_drawn_inputs = setup_inputs


def setup_inputs(seed=0):
    import zlib

    import numpy as np

    out = dict(_drawn_inputs(seed))
    spreads = {}
    factors = {'rel_bias': 2.952,
     'kv_norm': 8.0,
     'q_norm': 8.0,
     'k_norm': 8.0,
     'idx_k_ln_w': 8.0,
     'idx_k_ln_b': 8.0,
     'conv_b': 5.358,
     'd_skip': 19.211,
     'ssm_norm': 3.635,
     'b_router': 4.434,
     'b_gu': 8.0,
     'b_dn': 8.0,
     'a_ln_w_2': 4.409,
     'a_ln_b_2': 25.623,
     'a_b_s_2': 3.338,
     'b_gate_a_b_2': 64.0,
     'b_gate_x_b_2': 31.614}
    for name, (base, spread) in spreads.items():
        noise = np.random.default_rng([zlib.crc32(name.encode()), seed]).standard_normal(out[name].shape)
        drawn = base * np.exp(spread * noise) if base else spread * noise
        out[name] = __import__('jax').numpy.asarray(drawn.astype(out[name].dtype))
    for name, factor in factors.items():
        out[name] = (out[name] * factor).astype(out[name].dtype)
    return out
```

```python
import math
from contextlib import ExitStack

import numpy as np

import concourse.bass as bass
from concourse import mybir
from concourse.alu_op_type import AluOpType as ALU

F32, I32, BF16 = mybir.dt.float32, mybir.dt.int32, mybir.dt.bfloat16
ACT, AX = mybir.ActivationFunctionType, mybir.AxisListType

P = 128
T = 512
TT = T // P
D = 1024
DK = D // P
H, HD = 8, 64
TOPK = 128
NB, MAXD = 32, 128
SH, SP_ = 16, 64
SG, SN = 2, 128
CT = 12
E, EK = 32, 4
OB = T * EK // P
AW = 2048
BW = 1536
BT = BW // P
EPS, LN_EPS = 1e-6, 1e-5
NEG = -1.0e30
C_Q, C_KV, C_QI, C_KI, C_WI, C_Z, C_X, C_DT, C_G = 0, 512, 768, 1280, 1344, 1352, 2376, 3912, 3928
SLOT = 2048
RING = 6
ROOM = 28800

VEC = {}
for _name, _n in [("c", 8), ("b_ada", 48), ("norm_mix", 8), ("norm_ffn", 8), ("kv_norm", 2), ("conv_w", 48),
                  ("conv_b", 12), ("ssm_norm", 8), ("norm_w_2", 16), ("b_conv_w_2", 48), ("b_conv_b_2", 12),
                  ("b_gate_a_b_2", 12), ("b_gate_x_b_2", 12), ("b_lambda_2", 12), ("norm_f_w_2", 8),
                  ("q_norm", 1), ("k_norm", 1), ("idx_k_ln_w", 1), ("idx_k_ln_b", 1), ("d_skip", 8),
                  ("dt_bias", 16), ("a_log", 16), ("b_router", 32)]:
    VEC[_name] = (sum(n for _, n in VEC.values()), _n)
NVEC = sum(n for _, n in VEC.values())

CON = {}
for _name, _n in [("ident", P), ("ones", P), ("heads", P), ("tri", P), ("after", P), ("before", P),
                  ("causal", T), ("slot", P), ("flip", P), ("ebase", E), ("eone", E), ("tok", 2), ("bucket", T + P)]:
    CON[_name] = (sum(n for _, n in CON.values()), _n)
NCON = sum(n for _, n in CON.values())


def shape_constants():
    k = np.arange(P)
    out = np.zeros((P, NCON), np.float32)

    def put(name, value):
        a, n = CON[name]
        out[:value.shape[0], a:a + n] = value

    put("ident", np.eye(P))
    put("ones", np.ones((P, P)))
    put("heads", (k[:, None] // HD == k[None] // HD) * 1.0)
    put("tri", (k[:, None] <= k[None]) * 1.0)
    put("after", (k[:, None] > k[None]) * 1.0)
    put("before", (k[:, None] < k[None]) * 1.0)
    put("causal", np.where(np.arange(T)[None] <= k[:, None] + T - P, 0.0, NEG))
    put("slot", np.broadcast_to(k[None] * 1.0, (P, P)))
    put("flip", np.eye(P)[::-1])
    put("ebase", np.broadcast_to(np.arange(E)[None] * float(P), (P, E)))
    put("eone", np.broadcast_to(np.arange(E)[None] * 1.0, (P, E)))
    put("tok", np.stack([k * 1.0, np.ones(P)], 1))
    dist = np.maximum(T - 1 - np.arange(T + P), 0)
    nf = np.maximum(dist, 1).astype(np.float32)
    far = NB // 2 + (np.log(nf / (NB // 2)) / math.log(MAXD / (NB // 2)) * (NB - NB // 2)).astype(np.int32)
    bucket = np.where(dist < NB // 2, dist, np.minimum(far, NB - 1))
    put("bucket", (bucket[None] == np.arange(NB)[:, None]) * 1.0)
    return out


class Engine:

    def __init__(self, sem):
        self.sem, self.count, self.queue, self.seen = sem, 0, [], {}

    def do(self, after, issue):
        self.quiet(after, issue, self.sem)
        self.count += 1
        return (self.sem, self.count)

    def quiet(self, after, issue, sem=None, step=1):
        self.queue.append(([m for m in after if m], issue, sem, step))

    def mark(self):
        return (self.sem, self.count) if self.count else None

    def emit(self, eng, queue):
        seen = self.seen
        for marks, issue, sem, step in queue:
            for s, value in marks:
                if seen.get(s.name, 0) < value:
                    eng.wait_ge(s, value)
                    seen[s.name] = value
            if issue is not None:
                ins = issue(eng)
                if ins is not None and sem is not None:
                    ins.then_inc(sem, step)


class Buffers:

    def __init__(self, views):
        self.views, self.free, self.at = views, [[] for _ in views], -1

    def take(self):
        self.at = (self.at + 1) % len(self.views)
        return self.at, self.views[self.at], self.free[self.at]

    def release(self, i, *marks):
        self.free[i] = list(marks)


class Room:

    def __init__(self, view, start=0):
        self.view, self.at = view, start

    def take(self, *shape, dt=None):
        n = int(np.prod(shape[1:]))
        words = n if dt is not BF16 else (n + 1) // 2
        v = self.view[0:shape[0], self.at:self.at + words]
        self.at += (words + 7) // 8 * 8
        assert self.at <= ROOM, self.at
        if dt is not None:
            v = v.bitcast(dt)
        if len(shape) == 3:
            v = v.rearrange("p (a b) -> p a b", a=shape[1])
        elif len(shape) == 4:
            v = v.rearrange("p (a b c) -> p a b c", a=shape[1], b=shape[2])
        return v


class Load:

    def __init__(self, sem):
        self.sem, self.count = sem, 0

    def start(self, queue, after, out, in_, parts=1):
        self.count += 16
        queue.quiet(after, lambda e: e.dma_start(out, in_() if callable(in_) else in_), self.sem, 16)
        return (self.sem, self.count)


def build(nc, io, out, debug=None, stop=None):
    stack = ExitStack()
    with stack:
        def sb(name, shape, dt=F32, where=stack):
            return where.enter_context(nc.sbuf_tensor(name, shape, dt))

        def semaphore(name):
            return stack.enter_context(nc.semaphore(name))

        pe, act, dve, pool, sp = (Engine(semaphore(n)) for n in
                                  ("pe_done", "act_done", "dve_done", "pool_done", "sp_done"))

        vec = sb("vec", [P, NVEC])
        con = sb("con", [P, NCON])
        xT = sb("xT", [P, DK, T])
        hT = sb("hT", [P, DK, T])
        ring = sb("ring", [P, RING, SLOT])
        mod = sb("mod", [P, 48])
        rs_v, rs_t = sb("rs_v", [P, T]), sb("rs_t", [P, T])
        rs_y = sb("rs_y", [P, 2, T])
        sq = sb("sq", [P, 2, T])
        cond, one_plus = sb("cond", [P, DK]), sb("one_plus", [P, DK])
        over_i = sb("over_i", [P, 8], I32)
        work = sb("work", [P, ROOM])
        psum = [stack.enter_context(nc.psum_tensor(f"bank{i}", [P, 512], F32)) for i in range(8)]
        banks = Buffers(psum[:6])
        held = Buffers(psum[6:])

        def V(name, j=0, n=None):
            a, w = VEC[name]
            return vec[:, a + j:a + j + (n or 1)] if n is not None or w > 1 else vec[:, a:a + 1]

        def C(name, rows=P, lo=0, n=None):
            a, w = CON[name]
            return con[0:rows, a + lo:a + lo + (n or w)]

        ident, ones = C("ident"), C("ones")

        bias_dram = nc.dram_tensor("bias_rows", (H, T + P), F32).ap()
        h_dram = nc.dram_tensor("h_rows", (T, D), F32).ap()
        y_dram = nc.dram_tensor("expert_rows", (E * P, D), F32).ap()
        over_dram = nc.dram_tensor("overflow_rows", (OB * P, D), F32).ap()

        vec_in = Load(semaphore("vec_in")).start(act, [], vec[:, :], io["vec"])
        con_in = Load(semaphore("con_in")).start(act, [], con[:, :], io["con"])

        chunks = []

        def plan(src, k, n):
            chunks.append((src, k, n))

        class Weights:

            def __init__(self, name, view, slots, plan, start=()):
                self.view, self.slots, self.plan = view, slots, plan
                self.started = self.used = self.released = 0
                self.sems = [semaphore(f"{name}{i}") for i in range(slots)]
                self.free = [list(start) for _ in range(slots)]

            def start_next(self):
                if self.started < len(self.plan):
                    i, (src, k, n) = self.started, self.plan[self.started]
                    slot = i % self.slots
                    dst = self.view[:, slot, 0:k * n].rearrange("p (k n) -> p k n", k=k)
                    sp.quiet(self.free[slot], lambda e: e.dma_start(dst, src() if callable(src) else src),
                             self.sems[slot], 16)
                    self.started += 1

            def next(self):
                i = self.used
                _, k, n = self.plan[i]
                self.used += 1
                slot = i % self.slots
                return (self.view[:, slot, 0:k * n].rearrange("p (k n) -> p k n", k=k),
                        (self.sems[slot], 16 * (i // self.slots + 1)))

            def done(self, mark):
                self.free[self.released % self.slots] = [mark]
                self.released += 1
                self.start_next()

            def last_marks(self):
                return [(self.sems[i % self.slots], 16 * (i // self.slots + 1)) for i in range(self.started)][-self.slots:]

        weights = Weights("ring", ring, RING, chunks)

        def rows(w, cols=None):
            w = w if cols is None else w[:, cols[0]:cols[1]]
            return w.rearrange("(k p) n -> p k n", p=P)

        def plan_columns(w, lo, hi, step):
            for a in range(lo, hi, step):
                plan(rows(w, (a, a + step)), w.shape[0] // P, step)

        w_ada, w_in = io["w_ada"][0], io["w_in"][0]
        for k in range(DK):
            plan(w_ada[k * P:(k + 1) * P, 0:2048].unsqueeze(1), 1, 2048)
        plan_columns(w_in, C_KV, C_KV + 256, 256)
        plan(rows(io["w_kv_up"][0]), 2, 1024)
        plan_columns(w_in, C_Q, C_Q + 512, 256)
        plan_columns(w_in, C_QI, C_QI + 512, 256)
        plan_columns(w_in, C_X, C_X + 1536, 256)
        plan_columns(w_in, C_Z, C_Z + 1024, 256)
        for b in range(4):
            plan_columns(w_in, C_G + 256 * b, C_G + 256 * b + 256, 256)
            plan_columns(io["w_attn_o"][0], 256 * b, 256 * b + 256, 256)
            plan_columns(w_in, C_G + 1024 + 256 * b, C_G + 1024 + 256 * b + 256, 256)
            plan_columns(io["w_ssm_o"][0], 256 * b, 256 * b + 256, 256)
        for half in range(2):
            for k in range(DK):
                a = 2048 + 2048 * half
                plan(w_ada[k * P:(k + 1) * P, a:a + 2048].unsqueeze(1), 1, 2048)
        plan_columns(io["w_out"][0], 0, D, 256)

        def plan_up(e):
            for k in range(DK):
                plan(io["w_gu"][0][e][k * P:(k + 1) * P, :].unsqueeze(1), 1, 2048)

        def plan_down(e):
            for k in range(0, DK, 2):
                plan(rows(io["w_dn"][0][e][k * P:(k + 2) * P, :]), 2, 1024)

        plan_up(0)
        for e in range(1, E):
            plan_up(e)
            plan_down(e - 1)
        plan_down(E - 1)
        plan_columns(io["a_w_in_2"][0], 0, 3 * AW, 256)
        plan_columns(io["a_w_out_2"][0], 0, D, 128)
        for b in range(BW // 256):
            plan_columns(io["b_w_in_2"][0], 256 * b, 256 * b + 256, 256)
            plan_columns(io["b_w_in_2"][0], BW + 256 * b, BW + 256 * b + 256, 256)
        plan_columns(io["b_w_out_2"][0], 0, D, 128)
        for _ in range(RING):
            weights.start_next()

        def matmuls(after, pairs, o, start=True, stop=True):
            for i, (lhsT, rhs) in enumerate(pairs):
                last = i == len(pairs) - 1
                f = (lambda e, l=lhsT, r=rhs, s=(start and i == 0), t=(stop and last):
                     e.matmul(o, l, r, start=s, stop=t))
                if last:
                    return pe.do(after if i == 0 else [], f)
                pe.quiet(after if i == 0 else [], f)

        def transpose(after, o, in_):
            return pe.do(after, lambda e: e.transpose(o, in_, ident))

        def copy(eng, after, o, in_, scale=None):
            if eng is act:
                return act.do(after, lambda e: e.activation(o, in_, ACT.Copy, scale=1.0 if scale is None else scale))
            return eng.do(after, lambda e: e.tensor_copy(o, in_) if scale is None else
                          e.tensor_scalar(o, in_, scale, None, ALU.mult))

        def activate(after, o, in_, f, **kw):
            return act.do(after, lambda e: e.activation(o, in_, f, **kw))

        def tt(after, o, a, b, op, eng=None):
            return (eng or dve).do(after, lambda e: e.tensor_tensor(o, a, b, op))

        def ts(after, o, a, s1, op0, s2=None, op1=None, eng=None):
            if op1 is None:
                return (eng or dve).do(after, lambda e: e.tensor_scalar(o, a, s1, None, op0))
            return (eng or dve).do(after, lambda e: e.tensor_scalar(o, a, s1, s2, op0, op1))

        def stt(after, o, a, s, b, op0, op1):
            return dve.do(after, lambda e: e.scalar_tensor_tensor(out=o, in0=a, scalar=s, in1=b, op0=op0, op1=op1))

        rs_ring = Buffers([0, 1])
        sq_ring = Buffers([sq[:, 0, :], sq[:, 1, :]])

        def rsqrt(after, total, n, eps):
            i, j, free = rs_ring.take()
            v, y, t = rs_v[:, :], rs_y[:, j, :], rs_t[:, :]
            m = ts(after + free, v, total, 1.0 / n, ALU.mult, eps, ALU.add)
            a = activate([m] + free, y, v, ACT.Ln)
            a = activate([a], y, y, ACT.Exp, scale=-0.5)
            m = tt([a], t, y, y, ALU.mult)
            m = tt([m], t, t, v, ALU.mult)
            m = ts([m], t, t, -0.5, ALU.mult, 1.5, ALU.add)
            m = tt([m], y, y, t, ALU.mult)
            return i, y, m

        def sum_squares(tiles, after, lhs, n, eps):
            b, bank, free = banks.take()
            for i, x in enumerate(tiles):
                s, sv, sfree = sq_ring.take()
                a = activate(after + sfree, sv, x, ACT.Square)
                m = pe.do([a] + (free if i == 0 else []),
                          lambda e, sv=sv, i=i: e.matmul(bank[:, :], lhs, sv, start=(i == 0), stop=(i == len(tiles) - 1)))
                sq_ring.release(s, m)
            i, y, m = rsqrt([m], bank[:, :], n, eps)
            banks.release(b, m)
            return i, y, m

        def project(ktiles, source, after, n_tiles, sink):
            tile = 0
            while tile < n_tiles:
                w, arrived = weights.next()
                for c in range(w.shape[2] // P):
                    b, bank, free = banks.take()
                    m = matmuls(after + free + [arrived],
                                [(w[:, k, c * P:(c + 1) * P], source(k)) for k in range(ktiles)], bank[:, :])
                    last = m
                    banks.release(b, *sink(tile, bank[:, :], m))
                    tile += 1
                weights.done(last)

        def join():
            return [e.mark() for e in (pe, act, dve, pool)]

        def softplus(after, o, x, tmp):
            ax, u, s, z = tmp
            m = activate(after, ax, x, ACT.Abs)
            a = activate([m], u, ax, ACT.Exp, scale=-1.0)
            m = ts([a], ax, u, 2.0, ALU.add)
            m = dve.do([m], lambda e: e.reciprocal(ax, ax))
            m = tt([m], s, u, ax, ALU.mult)
            m = tt([m], z, s, s, ALU.mult)
            m = ts([m], u, z, 1.0 / 17, ALU.mult)
            for d in (15, 13, 11, 9, 7, 5, 3):
                m = stt([m], u, u, 1.0 / d, z, ALU.add, ALU.mult)
            m = stt([m], u, u, 1.0, s, ALU.add, ALU.mult)
            m = ts([m], ax, x, 0.0, ALU.max)
            return stt([m], o, u, 2.0, ax, ALU.mult, ALU.add)

        def show(name, view, after):
            if debug is not None and name in debug:
                s = Load(semaphore("dbg_" + name))
                dbg_marks.append(s.start(act, after, debug[name], view))

        dbg_marks = []
        stores = []

        def finish(after):
            sp.quiet(after + dbg_marks + stores + weights.last_marks(), None)
            close_part(None)
            for engines, flag in parts:
                if flag is None:
                    emit_part(engines)
                else:
                    taken = nc.values_load(flag, min_val=0, max_val=1)
                    with nc.If(taken > 0):
                        emit_part(engines)

        parts = []

        def close_part(flag):
            engines = (pe, act, dve, pool, sp)
            parts.append(([(e, e.queue) for e in engines], flag))
            for e in engines:
                e.queue = []

        def emit_part(engines):
            with nc.Block() as block:
                for (engine, queue), on in zip(engines, (block.tensor, block.scalar, block.vector, block.gpsimd, block.sync)):
                    on(lambda e, engine=engine, queue=queue: engine.emit(e, queue))

        phase = Room(work)
        x_tok = phase.take(P, TT, D)
        x_in = Load(semaphore("x_in")).start(act, [], x_tok[:, :, :], io["x"][0].rearrange("(t p) d -> p t d", p=P))
        m_cond = activate([vec_in], cond[:, :], V("c", 0, 8), ACT.Silu)

        def modulation(block, after, ada):
            m = None
            for k in range(DK):
                w, arrived = weights.next()
                if k == 0:
                    m = ts([arrived, m_cond] + after, ada[:, :], w[:, 0, :], cond[:, k:k + 1], ALU.mult)
                else:
                    m = stt([arrived, m], ada[:, :], w[:, 0, :], cond[:, k:k + 1], ada[:, :], ALU.mult, ALU.add)
                weights.done(m)
            b, bank, free = banks.take()
            for j in range(16):
                p_ = pe.do([m, con_in] + free, lambda e, j=j: e.matmul(bank[:, j:j + 1], ada[:, j * P:(j + 1) * P],
                                                             ones[:, 0:1], start=True, stop=True))
            m = tt([p_, vec_in], mod[:, 16 * block:16 * block + 16], bank[:, 0:16], V("b_ada", 16 * block, 16), ALU.add)
            banks.release(b, m)
            return m

        for k in range(DK):
            b, bank, free = banks.take()
            for t in range(TT):
                m = transpose([x_in, con_in] + free, bank[:, t * P:(t + 1) * P], x_tok[:, t, k * P:(k + 1) * P])
            m = copy(act, [m], xT[:, k, :], bank[:, :])
            banks.release(b, m)
        m_x = m
        m_mod = modulation(0, [], phase.take(P, 2048))

        def normalise(gain, shift_block, m_ready):
            i, rs, m_rs = sum_squares([xT[:, k, :] for k in range(DK)], m_ready, ones, D, EPS)
            for k in range(DK):
                m = stt([m_rs], hT[:, k, :], xT[:, k, :], V(gain[0], gain[1] + k), rs, ALU.mult, ALU.mult)
                if shift_block is not None:
                    m1 = activate([m], hT[:, k, :], hT[:, k, :], ACT.Identity,
                                  scale=one_plus[:, k:k + 1], bias=mod[:, shift_block * 8 + k:shift_block * 8 + k + 1])
            rs_ring.release(i, m)
            return m1 if shift_block is not None else m

        m_op = ts([m_mod], one_plus[:, :], mod[:, 8:16], 1.0, ALU.add)
        m_h = normalise(("norm_mix", 0), 0, [m_x, m_op])
        show("hT", hT[:, :, :], [m_h])
        if stop == "h":
            return finish([m_h])

        room = Room(work)
        oT = room.take(P, 4, T)
        yT = room.take(P, 8, T)
        wi_dt = room.take(P, TT, 24)
        after_mixers = room.at
        qT, kT, qiT = (room.take(P, 4, T) for _ in range(3))
        kiT = room.take(P, T)
        v_tok = room.take(P, TT, T)
        kvT_at = room.at
        kvT = room.take(P, 2, T)
        rawT = room.take(P, 2, T)
        start = join()

        narrow = room.take(P, DK, 152)
        narrow_in = Load(semaphore("narrow_in"))
        for dst, lo, n in ((0, C_KI, 64), (64, C_KI, 64), (128, C_WI, 8), (136, C_DT, 16)):
            m_narrow = narrow_in.start(act, start, narrow[:, :, dst:dst + n], rows(w_in, (lo, lo + n)))

        bias_row = room.take(8, T + P)
        rel = room.take(NB, 8)
        rel_in = Load(semaphore("rel_in")).start(act, start, rel, io["rel_bias"])
        for lo, n in ((0, T), (T, P)):
            b, bank, free = banks.take()
            m = matmuls(free + [rel_in, con_in], [(rel, C("bucket", NB, lo, n))], bank[0:8, 0:n])
            m = copy(dve, start + [m], bias_row[:, lo:lo + n], bank[0:8, 0:n])
            banks.release(b, m)
        bias_out = Load(semaphore("bias_out")).start(act, [m], bias_dram[:, :], bias_row)
        stores.append(bias_out)

        def h_tile(k):
            return hT[:, k, :]

        raw_ring = Buffers([rawT[:, 0, :], rawT[:, 1, :]])

        def keep_raw(bank, m, scale=None):
            r, raw, rfree = raw_ring.take()
            return r, raw, copy(act, [m] + rfree + start, raw, bank, scale)

        def sink_kv(tile, bank, m):
            return [copy(act, [m] + start, kvT[:, tile, :], bank)]

        project(DK, h_tile, [m_h], 2, sink_kv)
        m_kv = act.mark()
        i, rs, m = sum_squares([kvT[:, j, :] for j in range(2)], [m_kv], ones, 256, EPS)
        for j in range(2):
            m = stt([m], kvT[:, j, :], kvT[:, j, :], V("kv_norm", j), rs, ALU.mult, ALU.mult)
        rs_ring.release(i, m)
        m_kv = m

        gains = room.take(P, 2)
        m_gain = ts([vec_in] + start, gains[:, 0:1], V("q_norm"), HD ** -0.5, ALU.mult)
        heads = C("heads")

        def head_norm(dst, gain):
            def sink(tile, bank, m):
                r, raw, m = keep_raw(bank, m)
                i, rs, m2 = sum_squares([raw], [m], heads, HD, EPS)
                m2 = stt([m2, m_gain], dst[:, tile, :], raw, gain, rs, ALU.mult, ALU.mult)
                rs_ring.release(i, m2)
                raw_ring.release(r, m2)
                return [m]
            return sink

        w_up, arrived = weights.next()
        for c in range(4):
            b, bank, free = banks.take()
            m = matmuls(free + [arrived, m_kv], [(w_up[:, k, c * P:(c + 1) * P], kvT[:, k, :]) for k in range(2)],
                        bank[:, :])
            banks.release(b, *head_norm(kT, V("k_norm"))(c, bank[:, :], m))
        for t in range(TT):
            b, bank, free = banks.take()
            m = matmuls(free + [arrived, m_kv], [(kvT[:, k, t * P:(t + 1) * P], w_up[:, k, 512:1024]) for k in range(2)],
                        bank[:, :])
            if t == TT - 1:
                weights.done(m)
            m = copy(act, [m] + start, v_tok[:, t, :], bank[:, :])
            banks.release(b, m)
        project(DK, h_tile, [m_h], 4, head_norm(qT, gains[:, 0:1]))
        project(DK, h_tile, [m_h], 4, lambda tile, bank, m: [copy(act, [m] + start, qiT[:, tile, :], bank, HD ** -0.5)])

        b, bank, free = banks.take()
        m = matmuls(free + [m_narrow], [(narrow[:, k, 0:P], hT[:, k, :]) for k in range(DK)], bank[:, :])
        r, raw, m = keep_raw(bank[:, :], m)
        banks.release(b, m)
        b, bank, free = banks.take()
        m = matmuls(free + [m], [(heads, raw)], bank[:, :])
        m = stt([m], raw, bank[:, :], -1.0 / HD, raw, ALU.mult, ALU.add)
        banks.release(b, m)
        i, rs, m = sum_squares([raw], [m], heads, HD, EPS)
        m = tt([m], kiT, raw, rs, ALU.mult)
        rs_ring.release(i, m)
        raw_ring.release(r, m)
        m_ki = ts([m], kiT, kiT, V("idx_k_ln_w"), ALU.mult, V("idx_k_ln_b"), ALU.add)

        b, bank, free = banks.take()
        for t in range(TT):
            m = matmuls(free + [m_narrow], [(hT[:, k, t * P:(t + 1) * P], narrow[:, k, 128:152]) for k in range(DK)],
                        bank[:, 24 * t:24 * t + 24])
        m = copy(dve, [m] + start, wi_dt.rearrange("p a b -> p (a b)"), bank[:, 0:96])
        banks.release(b, m)
        m_wi = ts([m], wi_dt[:, :, 0:8], wi_dt[:, :, 0:8], H ** -0.5, ALU.mult)
        show("qT", qT, join()); show("kT", kT, join()); show("v", v_tok, join()); show("kiT", kiT, join())
        show("qiT", qiT, join()); show("widt", wi_dt, join())
        if stop == "att_in":
            return finish(join())

        room.at = kvT_at
        bias = room.take(P, H, T)
        keep = room.take(P, T)
        score, sel_a, sel_b = (room.take(P, T) for _ in range(3))
        best = room.take(P, 8)
        count = room.take(P, 2)
        relu_buf = Buffers([room.take(P, T) for _ in range(2)])
        logit_buf = Buffers([room.take(P, T) for _ in range(3)])
        prob_t_buf = Buffers([room.take(P, T) for _ in range(2)])
        stats = room.take(P, TT * H, 3)
        start = join()
        row = bias_dram[0:1, 0:1]
        bias_src = bass.AP(row.tensor, row.offset, [[1, P], [T + P, H], [1, T]])
        m_bias = Load(semaphore("bias_in")).start(act, start + [bias_out], bias, bias_src)
        for h in range(H):
            b, bank, free = banks.take()
            m = matmuls(free + [m_bias], [(C("flip"), bias[:, h, :])], bank[:, :])
            bias_in = copy(dve, [m], bias[:, h, :], bank[:, :])
            banks.release(b, bias_in)

        def select(after, src, width, k, cap_a, cap_b, o):
            m = None
            rounds = k // 8
            cur = src
            for r in range(rounds):
                m = dve.do((after if r == 0 else []) + [m], lambda e, cur=cur: e.max(best, cur))
                if r < rounds - 1:
                    m = dve.do([m], lambda e, cur=cur: e.match_replace(cap_a, best, cur, -3.0e38))
                    cur = cap_a
            return threshold(after + [m], src, width, k, best[:, 7:8], cap_a, cap_b, o, count)

        def threshold(after, src, width, k, kth, cap_a, cap_b, o, count):
            m = dve.do(after, lambda e: e.tensor_scalar(o, src, kth, None, ALU.is_gt, ALU.add, accum_out=count[:, 0:1]))
            m = ts([m], count[:, 1:2], count[:, 0:1], -1.0, ALU.mult, float(k), ALU.add)
            m = ts([m], cap_a, src, kth, ALU.is_equal)
            m = dve.do([m], lambda e: e.tensor_tensor_scan(cap_b, cap_a, cap_a, 0.0, ALU.add, ALU.bypass))
            m = stt([m], cap_b, cap_b, count[:, 1:2], cap_a, ALU.is_le, ALU.mult)
            return tt([m], o, o, cap_b, ALU.add)

        for t in range(TT):
            width = (t + 1) * P
            lo = T - width
            causal = C("causal", P, lo, width)
            sc = score[:, 0:width]
            if t == 0:
                m_keep = copy(dve, start + [con_in, dve.mark()], keep[:, 0:width], causal)
            else:
                for h in range(H):
                    half = slice((h % 2) * 64, (h % 2) * 64 + 64)
                    b, bank, free = banks.take()
                    m = matmuls(free + [m_ki, act.mark()],
                                [(qiT[half, h // 2, t * P:(t + 1) * P], kiT[half, 0:width])], bank[:, 0:width])
                    r, rv, rfree = relu_buf.take()
                    m = activate([m] + rfree + start, rv[:, 0:width], bank[:, 0:width], ACT.Relu)
                    banks.release(b, m)
                    w = wi_dt[:, t, h:h + 1]
                    if h == 0:
                        m_sc = ts([m, m_wi] + start, sc, rv[:, 0:width], w, ALU.mult)
                    else:
                        m_sc = stt([m, m_sc], sc, rv[:, 0:width], w, sc, ALU.mult, ALU.add)
                    relu_buf.release(r, m_sc)
                m = tt([m_sc], sc, sc, causal, ALU.add)
                m = select([m], sc, width, TOPK, sel_a[:, 0:width], sel_b[:, 0:width], keep[:, 0:width])
                m_keep = ts([m], keep[:, 0:width], keep[:, 0:width], 1.0, ALU.subtract, -NEG, ALU.mult)
            show("keep%d" % t, keep, [m_keep])

            ob, obank, ofree = held.take()
            for h in range(H):
                half = slice((h % 2) * 64, (h % 2) * 64 + 64)
                st = stats[:, t * H + h, :]
                b, bank, free = banks.take()
                m = matmuls(free + [dve.mark()], [(qT[half, h // 2, t * P:(t + 1) * P], kT[half, h // 2, 0:width])],
                            bank[:, 0:width])
                l, lv, lfree = logit_buf.take()
                lw = lv[:, 0:width]
                m = tt([m, bias_in] + lfree, lw, bank[:, 0:width], bias[:, h, lo:T], ALU.add)
                banks.release(b, m)
                m = dve.do([m, m_keep], lambda e, lw=lw, st=st, width=width: e.tensor_tensor_reduce(
                    out=lw, in0=lw, in1=keep[:, 0:width], scale=1.0, scalar=-3.0e38, op0=ALU.add, op1=ALU.max,
                    accum_out=st[:, 0:1]))
                m = ts([m], st[:, 0:1], st[:, 0:1], -1.0, ALU.mult)
                m = activate([m], lw, lw, ACT.Exp, bias=st[:, 0:1], accum_out=st[:, 1:2])
                m = dve.do([m], lambda e, st=st: e.reciprocal(st[:, 2:3], st[:, 1:2]))
                m = ts([m], lw, lw, st[:, 2:3], ALU.mult)
                b, bank, free = banks.take()
                for s in range(t + 1):
                    mt = transpose(free + [m], bank[:, s * P:(s + 1) * P], lw[:, s * P:(s + 1) * P])
                logit_buf.release(l, mt)
                q, pt, pfree = prob_t_buf.take()
                m = copy(act, [mt] + pfree, pt[:, 0:width], bank[:, 0:width])
                banks.release(b, m)
                m_o = matmuls([m] + ofree, [(v_tok[:, s, h * HD:(h + 1) * HD], pt[:, s * P:(s + 1) * P]) for s in range(t + 1)],
                            obank[half, (h // 2) * P:(h // 2 + 1) * P])
                prob_t_buf.release(q, m_o)
            m = copy(act, [m_o], oT[:, :, t * P:(t + 1) * P], obank[:, :].rearrange("p (a b) -> p a b", a=4))
            held.release(ob, m)
        m_oT = m
        show("oT", oT, [m_oT])
        if stop == "att":
            return finish(join())

        room.at = after_mixers
        xbcT = room.take(P, CT, T)
        pad_room, acc_room = room.take(P, 2, T + 8), room.take(P, 2, T)
        padded = Buffers([pad_room[:, j, 0:T + 3] for j in range(2)])
        acc_buf = Buffers([acc_room[:, j, :] for j in range(2)])
        xs_tok = room.take(P, TT, D)
        bm_tok = room.take(P, TT, 2 * SN)
        dt = room.take(P, TT, SH)
        dA = room.take(P, TT, SH)
        a_neg = room.take(P, SH)
        tmp4 = [room.take(P, TT, SH) for _ in range(4)]
        dec = room.take(P, SH)
        spread = room.take(P, SH, P)
        lmat = room.take(P, SH, P)
        grow = room.take(P, SH, P)
        x_dt, x_end = acc_room.rearrange("p a b -> p (a b)"), pad_room.rearrange("p a b -> p (a b)")[:, 0:D]
        cb = room.take(P, 2, P)
        state = room.take(P, D)
        start = join()

        dtb = V("dt_bias", 0, SH).unsqueeze(1).to_broadcast([P, TT, SH])
        m = tt(start + [m_wi], dt, wi_dt[:, :, 8:24], dtb, ALU.add)
        m = softplus([m], dt, dt, tmp4)
        a = activate(start, a_neg, V("a_log", 0, SH), ACT.Exp)
        m = stt([m, a], dA, dt, -1.0, a_neg.unsqueeze(1).to_broadcast([P, TT, SH]), ALU.mult, ALU.mult)
        m_dA = m

        pads = [dve.do(start, lambda e, v=v: e.memset(v[:, 0:3], 0.0)) for v in padded.views]

        def convolve(tile, bank, m, w_name, tiles, o):
            i, pv, pfree = padded.take()
            m = copy(act, [m, pads[i]] + pfree + start, pv[:, 3:], bank)
            bank_read = m
            m = ts([m] + start, o, pv[:, 0:T], V(w_name, tile), ALU.mult)
            for tap in range(1, 4):
                m = stt([m], o, pv[:, tap:tap + T], V(w_name, tap * tiles + tile), o, ALU.mult, ALU.add)
            padded.release(i, m)
            return bank_read, m

        def sink_conv(tile, bank, m):
            j, av, afree = acc_buf.take()
            dve.quiet(afree, None)
            bank_read, m = convolve(tile, bank, m, "conv_w", CT, av)
            m = activate([m], xbcT[:, tile, :], av, ACT.Silu, bias=V("conv_b", tile))
            acc_buf.release(j, m)
            return [bank_read]

        project(DK, h_tile, [m_h], CT, sink_conv)
        m_xbc = act.mark()

        for t in range(TT):
            for j in range(0, 10, 4):
                n = min(4, 10 - j)
                b, bank, free = banks.take()
                for q in range(n):
                    m = transpose(free + [m_xbc], bank[:, q * P:(q + 1) * P], xbcT[:, j + q, t * P:(t + 1) * P])
                dst = xs_tok[:, t, j * P:(j + 4) * P] if j < 8 else bm_tok[:, t, :]
                m = copy(act, [m] + start, dst, bank[:, 0:n * P])
                banks.release(b, m)
        m_tok = m

        tri, after_mask = C("tri"), C("after")
        for c in range(TT):
            here = slice(c * P, (c + 1) * P)
            old = join() if c else start
            m_spread = tt(old + [m_dA, con_in], spread, dA[:, c, :].unsqueeze(2).to_broadcast([P, SH, P]),
                          tri.unsqueeze(1).to_broadcast([P, SH, P]), ALU.mult)
            for lhs, dst in ((after_mask, lmat), (ones, grow)):
                for q in range(4):
                    b, bank, free = banks.take()
                    m = matmuls(free + [m_spread], [(lhs, spread[:, 4 * q:4 * q + 4, :].rearrange("p a b -> p (a b)"))],
                                bank[:, :])
                    m = activate([m], dst[:, 4 * q:4 * q + 4, :].rearrange("p a b -> p (a b)"), bank[:, :], ACT.Exp)
                    banks.release(b, m)
                if dst is lmat:
                    m_lmat = m
            m_grow = m
            b, bank, free = banks.take()
            m = matmuls(free + [m_dA], [(after_mask, dA[:, c, :])], bank[:, 0:SH])
            m = activate([m], dec, bank[:, 0:SH], ACT.Exp)
            banks.release(b, m)
            b, bank, free = banks.take()
            for g in range(SG):
                m = matmuls(free + [m_xbc], [(xbcT[:, 8 + g, here], xbcT[:, 10 + g, here])], bank[:, g * P:(g + 1) * P])
            m = tt([m] + old, cb, bank[:, 0:2 * P].rearrange("p (a b) -> p a b", a=2),
                   tri.unsqueeze(1).to_broadcast([P, SG, P]), ALU.mult)
            banks.release(b, m)
            xs3 = xs_tok[:, c, :].rearrange("p (h d) -> p h d", h=SH)
            x_dt3, x_end3 = (v.rearrange("p (h d) -> p h d", h=SH) for v in (x_dt, x_end))
            m_xdt = tt(old + [m_tok], x_dt3, xs3, dt[:, c, :].unsqueeze(2).to_broadcast([P, SH, SP_]), ALU.mult)
            for g in range(SG):
                hs = slice(8 * g, 8 * g + 8)
                m_w = tt([m_lmat, m], lmat[:, hs, :], lmat[:, hs, :], cb[:, g, :].unsqueeze(1).to_broadcast([P, 8, P]),
                         ALU.mult)
                if c:
                    m_cs = tt([m_grow, m_xbc], spread[:, hs, :], grow[:, hs, :],
                              xbcT[:, 10 + g, here].unsqueeze(1).to_broadcast([P, 8, P]), ALU.mult)
            m_end = tt([act.mark(), m_xdt], x_end3, x_dt3, dec.unsqueeze(2).to_broadcast([P, SH, SP_]), ALU.mult)
            for q in range(2):
                b, bank, free = banks.take()
                for pair in range(4):
                    for half in range(2):
                        h = 8 * q + 2 * pair + half
                        terms = [(x_dt[:, h * SP_:(h + 1) * SP_], lmat[:, h, :])]
                        if c:
                            terms.append((state[:, h * SP_:(h + 1) * SP_], spread[:, h, :]))
                        m = matmuls(free + [m_xdt, m_w, dve.mark()], terms,
                                    bank[half * 64:half * 64 + 64, pair * P:(pair + 1) * P])
                for pair in range(4):
                    tile = 4 * q + pair
                    my = stt([m], yT[:, tile, here], xbcT[:, tile, here], V("d_skip", tile),
                             bank[:, pair * P:(pair + 1) * P], ALU.mult, ALU.add)
                banks.release(b, my)
            if c < TT - 1:
                m_read = m
                for g in range(SG):
                    cols = slice(512 * g, 512 * g + 512)
                    b, bank, free = banks.take()
                    m = matmuls(free + [m_tok, m_end], [(bm_tok[:, c, g * SN:(g + 1) * SN], x_end[:, cols])], bank[:, :])
                    if c == 0:
                        m = copy(dve, [m] + start, state[:, cols], bank[:, :])
                    else:
                        st3 = state[:, cols].rearrange("p (h d) -> p h d", h=8)
                        m2 = tt([m_grow, m_read, dve.mark()], st3, st3,
                                grow[:, 8 * g:8 * g + 8, P - 1:P].to_broadcast([P, 8, SP_]), ALU.mult)
                        m = tt([m, m2], state[:, cols], state[:, cols], bank[:, :], ALU.add)
                    banks.release(b, m)

        m_y = dve.mark()

        def sink_z(tile, bank, m):
            j, av, afree = acc_buf.take()
            a = activate([m, m_y] + afree, av, bank, ACT.Silu)
            m = tt([a, m_y], yT[:, tile, :], yT[:, tile, :], av, ALU.mult)
            acc_buf.release(j, m)
            return [a]

        project(DK, h_tile, [m_h], 8, sink_z)
        m_y = dve.mark()
        for g in range(SG):
            i, rs, m = sum_squares([yT[:, 4 * g + j, :] for j in range(4)], [m_y], ones, 512, EPS)
            for j in range(4):
                tile = 4 * g + j
                m = stt([m], yT[:, tile, :], yT[:, tile, :], V("ssm_norm", tile), rs, ALU.mult, ALU.mult)
            rs_ring.release(i, m)
        m_yT = m
        show("yT", yT, [m_yT])
        if stop == "ssd":
            return finish(join())

        room.at = after_mixers
        mixedT = room.take(P, DK, T)
        gate_buf = Buffers([room.take(P, 2, T) for _ in range(2)])
        ada = room.take(P, 2048)
        start = join()
        for blk in range(4):
            gate = {}
            for which in range(2):
                gi, gv, gfree = gate_buf.take()
                gate[which] = (gi, gv)

                def sink_gate(tile, bank, m, gv=gv, gfree=gfree):
                    return [activate([m] + gfree + start, gv[:, tile, :], bank, ACT.Sigmoid)]

                project(DK, h_tile, [m_h], 2, sink_gate)
                m_gate = act.mark()

                def sink_mix(tile, bank, m, gv=gv, which=which):
                    o = mixedT[:, 2 * blk + tile, :]
                    if which == 0:
                        return [tt([m, m_gate] + start, o, bank, gv[:, tile, :], ALU.mult)]
                    m = tt([m, m_gate], gv[:, tile, :], bank, gv[:, tile, :], ALU.mult)
                    tt([m], o, o, gv[:, tile, :], ALU.add)
                    return [m]

                if which == 0:
                    project(4, lambda k: oT[:, k, :], [m_oT], 2, sink_mix)
                else:
                    project(DK, lambda k: yT[:, k, :], [m_yT], 2, sink_mix)
                gate_buf.release(gi, dve.mark())
        m_mix = dve.mark()
        m_mod1 = modulation(1, start, ada)
        m_mod2 = modulation(2, [pe.mark()], ada)

        def sink_out(tile, bank, m):
            return [stt([m, m_mod1, m_h], xT[:, tile, :], bank, mod[:, 16 + tile:17 + tile], xT[:, tile, :],
                        ALU.mult, ALU.add)]

        project(DK, lambda k: mixedT[:, k, :], [m_mix], DK, sink_out)
        m_x = dve.mark()
        show("xT", xT[:, :, :], [m_x])
        if stop == "x1":
            return finish(join())

        room = Room(work)
        top = room.take(P, TT, E)
        gate_e = room.take(P, TT, E)
        place = room.take(P, TT, E)
        slot_of = room.take(P, TT, E)
        first = room.take(P, TT, E)
        gate_1 = room.take(P, TT, E)
        row_of = room.take(P, TT, E)
        logits = room.take(P, TT, E)
        route_a, route_b = room.take(P, E), room.take(P, E)
        best_r = room.take(P, TT, 8)
        rows_i = room.take(P, TT, 8, dt=I32)
        gates_k = room.take(P, TT, EK)
        totals = room.take(P, E)
        over = room.take(P, 2)
        tok_v = room.take(P, TT, 2, dt=BF16)
        w_router = room.take(P, DK, E)
        after_route = room.at
        h_tok = room.take(P, TT, D)
        start = join()
        router_in = Load(semaphore("router_in")).start(act, start, w_router, rows(io["w_router"][0]))
        m = ts([m_mod2, dve.mark()], one_plus[:, :], mod[:, 32:40], 1.0, ALU.add)
        m_h = normalise(("norm_ffn", 0), 3, [m_x, m] + start)

        for t in range(TT):
            for j in range(0, DK, 4):
                b, bank, free = banks.take()
                for q in range(4):
                    m = transpose(free + [m_h], bank[:, q * P:(q + 1) * P], hT[:, j + q, t * P:(t + 1) * P])
                m = copy(act, [m], h_tok[:, t, j * P:(j + 4) * P], bank[:, :])
                banks.release(b, m)
        h_out = Load(semaphore("h_out")).start(act, [m], h_dram.rearrange("(t p) d -> p t d", p=P), h_tok)
        stores.append(h_out)

        b, bank, free = banks.take()
        for t in range(TT):
            m = matmuls(free + [m_h, router_in], [(hT[:, k, t * P:(t + 1) * P], w_router[:, k, :]) for k in range(DK)],
                        bank[:, t * E:(t + 1) * E])
        m_log = tt([m] + start, logits, bank[:, 0:TT * E].rearrange("p (a b) -> p a b", a=TT),
                   V("b_router", 0, E).unsqueeze(1).to_broadcast([P, TT, E]), ALU.add)
        banks.release(b, m_log)
        for t in range(TT):
            lg = logits[:, t, :]
            br = best_r[:, t, :]
            m = dve.do([m_log], lambda e, br=br, lg=lg: e.max(br, lg))
            m = threshold([m], lg, E, EK, br[:, EK - 1:EK], route_a, route_b, top[:, t, :], over)
            m2 = ts([m], route_b, lg, br[:, 0:1], ALU.subtract)
            a = activate([m2], route_b, route_b, ACT.Exp)
            m = dve.do([a, m], lambda e, t=t: e.tensor_tensor_reduce(
                out=gate_e[:, t, :], in0=route_b, in1=top[:, t, :], scale=1.0, scalar=0.0, op0=ALU.mult, op1=ALU.add,
                accum_out=over[:, 0:1]))
            m = dve.do([m], lambda e: e.reciprocal(over[:, 1:2], over[:, 0:1]))
            m = ts([m], gate_e[:, t, :], gate_e[:, t, :], over[:, 1:2], ALU.mult)
        m_top = m
        b, bank, free = banks.take()
        for t in range(TT):
            m = matmuls(free + [m_top], [(C("before"), top[:, t, :])] + [(ones, top[:, s, :]) for s in range(t)],
                        bank[:, t * E:(t + 1) * E])
        m_tot = matmuls([], [(ones, top[:, s, :]) for s in range(TT)], bank[:, TT * E:(TT + 1) * E])
        flat = "p a b -> p (a b)"
        m = stt([m_tot, m_top], place.rearrange(flat), bank[:, 0:TT * E], 1.0, top.rearrange(flat), ALU.add, ALU.mult)
        m_slot = ts([m], slot_of, place, 1.0, ALU.subtract)
        m2 = stt([m], first, place, float(P), top, ALU.is_le, ALU.mult)
        m_g1 = tt([m2], gate_1, gate_e, first, ALU.mult)
        m2 = tt([m2], row_of, place, C("ebase").unsqueeze(1).to_broadcast([P, TT, E]), ALU.add)
        m_row = tt([m2, m_g1], row_of, row_of, first, ALU.mult)
        m_tot = copy(dve, [m_tot, m_slot], totals, bank[:, TT * E:(TT + 1) * E])
        m = dve.do([m_tot, m_row], lambda e, bank=bank: e.tensor_reduce(over[:, 0:1], bank[:, TT * E:(TT + 1) * E], AX.X, ALU.max))
        banks.release(b, m)
        m_over = ts([m], over_i[:, 0:1], over[:, 0:1], float(P), ALU.is_gt)
        for t in range(TT):
            m = copy(dve, [con_in], tok_v[:, t, 0:1], C("tok", P, 0, 1))
            m = ts([con_in], tok_v[:, t, 1:2], C("tok", P, 1, 1), float(t * P), ALU.mult)
        m_tokv = m
        for t in range(TT):
            br = best_r[:, t, :]
            m = dve.do([m_row], lambda e, br=br, t=t: e.max(br, row_of[:, t, :]))
            for k in range(EK):
                m2 = dve.do([m], lambda e, br=br, t=t, k=k: e.scalar_tensor_tensor(
                    out=route_a, in0=row_of[:, t, :], scalar=br[:, k:k + 1], in1=gate_1[:, t, :],
                    op0=ALU.is_equal, op1=ALU.mult, accum_out=gates_k[:, t, k:k + 1]))
                m = m2
            m_rows = ts([m], rows_i[:, t, :], br, 1.0, ALU.subtract, 0.0, ALU.max)

        room.at = after_route
        pick = Buffers([room.take(P, TT, P, dt=BF16) for _ in range(2)])
        index_sum = room.take(P, 1)
        index = Buffers([room.take(P, 1, dt=I32) for _ in range(2)])
        xe = Buffers([room.take(P, D) for _ in range(2)])
        xeT = Buffers([room.take(P, DK, P) for _ in range(2)])
        bias_rows = room.take(P, 3 * D)
        bias_all = Buffers([room.take(P, 3 * D) for _ in range(3)])
        g_act, u_act, s_act = room.take(P, D), room.take(P, D), room.take(P, D)
        acted = room.take(P, D)
        aT = room.take(P, DK, P)
        ye = Buffers([room.take(P, D) for _ in range(2)])
        moe_end = room.at
        moe_start = join() + [h_out]
        up_banks, turn_banks, down_banks = psum[0:4], Buffers(psum[4:6]), psum[6:8]
        up_free, down_free = [], []
        bias_load = [Load(semaphore(f"bias_row{j}")) for j in range(2)]
        xe_load = [Load(semaphore(f"xe_in{j}")) for j in range(2)]
        ye_store = [Load(semaphore(f"ye_out{j}")) for j in range(2)]
        bias_row_free, bias_row_turn = [None, None], [1]

        def gather_rows(after, o, table, ids, load):
            load.count += 16
            prior = pool.mark()
            pool.count += 1
            done = pool.sem
            pool.quiet(after + [prior], lambda e: e.indirect_dma_start(
                out=o, out_offset=None, in_=table, in_offset=bass.IndirectOffsetOnAxis(ap=ids, axis=0),
                engine_sem=done), load.sem, 16)
            return (load.sem, load.count)

        def gather_tokens(slots):
            i, pv, pfree = pick.take()
            for t in range(TT):
                m = ts(moe_start + pfree + slots[1], pv[:, t, :], C("slot"), slots[0](t), ALU.is_equal)
            b, bank, free = turn_banks.take()
            m = matmuls(free + moe_start + [m, m_tokv], [(pv[:, t, :], tok_v[:, t, :]) for t in range(TT)], bank[:, 0:2])
            pick.release(i, m)
            j, iv, ifree = index.take()
            m = dve.do([m] + ifree, lambda e, o=index_sum: e.tensor_reduce(o, bank[:, 0:2], AX.X, ALU.add))
            turn_banks.release(b, m)
            m = copy(dve, [m], iv, index_sum)
            j2, xv, xfree = xe.take()
            landed = gather_rows([m] + xfree, xv, h_dram, iv, xe_load[j2])
            index.release(j, landed)
            return j2, xv, landed

        def turn_tokens(j2, xv, landed):
            i, tv, tfree = xeT.take()
            for q in range(0, DK, 4):
                b, bank, free = turn_banks.take()
                for r in range(4):
                    m = transpose(free + [landed], bank[:, r * P:(r + 1) * P], xv[:, (q + r) * P:(q + r + 1) * P])
                m_t = m
                m = copy(act, [m] + tfree, tv[:, q:q + 4, :].rearrange(flat), bank[:, :])
                turn_banks.release(b, m)
            xe.release(j2, m_t)
            return i, tv, m

        def spread_bias(e_gu, e_dn, marks=()):
            held_bias, bv, bfree = bias_all.take()
            j = bias_row_turn[0] = 1 - bias_row_turn[0]
            row = bias_rows[32 * j:32 * j + 1, :]
            bias_load[j].start(act, moe_start + [bias_row_free[j]] + list(marks), row[:, 0:2 * D], e_gu)
            m = bias_load[j].start(act, [], row[:, 2 * D:3 * D], e_dn)
            m = pool.do([m, pool.mark()] + bfree + moe_start, lambda e: e.partition_broadcast(bv, row))
            bias_row_free[j] = m
            return held_bias, bv, m

        def up_part(tv, after, lo, hi):
            for k in range(lo, hi):
                w, arrived = weights.next()
                for n in range(4):
                    f = (lambda e, n=n, w=w, k=k: e.matmul(up_banks[n][:, :], tv[:, k, :], w[:, 0, n * 512:(n + 1) * 512],
                                                           start=(k == 0), stop=(k == DK - 1)))
                    m = pe.do(after + up_free + [arrived], f)
                weights.done(m)
            return m

        def gate_up(m, bv, m_bias):
            for n in range(4):
                o = (g_act if n < 2 else u_act)[:, (n % 2) * 512:(n % 2) * 512 + 512]
                r = tt([m, m_bias, act.mark()], o, up_banks[n][:, :], bv[:, n * 512:(n + 1) * 512], ALU.add)
            up_free[:] = [r]
            m = ts([r], g_act, g_act, 7.0, ALU.min)
            a = activate([m], s_act, g_act, ACT.Sigmoid, scale=1.702)
            m = ts([r], u_act, u_act, 7.0, ALU.min, -7.0, ALU.max)
            m2 = tt([a], g_act, g_act, s_act, ALU.mult)
            return stt([m, m2] + acted_free, acted, u_act, 1.0, g_act, ALU.add, ALU.mult)

        acted_free, aT_free = [], []

        def turn_acted(m_act):
            for q in range(0, DK, 4):
                b, bank, free = turn_banks.take()
                for r in range(4):
                    m = transpose(free + [m_act], bank[:, r * P:(r + 1) * P], acted[:, (q + r) * P:(q + r + 1) * P])
                m_t = m
                m = copy(act, [m] + aT_free, aT[:, q:q + 4, :].rearrange(flat), bank[:, :])
                turn_banks.release(b, m)
            acted_free[:] = [m_t]
            return m

        def down(m_aT, j, bv, m_bias, dst):
            for k in range(0, DK, 2):
                w, arrived = weights.next()
                for kk in range(2):
                    for n in range(2):
                        f = (lambda e, n=n, w=w, k=k, kk=kk, x=aT: e.matmul(
                            down_banks[n][:, :], x[:, k + kk, :], w[:, kk, n * 512:(n + 1) * 512],
                            start=(k + kk == 0), stop=(k + kk == DK - 1)))
                        m = pe.do([m_aT, arrived] + down_free, f)
                weights.done(m)
            aT_free[:] = [m]
            i, yv, yfree = ye.take()
            for n in range(2):
                r = tt([m, m_bias] + yfree, yv[:, n * 512:(n + 1) * 512], down_banks[n][:, :],
                       bv[:, 2 * D + n * 512:2 * D + (n + 1) * 512], ALU.add)
            down_free[:] = [r]
            if j is not None:
                bias_all.release(j, r)
            m = ye_store[i].start(act, [r], dst, yv)
            ye.release(i, m)
            return m

        def primary(e):
            return gather_tokens((lambda t: slot_of[:, t, e:e + 1], [m_slot]))

        def bias_of(e):
            return spread_bias(io["b_gu"][0][e:e + 1, :], io["b_dn"][0][e:e + 1, :])

        tokens = turn_tokens(*primary(0))
        ahead = primary(1)
        biases = {0: bias_of(0)}
        for e in range(E):
            i, tv, m_tv = tokens
            if e:
                m_aT = turn_acted(m_act)
            up_part(tv, [m_tv], 0, 4)
            if e + 1 < E:
                tokens = turn_tokens(*ahead)
                biases[e + 1] = bias_of(e + 1)
            if e + 2 < E:
                ahead = primary(e + 2)
            m = up_part(tv, [], 4, DK)
            xeT.release(i, m)
            m_act = gate_up(m, *biases[e][1:])
            if e:
                down(m_aT, *biases.pop(e - 1), y_dram[(e - 1) * P:e * P, :])
        down(turn_acted(m_act), *biases.pop(E - 1), y_dram[(E - 1) * P:E * P, :])
        stored = [(s.sem, s.count) for s in ye_store]
        stores.extend(stored)

        room.at = after_route
        y_tok = room.take(P, TT, D)
        after_y = room.at
        picked = Buffers([room.take(P, D) for _ in range(6)])
        picked_load = [Load(semaphore(f"picked{j}")) for j in range(6)]
        start = join() + stored
        for t in range(TT):
            for k in range(EK):
                j, pv, pfree = picked.take()
                landed = gather_rows(start + [m_rows] + pfree, pv, y_dram, rows_i[:, t, k:k + 1], picked_load[j])
                if k == 0:
                    m = ts([landed], y_tok[:, t, :], pv, gates_k[:, t, k:k + 1], ALU.mult)
                else:
                    m = stt([landed, m], y_tok[:, t, :], pv, gates_k[:, t, k:k + 1], y_tok[:, t, :], ALU.mult, ALU.add)
                picked.release(j, m)
        m_y_tok = m

        close_part(None)
        main = (pe, act, dve, pool, sp, weights, m_y_tok)
        pe, act, dve, pool, sp = (Engine(semaphore("over_" + n)) for n in ("pe", "act", "dve", "pool", "sp"))
        room.at = after_y
        over_count, incl, base, hot, hot_a = (room.take(P, E) for _ in range(5))
        over_place = room.take(P, OB, TT)
        over_e, over_b = room.take(P, OB), room.take(P, OB)
        over_e_i = room.take(P, OB, dt=I32)
        row_over, gate_over = room.take(P, TT, E), room.take(P, TT, E)
        over_ring = room.take(P, 4, SLOT)
        pick = Buffers([room.take(P, TT, P, dt=BF16)])
        index_sum = room.take(P, 1)
        index = Buffers([room.take(P, 1, dt=I32)])
        xe, xeT = Buffers([room.take(P, D)]), Buffers([room.take(P, DK, P)])
        bias_one = room.take(P, 3 * D)
        g_act, u_act, s_act, acted = (room.take(P, D) for _ in range(4))
        aT = room.take(P, DK, P)
        ye = Buffers([room.take(P, D)])
        moe_start, m_tokv = [], None
        turn_banks = Buffers(psum[4:6])
        for marks in (up_free, down_free, acted_free, aT_free):
            marks[:] = []
        xe_load, ye_store = [Load(semaphore("over_xe_in"))], [Load(semaphore("over_ye_out"))]
        over_bias = Load(semaphore("over_bias_in"))
        picked_load = [Load(semaphore("over_picked_in"))]

        m = ts([], over_count, totals, float(P), ALU.is_gt)
        for k in (2, 3):
            m = stt([m], over_count, totals, float(k * P), over_count, ALU.is_gt, ALU.add)
        m = dve.do([m], lambda e: e.tensor_tensor_scan(incl, over_count, over_count, 0.0, ALU.add, ALU.bypass))
        m = tt([m], base, incl, over_count, ALU.subtract)
        for j in range(OB):
            m = ts([m], hot_a, base, float(j), ALU.is_le)
            m = stt([m], hot, incl, float(j), hot_a, ALU.is_gt, ALU.mult)
            for dst, src in [(over_e[:, j:j + 1], C("eone")), (over_b[:, j:j + 1], base)] + [
                    (over_place[:, j, t:t + 1], place[:, t, :]) for t in range(TT)]:
                m = dve.do([m], lambda e, dst=dst, src=src: e.tensor_tensor_reduce(
                    out=hot_a, in0=hot, in1=src, scale=1.0, scalar=0.0, op0=ALU.mult, op1=ALU.add, accum_out=dst))
            m = ts([m], over_b[:, j:j + 1], over_b[:, j:j + 1], float(P), ALU.mult, -float(P * (1 + j) + 1), ALU.add)
            m = ts([m], over_place[:, j, :], over_place[:, j, :], over_b[:, j:j + 1], ALU.add)
        m_list = m
        m_e = copy(dve, [m], over_e_i, over_e)
        m = ts([m], row_over, place, float(P), ALU.is_gt)
        m_gate = tt([m], gate_over, row_over, gate_e, ALU.mult)
        m = ts([m], base, base, float(P), ALU.mult, -float(P), ALU.add)
        m = tt([m], logits, place, base.unsqueeze(1).to_broadcast([P, TT, E]), ALU.add)
        m_row = tt([m, m_gate], row_over, row_over, logits, ALU.mult)

        expert = {}

        def over_chunks(j):
            def up(k):
                return lambda: io["w_gu"][0][bass.ds(expert[j], 1), k * P:(k + 1) * P, :].rearrange("a p n -> p a n")

            def dn(k):
                return lambda: io["w_dn"][0][bass.ds(expert[j], 1), k * P:(k + 2) * P, :].rearrange(
                    "a (k p) n -> p (a k) n", p=P)
            return [(up(k), 1, 2048) for k in range(DK)] + [(dn(k), 2, 1024) for k in range(0, DK, 2)]

        def read_expert(e, j):
            expert[j] = e.value_load(over_e_i[0:1, j:j + 1], min_val=0, max_val=E - 1)

        weights = Weights("over_ring", over_ring, 4, [])
        m = None
        for j in range(OB):
            weights.plan.extend(over_chunks(j))
            sp.quiet([m_e], lambda e, j=j: read_expert(e, j))
            over_bias.start(sp, [m], bias_one[:, 0:2 * D],
                            lambda j=j: io["b_gu"][0][bass.ds(expert[j], 1), :].to_broadcast([P, 2 * D]))
            m_bias = over_bias.start(sp, [], bias_one[:, 2 * D:3 * D],
                                     lambda j=j: io["b_dn"][0][bass.ds(expert[j], 1), :].to_broadcast([P, D]))
            for _ in range(4):
                weights.start_next()
            got = gather_tokens((lambda t: over_place[:, j, t:t + 1], [m_list]))
            i, tv, m_tv = turn_tokens(*got)
            m = up_part(tv, [m_tv], 0, DK)
            xeT.release(i, m)
            m_act = gate_up(m, bias_one, m_bias)
            down(turn_acted(m_act), None, bias_one, m_bias, over_dram[j * P:(j + 1) * P, :])
            m = dve.mark()
        stored_over = (ye_store[0].sem, ye_store[0].count)
        for t in range(TT):
            br = best_r[:, t, :]
            m = dve.do([m_row], lambda e, br=br, t=t: e.max(br, row_over[:, t, :]))
            for k in range(EK):
                m = dve.do([m], lambda e, br=br, t=t, k=k: e.scalar_tensor_tensor(
                    out=hot, in0=row_over[:, t, :], scalar=br[:, k:k + 1], in1=gate_over[:, t, :],
                    op0=ALU.is_equal, op1=ALU.mult, accum_out=gates_k[:, t, k:k + 1]))
            m = ts([m], rows_i[:, t, :], br, 1.0, ALU.subtract, 0.0, ALU.max)
            for k in range(EK):
                landed = gather_rows([m, stored_over], xe.views[0], over_dram, rows_i[:, t, k:k + 1], picked_load[0])
                m = stt([landed, m], y_tok[:, t, :], xe.views[0], gates_k[:, t, k:k + 1], y_tok[:, t, :], ALU.mult, ALU.add)
        sp.quiet(join() + [stored_over] + weights.last_marks(), None)
        close_part(over_i[0:1, 0:1])
        pe, act, dve, pool, sp, weights, m_y = main

        banks = Buffers(psum[:6])
        held = Buffers(psum[6:])
        for k in range(DK):
            b, bank, free = banks.take()
            for t in range(TT):
                m = transpose(free + start + [m_y], bank[:, t * P:(t + 1) * P], y_tok[:, t, k * P:(k + 1) * P])
            m = stt([m], xT[:, k, :], bank[:, :], mod[:, 40 + k:41 + k], xT[:, k, :], ALU.mult, ALU.add)
            banks.release(b, m)
        m_x = m
        show("xT2", xT[:, :, :], [m_x])
        if stop == "moe":
            return finish(join())

        room = Room(work)
        uT = room.take(P, AW // P, T)
        v_tok = room.take(P, TT, AW)
        b_s = room.take(P, 8, P)
        w_sT = room.take(P, 8, P)
        ln_row = room.take(P, AW)
        part = room.take(P, TT, 8)
        stat = room.take(P, TT, 4)
        start = join()
        w_s_load, ln_load = Load(semaphore("w_s_in")), Load(semaphore("ln_in"))
        w_s_raw = ln_row.rearrange("p (a b) -> p a b", a=16)[:, 0:8, :]
        w_s_in = w_s_load.start(act, start, w_s_raw, io["a_w_s_2"][0].rearrange("g t s -> t g s"))
        b_s_in = Load(semaphore("b_s_in")).start(
            act, start, b_s.rearrange(flat),
            io["a_b_s_2"].rearrange("a g t -> a (g t)").to_broadcast([P, 8 * P]))
        m_h = normalise(("norm_w_2", 0), None, [m_x] + start)
        for g in range(0, 8, 4):
            b, bank, free = banks.take()
            for q in range(4):
                m = transpose(free + [w_s_in], bank[:, q * P:(q + 1) * P], w_s_raw[:, g + q, :])
            m = tt([m] + start, w_sT[:, g:g + 4, :], bank[:, :].rearrange("p (a b) -> p a b", a=4),
                   C("tri").unsqueeze(1).to_broadcast([P, 4, P]), ALU.mult)
            banks.release(b, m)
        m_ws = m
        ln_in = ln_load.start(act, [pe.mark()], ln_row, io["a_ln_w_2"].to_broadcast([P, AW]))
        project(DK, h_tile, [m_h], AW // P,
                lambda tile, bank, m: [activate([m] + start, uT[:, tile, :], bank, ACT.Gelu_apprx_tanh)])
        for piece in range(8):
            w, arrived = weights.next()
            for t in range(TT):
                b, bank, free = banks.take()
                m = matmuls(free + [arrived, m_h], [(hT[:, k, t * P:(t + 1) * P], w[:, k, :]) for k in range(DK)],
                            bank[:, 0:256])
                a = activate([m] + start, v_tok[:, t, piece * 256:(piece + 1) * 256], bank[:, 0:256],
                             ACT.Gelu_apprx_tanh, accum_out=part[:, t, piece:piece + 1])
                banks.release(b, a)
            weights.done(m)
        m_v = a
        for t in range(TT):
            vt = v_tok[:, t, :]
            m = dve.do([m_v], lambda e, t=t: e.tensor_reduce(stat[:, t, 0:1], part[:, t, :], AX.X, ALU.add))
            m = ts([m], stat[:, t, 0:1], stat[:, t, 0:1], 1.0 / AW, ALU.mult)
            m = ts([m], vt, vt, stat[:, t, 0:1], ALU.subtract)
            for q in range(4):
                s, sv, sfree = sq_ring.take()
                m2 = activate([m] + sfree, sv, vt[:, q * 512:(q + 1) * 512], ACT.Square, accum_out=part[:, t, q:q + 1])
                sq_ring.release(s, m2)
            m = dve.do([m2], lambda e, t=t: e.tensor_reduce(stat[:, t, 1:2], part[:, t, 0:4], AX.X, ALU.add))
            m = ts([m], stat[:, t, 1:2], stat[:, t, 1:2], 1.0 / AW, ALU.mult, LN_EPS, ALU.add)
            a = activate([m], stat[:, t, 2:3], stat[:, t, 1:2], ACT.Sqrt)
            m = dve.do([a], lambda e, t=t: e.reciprocal(stat[:, t, 3:4], stat[:, t, 2:3]))
            m = stt([m, ln_in], vt, vt, stat[:, t, 3:4], ln_row, ALU.mult, ALU.mult)
        ln_in = ln_load.start(act, [m], ln_row, io["a_ln_b_2"].to_broadcast([P, AW]))
        for t in range(TT):
            m = tt([m, ln_in], v_tok[:, t, :], v_tok[:, t, :], ln_row, ALU.add)
        m_v = m
        s_buf = Buffers([ln_row[:, 0:T], ln_row[:, T:2 * T]])
        g_buf = Buffers([ln_row[:, 2 * T:3 * T], ln_row[:, 3 * T:4 * T]])

        def sink_spatial(tile, bank, m):
            g = tile // 2
            i, gv, gfree = g_buf.take()
            a = activate([m, m_v] + gfree, gv, bank, ACT.Silu)
            b, sbank, free = held.take()
            for t in range(TT):
                m = matmuls(free + [m_v, m_ws], [(v_tok[:, t, tile * P:(tile + 1) * P], w_sT[:, g, :])],
                            sbank[:, t * P:(t + 1) * P])
            j, sv, sfree = s_buf.take()
            m = tt([m, b_s_in, m_v] + sfree, sv.rearrange("p (a b) -> p a b", a=TT),
                   sbank[:, :].rearrange("p (a b) -> p a b", a=TT), b_s[:, g, :].unsqueeze(1).to_broadcast([P, TT, P]),
                   ALU.add)
            held.release(b, m)
            m = tt([m], sv, sv, uT[:, tile, :], ALU.mult)
            m = tt([m, a], uT[:, tile, :], sv, gv, ALU.mult)
            s_buf.release(j, m)
            g_buf.release(i, m)
            return [a]

        project(DK, h_tile, [m_h], AW // P, sink_spatial)
        m_y = dve.mark()

        def sink_add(tile, bank, m):
            return [tt([m], xT[:, tile, :], xT[:, tile, :], bank, ALU.add)]

        project(AW // P, lambda k: uT[:, k, :], [m_y], DK, sink_add)
        m_x = dve.mark()
        show("xT3", xT[:, :, :], [m_x])
        if stop == "a":
            return finish(join())

        room = Room(work)
        yT = room.take(P, BT, T)
        gate_w = room.take(P, 2, BT, P)
        padded = Buffers([room.take(P, T + 8)[:, 0:T + 3] for _ in range(2)])
        conv_buf = Buffers([room.take(P, T) for _ in range(4)])
        tmp = Buffers([room.take(P, 5, T) for _ in range(2)])
        lam = room.take(P, BT)
        tmp4 = [room.take(P, BT) for _ in range(4)]
        start = join()
        gate_load = Load(semaphore("gate_w_in"))
        for j, name in enumerate(("b_gate_a_w_2", "b_gate_x_w_2")):
            gate_in = gate_load.start(act, start, gate_w[:, j, :, :], io[name][0].rearrange("h i j -> i h j"))
        m = ts([vec_in] + start, lam, V("b_lambda_2", 0, BT), -1.0, ALU.mult)
        m = softplus([m], lam, lam, tmp4)
        m_lam = ts([m], lam, lam, 8.0, ALU.mult)
        m_h = normalise(("norm_w_2", 8), None, [m_x] + start)
        pads = [dve.do(start, lambda e, v=v: e.memset(v[:, 0:3], 0.0)) for v in padded.views]
        convolved = {}

        def sink_branch(tile, bank, m):
            i, cv, cfree = conv_buf.take()
            dve.quiet(cfree, None)
            bank_read, m = convolve(tile, bank, m, "b_conv_w_2", BT, cv)
            m = ts([m], cv, cv, V("b_conv_b_2", tile), ALU.add)
            convolved[tile] = (i, cv, m)
            return [bank_read]

        def sink_rglru(tile, bank, m):
            i, cv, m_c = convolved.pop(tile)
            k, tv, tfree = tmp.take()
            r, inp, a_, gz, tau = (tv[:, j, :] for j in range(5))
            m_gz = activate([m] + tfree + start, gz, bank, ACT.Silu)
            for j, (o, name) in enumerate(((r, "b_gate_a_b_2"), (inp, "b_gate_x_b_2"))):
                b, gbank, free = held.take()
                m = matmuls(free + [m_c, gate_in], [(gate_w[:, j, tile, :], cv)], gbank[:, :])
                m = activate([m], o, gbank[:, :], ACT.Sigmoid, bias=V(name, tile))
                held.release(b, m)
            m = ts([m, m_lam], r, r, lam[:, tile:tile + 1], ALU.mult)
            m_a = activate([m], a_, r, ACT.Exp, scale=-1.0)
            m = activate([m], tau, r, ACT.Tanh)
            m2 = tt([m], inp, inp, cv, ALU.mult)
            conv_buf.release(i, m2)
            m = ts([m], r, tau, 1.0, ALU.add)
            m = dve.do([m], lambda e: e.reciprocal(r, r))
            m = stt([m], tau, tau, 2.0, r, ALU.mult, ALU.mult)
            m = activate([m], tau, tau, ACT.Sqrt)
            m = tt([m, m2], inp, inp, tau, ALU.mult)
            m = dve.do([m, m_a], lambda e: e.tensor_tensor_scan(r, a_, inp, 0.0, ALU.mult, ALU.add))
            m = tt([m, m_gz], yT[:, tile, :], r, gz, ALU.mult)
            tmp.release(k, m)
            return [m_gz]

        for blk in range(BT // 2):
            project(DK, h_tile, [m_h], 2, lambda tile, bank, m: sink_branch(2 * blk + tile, bank, m))
            project(DK, h_tile, [m_h], 2, lambda tile, bank, m: sink_rglru(2 * blk + tile, bank, m))
        m_y = dve.mark()
        project(BT, lambda k: yT[:, k, :], [m_y], DK, sink_add)
        m_x = dve.mark()

        m_h = normalise(("norm_f_w_2", 0), None, [m_x, pe.mark()])
        room = Room(work)
        o_buf = [room.take(P, D) for _ in range(TT)]
        start = join()
        out_store = Load(semaphore("out_store"))
        for t in range(TT):
            for j in range(0, DK, 4):
                b, bank, free = banks.take()
                for q in range(4):
                    m = transpose(free + [m_h], bank[:, q * P:(q + 1) * P], hT[:, j + q, t * P:(t + 1) * P])
                m = copy((act, dve)[j // 4], [m] + start, o_buf[t][:, j * P:(j + 4) * P], bank[:, :])
                banks.release(b, m)
            stored = out_store.start(act, [m, act.mark()], out[0][t * P:(t + 1) * P, :], o_buf[t])
        stores.append(stored)
        finish(join())


def packed_vectors(i):
    out = np.zeros((P, NVEC), np.float32)

    def put(name, value):
        a, n = VEC[name]
        out[:, a:a + n] = value

    for name in ("c", "b_ada", "norm_mix", "norm_ffn", "kv_norm", "conv_w", "conv_b", "ssm_norm", "norm_w_2",
                 "b_conv_w_2", "b_conv_b_2", "b_gate_a_b_2", "b_gate_x_b_2", "b_lambda_2", "norm_f_w_2"):
        put(name, np.asarray(i[name]).reshape(-1, P).T)
    for name in ("q_norm", "k_norm", "idx_k_ln_w", "idx_k_ln_b"):
        put(name, np.tile(np.asarray(i[name]).reshape(-1), 2)[:, None])
    put("d_skip", np.repeat(np.asarray(i["d_skip"]).reshape(-1), SP_).reshape(-1, P).T)
    for name in ("dt_bias", "a_log", "b_router"):
        put(name, np.broadcast_to(np.asarray(i[name]).reshape(1, -1), (P, VEC[name][1])))
    return out


_WEIGHTS = ["x", "rel_bias", "w_ada", "w_in", "w_kv_up", "w_attn_o", "w_ssm_o", "w_out", "w_router", "w_gu", "b_gu",
            "w_dn", "b_dn", "a_w_in_2", "a_ln_w_2", "a_ln_b_2", "a_w_s_2", "a_b_s_2", "a_w_out_2", "b_w_in_2",
            "b_gate_a_w_2", "b_gate_x_w_2", "b_w_out_2"]


def make(nc, inputs, debug=None, stop=None):
    arrays = {name: np.ascontiguousarray(inputs[name]) for name in _WEIGHTS}
    arrays["vec"] = packed_vectors(inputs)
    arrays["con"] = shape_constants()
    io = {n: nc.dram_tensor(f"in_{n}", a.shape, F32, kind="ExternalInput").ap() for n, a in arrays.items()}
    out = nc.dram_tensor("out_x", (1, T, D), F32, kind="ExternalOutput").ap()
    dbg = {n: nc.dram_tensor(f"dbg_{n}", s, F32, kind="ExternalOutput").ap() for n, s in (debug or {}).items()}
    build(nc, io, out, dbg, stop)
    return {f"in_{n}": a for n, a in arrays.items()}


def kernel(**inputs):
    import concourse.bacc as bacc
    from concourse.bass_utils import run_bass_kernel_spmd
    nc = bacc.Bacc("TRN2", target_bir_lowering=False, num_devices=1, dynamic_dma_scratch_size=8192)
    arrays = make(nc, inputs)
    return run_bass_kernel_spmd(nc, [arrays], core_ids=[0]).results[0]["out_x"]
```

```python
import math
from contextlib import ExitStack

import numpy as np

import concourse.bass as bass
from concourse import mybir
from concourse.alu_op_type import AluOpType as ALU

F32, I32, BF16 = mybir.dt.float32, mybir.dt.int32, mybir.dt.bfloat16
ACT, AX = mybir.ActivationFunctionType, mybir.AxisListType

P = 128
T = 512
TT = T // P
D = 1024
DK = D // P
H, HD = 8, 64
TOPK = 128
NB, MAXD = 32, 128
SH, SP_ = 16, 64
SG, SN = 2, 128
CT = 12
E, EK = 32, 4
OB = T * EK // P
AW = 2048
BW = 1536
BT = BW // P
EPS, LN_EPS = 1e-6, 1e-5
NEG = -1.0e30
C_Q, C_KV, C_QI, C_KI, C_WI, C_Z, C_X, C_DT, C_G = 0, 512, 768, 1280, 1344, 1352, 2376, 3912, 3928
SLOT = 2048
RING = 6
ROOM = 28800

VEC = {}
for _name, _n in [("c", 8), ("b_ada", 48), ("norm_mix", 8), ("norm_ffn", 8), ("kv_norm", 2), ("conv_w", 48),
                  ("conv_b", 12), ("ssm_norm", 8), ("norm_w_2", 16), ("b_conv_w_2", 48), ("b_conv_b_2", 12),
                  ("b_gate_a_b_2", 12), ("b_gate_x_b_2", 12), ("b_lambda_2", 12), ("norm_f_w_2", 8),
                  ("q_norm", 1), ("k_norm", 1), ("idx_k_ln_w", 1), ("idx_k_ln_b", 1), ("d_skip", 8),
                  ("dt_bias", 16), ("a_log", 16), ("b_router", 32)]:
    VEC[_name] = (sum(n for _, n in VEC.values()), _n)
NVEC = sum(n for _, n in VEC.values())

CON = {}
for _name, _n in [("ident", P), ("ones", P), ("heads", P), ("tri", P), ("after", P), ("before", P),
                  ("causal", T), ("slot", P), ("flip", P), ("ebase", E), ("eone", E), ("tok", 2), ("bucket", T + P)]:
    CON[_name] = (sum(n for _, n in CON.values()), _n)
NCON = sum(n for _, n in CON.values())


def shape_constants():
    k = np.arange(P)
    out = np.zeros((P, NCON), np.float32)

    def put(name, value):
        a, n = CON[name]
        out[:value.shape[0], a:a + n] = value

    put("ident", np.eye(P))
    put("ones", np.ones((P, P)))
    put("heads", (k[:, None] // HD == k[None] // HD) * 1.0)
    put("tri", (k[:, None] <= k[None]) * 1.0)
    put("after", (k[:, None] > k[None]) * 1.0)
    put("before", (k[:, None] < k[None]) * 1.0)
    put("causal", np.where(np.arange(T)[None] <= k[:, None] + T - P, 0.0, NEG))
    put("slot", np.broadcast_to(k[None] * 1.0, (P, P)))
    put("flip", np.eye(P)[::-1])
    put("ebase", np.broadcast_to(np.arange(E)[None] * float(P), (P, E)))
    put("eone", np.broadcast_to(np.arange(E)[None] * 1.0, (P, E)))
    put("tok", np.stack([k * 1.0, np.ones(P)], 1))
    dist = np.maximum(T - 1 - np.arange(T + P), 0)
    nf = np.maximum(dist, 1).astype(np.float32)
    far = NB // 2 + (np.log(nf / (NB // 2)) / math.log(MAXD / (NB // 2)) * (NB - NB // 2)).astype(np.int32)
    bucket = np.where(dist < NB // 2, dist, np.minimum(far, NB - 1))
    put("bucket", (bucket[None] == np.arange(NB)[:, None]) * 1.0)
    return out


class Engine:

    def __init__(self, sem):
        self.sem, self.count, self.queue, self.seen = sem, 0, [], {}

    def do(self, after, issue):
        self.quiet(after, issue, self.sem)
        self.count += 1
        return (self.sem, self.count)

    def quiet(self, after, issue, sem=None, step=1):
        self.queue.append(([m for m in after if m], issue, sem, step))

    def mark(self):
        return (self.sem, self.count) if self.count else None

    def emit(self, eng, queue):
        seen = self.seen
        for marks, issue, sem, step in queue:
            for s, value in marks:
                if seen.get(s.name, 0) < value:
                    eng.wait_ge(s, value)
                    seen[s.name] = value
            if issue is not None:
                ins = issue(eng)
                if ins is not None and sem is not None:
                    ins.then_inc(sem, step)


class Buffers:

    def __init__(self, views):
        self.views, self.free, self.at = views, [[] for _ in views], -1

    def take(self):
        self.at = (self.at + 1) % len(self.views)
        return self.at, self.views[self.at], self.free[self.at]

    def release(self, i, *marks):
        self.free[i] = list(marks)


class Room:

    def __init__(self, view, start=0):
        self.view, self.at = view, start

    def take(self, *shape, dt=None):
        n = int(np.prod(shape[1:]))
        words = n if dt is not BF16 else (n + 1) // 2
        v = self.view[0:shape[0], self.at:self.at + words]
        self.at += (words + 7) // 8 * 8
        assert self.at <= ROOM, self.at
        if dt is not None:
            v = v.bitcast(dt)
        if len(shape) == 3:
            v = v.rearrange("p (a b) -> p a b", a=shape[1])
        elif len(shape) == 4:
            v = v.rearrange("p (a b c) -> p a b c", a=shape[1], b=shape[2])
        return v


class Load:

    def __init__(self, sem):
        self.sem, self.count = sem, 0

    def start(self, queue, after, out, in_, parts=1):
        self.count += 16
        queue.quiet(after, lambda e: e.dma_start(out, in_() if callable(in_) else in_), self.sem, 16)
        return (self.sem, self.count)


def build(nc, io, out, debug=None, stop=None):
    stack = ExitStack()
    with stack:
        def sb(name, shape, dt=F32, where=stack):
            return where.enter_context(nc.sbuf_tensor(name, shape, dt))

        def semaphore(name):
            return stack.enter_context(nc.semaphore(name))

        pe, act, dve, pool, sp = (Engine(semaphore(n)) for n in
                                  ("pe_done", "act_done", "dve_done", "pool_done", "sp_done"))

        vec = sb("vec", [P, NVEC])
        con = sb("con", [P, NCON])
        xT = sb("xT", [P, DK, T])
        hT = sb("hT", [P, DK, T])
        ring = sb("ring", [P, RING, SLOT])
        mod = sb("mod", [P, 48])
        rs_v, rs_t = sb("rs_v", [P, T]), sb("rs_t", [P, T])
        rs_y = sb("rs_y", [P, 2, T])
        sq = sb("sq", [P, 2, T])
        cond, one_plus = sb("cond", [P, DK]), sb("one_plus", [P, DK])
        over_i = sb("over_i", [P, 8], I32)
        work = sb("work", [P, ROOM])
        psum = [stack.enter_context(nc.psum_tensor(f"bank{i}", [P, 512], F32)) for i in range(8)]
        banks = Buffers(psum[:5])
        held = Buffers(psum[5:6])
        dense = Buffers(psum[6:])

        def V(name, j=0, n=None):
            a, w = VEC[name]
            return vec[:, a + j:a + j + (n or 1)] if n is not None or w > 1 else vec[:, a:a + 1]

        def C(name, rows=P, lo=0, n=None):
            a, w = CON[name]
            return con[0:rows, a + lo:a + lo + (n or w)]

        ident, ones = C("ident"), C("ones")

        bias_dram = nc.dram_tensor("bias_rows", (H, T + P), F32).ap()
        h_dram = nc.dram_tensor("h_rows", (T, D), F32).ap()
        y_dram = nc.dram_tensor("expert_rows", (E * P, D), F32).ap()
        over_dram = nc.dram_tensor("overflow_rows", (OB * P, D), F32).ap()

        vec_in = Load(semaphore("vec_in")).start(act, [], vec[:, :], io["vec"])
        con_in = Load(semaphore("con_in")).start(act, [], con[:, :], io["con"])

        chunks = []

        def plan(src, k, n):
            chunks.append((src, k, n))

        class Weights:

            def __init__(self, name, view, slots, plan, start=()):
                self.view, self.slots, self.plan = view, slots, plan
                self.started = self.used = self.released = 0
                self.sems = [semaphore(f"{name}{i}") for i in range(slots)]
                self.free = [list(start) for _ in range(slots)]

            def start_next(self):
                if self.started < len(self.plan):
                    i, (src, k, n) = self.started, self.plan[self.started]
                    slot = i % self.slots
                    dst = self.view[:, slot, 0:k * n].rearrange("p (k n) -> p k n", k=k)
                    sp.quiet(self.free[slot], lambda e: e.dma_start(dst, src() if callable(src) else src),
                             self.sems[slot], 16)
                    self.started += 1

            def next(self):
                i = self.used
                _, k, n = self.plan[i]
                self.used += 1
                slot = i % self.slots
                return (self.view[:, slot, 0:k * n].rearrange("p (k n) -> p k n", k=k),
                        (self.sems[slot], 16 * (i // self.slots + 1)))

            def done(self, mark):
                self.free[self.released % self.slots] = [mark]
                self.released += 1
                self.start_next()

            def last_marks(self):
                return [(self.sems[i % self.slots], 16 * (i // self.slots + 1)) for i in range(self.started)][-self.slots:]

        weights = Weights("ring", ring, RING, chunks)

        def rows(w, cols=None):
            w = w if cols is None else w[:, cols[0]:cols[1]]
            return w.rearrange("(k p) n -> p k n", p=P)

        def plan_columns(w, lo, hi, step):
            for a in range(lo, hi, step):
                plan(rows(w, (a, a + step)), w.shape[0] // P, step)

        w_ada, w_in = io["w_ada"][0], io["w_in"][0]
        for k in range(DK):
            plan(w_ada[k * P:(k + 1) * P, 0:2048].unsqueeze(1), 1, 2048)
        plan_columns(w_in, C_KV, C_KV + 256, 256)
        plan(rows(io["w_kv_up"][0]), 2, 1024)
        plan_columns(w_in, C_Q, C_Q + 512, 256)
        plan_columns(w_in, C_QI, C_QI + 512, 256)
        plan_columns(w_in, C_X, C_X + 1536, 256)
        plan_columns(w_in, C_Z, C_Z + 1024, 256)
        for b in range(4):
            for i, (w, lo) in enumerate(((w_in, C_G), (io["w_attn_o"][0], 0), (w_in, C_G + 1024), (io["w_ssm_o"][0], 0))):
                plan_columns(w, lo + 256 * b, lo + 256 * b + 256, 256)
                half, k = divmod(4 * b + i, DK)
                a = 2048 + 2048 * half
                plan(w_ada[k * P:(k + 1) * P, a:a + 2048].unsqueeze(1), 1, 2048)
        plan_columns(io["w_out"][0], 0, D, 256)

        def plan_up(e):
            for k in range(DK):
                plan(io["w_gu"][0][e][k * P:(k + 1) * P, :].unsqueeze(1), 1, 2048)

        def plan_down(e):
            for k in range(0, DK, 2):
                plan(rows(io["w_dn"][0][e][k * P:(k + 2) * P, :]), 2, 1024)

        plan_up(0)
        for e in range(1, E):
            plan_up(e)
            plan_down(e - 1)
        plan_down(E - 1)
        plan_columns(io["a_w_in_2"][0], 0, 3 * AW, 256)
        plan_columns(io["a_w_out_2"][0], 0, D, 128)
        for b in range(BW // 256):
            plan_columns(io["b_w_in_2"][0], 256 * b, 256 * b + 256, 256)
            plan_columns(io["b_w_in_2"][0], BW + 256 * b, BW + 256 * b + 256, 256)
        plan_columns(io["b_w_out_2"][0], 0, D, 128)
        for _ in range(RING):
            weights.start_next()

        def matmuls(after, pairs, o, start=True, stop=True):
            for i, (lhsT, rhs) in enumerate(pairs):
                last = i == len(pairs) - 1
                f = (lambda e, l=lhsT, r=rhs, s=(start and i == 0), t=(stop and last):
                     e.matmul(o, l, r, start=s, stop=t))
                if last:
                    return pe.do(after if i == 0 else [], f)
                pe.quiet(after if i == 0 else [], f)

        def transpose(after, o, in_):
            return pe.do(after, lambda e: e.transpose(o, in_, ident))

        def copy(eng, after, o, in_, scale=None):
            if eng is act:
                return act.do(after, lambda e: e.activation(o, in_, ACT.Copy, scale=1.0 if scale is None else scale))
            return eng.do(after, lambda e: e.tensor_copy(o, in_) if scale is None else
                          e.tensor_scalar(o, in_, scale, None, ALU.mult))

        def activate(after, o, in_, f, **kw):
            return act.do(after, lambda e: e.activation(o, in_, f, **kw))

        def tt(after, o, a, b, op, eng=None):
            return (eng or dve).do(after, lambda e: e.tensor_tensor(o, a, b, op))

        def ts(after, o, a, s1, op0, s2=None, op1=None, eng=None):
            if op1 is None:
                return (eng or dve).do(after, lambda e: e.tensor_scalar(o, a, s1, None, op0))
            return (eng or dve).do(after, lambda e: e.tensor_scalar(o, a, s1, s2, op0, op1))

        def stt(after, o, a, s, b, op0, op1):
            return dve.do(after, lambda e: e.scalar_tensor_tensor(out=o, in0=a, scalar=s, in1=b, op0=op0, op1=op1))

        rs_ring = Buffers([0, 1])
        sq_ring = Buffers([sq[:, 0, :], sq[:, 1, :]])

        def rsqrt(after, total, n, eps):
            i, j, free = rs_ring.take()
            v, y, t = rs_v[:, :], rs_y[:, j, :], rs_t[:, :]
            m = ts(after + free, v, total, 1.0 / n, ALU.mult, eps, ALU.add)
            a = activate([m] + free, y, v, ACT.Ln)
            a = activate([a], y, y, ACT.Exp, scale=-0.5)
            m = tt([a], t, y, y, ALU.mult)
            m = tt([m], t, t, v, ALU.mult)
            m = ts([m], t, t, -0.5, ALU.mult, 1.5, ALU.add)
            m = tt([m], y, y, t, ALU.mult)
            return i, y, m

        def sum_squares(tiles, after, lhs, n, eps):
            b, bank, free = banks.take()
            for i, x in enumerate(tiles):
                s, sv, sfree = sq_ring.take()
                a = activate(after + sfree, sv, x, ACT.Square)
                m = pe.do([a] + (free if i == 0 else []),
                          lambda e, sv=sv, i=i: e.matmul(bank[:, :], lhs, sv, start=(i == 0), stop=(i == len(tiles) - 1)))
                sq_ring.release(s, m)
            i, y, m = rsqrt([m], bank[:, :], n, eps)
            banks.release(b, m)
            return i, y, m

        def project_steps(ktiles, source, after, n_tiles, sink, step=2):
            tile = 0
            while tile < n_tiles:
                w, arrived = weights.next()
                for c in range(w.shape[2] // P):
                    b, bank, free = dense.take()
                    for k in range(0, ktiles, step):
                        m = matmuls(after + free + [arrived],
                                    [(w[:, kk, c * P:(c + 1) * P], source(kk)) for kk in range(k, k + step)],
                                    bank[:, :], start=(k == 0), stop=(k + step == ktiles))
                        if k + step < ktiles:
                            yield
                    last = m
                    dense.release(b, *sink(tile, bank[:, :], m))
                    tile += 1
                    yield
                weights.done(last)

        def project(ktiles, source, after, n_tiles, sink):
            run(project_steps(ktiles, source, after, n_tiles, sink, ktiles))

        def run(steps, n=None):
            while n is None or n > 0:
                if next(steps, run) is run:
                    return
                n = n if n is None else n - 1

        def join():
            return [e.mark() for e in (pe, act, dve, pool)]

        def softplus(after, o, x, tmp):
            ax, u, s, z = tmp
            m = activate(after, ax, x, ACT.Abs)
            a = activate([m], u, ax, ACT.Exp, scale=-1.0)
            m = ts([a], ax, u, 2.0, ALU.add)
            m = dve.do([m], lambda e: e.reciprocal(ax, ax))
            m = tt([m], s, u, ax, ALU.mult)
            m = tt([m], z, s, s, ALU.mult)
            m = ts([m], u, z, 1.0 / 17, ALU.mult)
            for d in (15, 13, 11, 9, 7, 5, 3):
                m = stt([m], u, u, 1.0 / d, z, ALU.add, ALU.mult)
            m = stt([m], u, u, 1.0, s, ALU.add, ALU.mult)
            m = ts([m], ax, x, 0.0, ALU.max)
            return stt([m], o, u, 2.0, ax, ALU.mult, ALU.add)

        def show(name, view, after):
            if debug is not None and name in debug:
                s = Load(semaphore("dbg_" + name))
                dbg_marks.append(s.start(act, after, debug[name], view))

        dbg_marks = []
        stores = []

        def finish(after):
            sp.quiet(after + dbg_marks + stores + weights.last_marks(), None)
            close_part(None)
            for engines, flag in parts:
                if flag is None:
                    emit_part(engines)
                else:
                    taken = nc.values_load(flag, min_val=0, max_val=1)
                    with nc.If(taken > 0):
                        emit_part(engines)

        parts = []

        def close_part(flag):
            engines = (pe, act, dve, pool, sp)
            parts.append(([(e, e.queue) for e in engines], flag))
            for e in engines:
                e.queue = []

        def emit_part(engines):
            with nc.Block() as block:
                for (engine, queue), on in zip(engines, (block.tensor, block.scalar, block.vector, block.gpsimd, block.sync)):
                    on(lambda e, engine=engine, queue=queue: engine.emit(e, queue))

        phase = Room(work)
        x_tok = phase.take(P, TT, D)
        x_in = Load(semaphore("x_in")).start(act, [], x_tok[:, :, :], io["x"][0].rearrange("(t p) d -> p t d", p=P))
        m_cond = activate([vec_in], cond[:, :], V("c", 0, 8), ACT.Silu)

        mod_mark = {}

        def modulation(block, after, ada):
            m = None
            for k in range(DK):
                w, arrived = weights.next()
                if k == 0:
                    m = ts([arrived, m_cond] + after, ada[:, :], w[:, 0, :], cond[:, k:k + 1], ALU.mult)
                else:
                    m = stt([arrived, m], ada[:, :], w[:, 0, :], cond[:, k:k + 1], ada[:, :], ALU.mult, ALU.add)
                weights.done(m)
                if k < DK - 1:
                    yield
            b, bank, free = banks.take()
            for j in range(16):
                p_ = pe.do([m, con_in] + free, lambda e, j=j: e.matmul(bank[:, j:j + 1], ada[:, j * P:(j + 1) * P],
                                                             ones[:, 0:1], start=True, stop=True))
            ada_read[:] = [p_]
            m = tt([p_, vec_in], mod[:, 16 * block:16 * block + 16], bank[:, 0:16], V("b_ada", 16 * block, 16), ALU.add)
            banks.release(b, m)
            mod_mark[block] = m
            yield

        ada_read = []
        for k in range(DK):
            b, bank, free = banks.take()
            for t in range(TT):
                m = transpose([x_in, con_in] + free, bank[:, t * P:(t + 1) * P], x_tok[:, t, k * P:(k + 1) * P])
            m = copy(act, [m], xT[:, k, :], bank[:, :])
            banks.release(b, m)
        m_x = m
        run(modulation(0, [], phase.take(P, 2048)))
        m_mod = mod_mark[0]

        def normalise(gain, shift_block, m_ready):
            i, rs, m_rs = sum_squares([xT[:, k, :] for k in range(DK)], m_ready, ones, D, EPS)
            for k in range(DK):
                m = stt([m_rs], hT[:, k, :], xT[:, k, :], V(gain[0], gain[1] + k), rs, ALU.mult, ALU.mult)
                if shift_block is not None:
                    m1 = activate([m], hT[:, k, :], hT[:, k, :], ACT.Identity,
                                  scale=one_plus[:, k:k + 1], bias=mod[:, shift_block * 8 + k:shift_block * 8 + k + 1])
            rs_ring.release(i, m)
            return m1 if shift_block is not None else m

        m_op = ts([m_mod], one_plus[:, :], mod[:, 8:16], 1.0, ALU.add)
        m_h = normalise(("norm_mix", 0), 0, [m_x, m_op])
        show("hT", hT[:, :, :], [m_h])
        if stop == "h":
            return finish([m_h])

        room = Room(work)
        oT = room.take(P, 4, T)
        yT = room.take(P, 8, T)
        wi_dt = room.take(P, TT, 24)
        bcT = room.take(P, 4, T)
        padded = Buffers([room.take(P, T + 8)[:, 0:T + 3] for _ in range(2)])
        after_conv = room.at
        qT, kT, qiT = (room.take(P, 4, T) for _ in range(3))
        kiT = room.take(P, T)
        v_tok = room.take(P, TT, T)
        kvT_at = room.at
        kvT = room.take(P, 2, T)
        rawT = room.take(P, 2, T)
        start = join()

        narrow = room.take(P, DK, 152)
        narrow_in = Load(semaphore("narrow_in"))
        for dst, lo, n in ((0, C_KI, 64), (64, C_KI, 64), (128, C_WI, 8), (136, C_DT, 16)):
            m_narrow = narrow_in.start(act, start, narrow[:, :, dst:dst + n], rows(w_in, (lo, lo + n)))

        bias_row = room.take(8, T + P)
        rel = room.take(NB, 8)
        rel_in = Load(semaphore("rel_in")).start(act, start, rel, io["rel_bias"])
        for lo, n in ((0, T), (T, P)):
            b, bank, free = banks.take()
            m = matmuls(free + [rel_in, con_in], [(rel, C("bucket", NB, lo, n))], bank[0:8, 0:n])
            m = copy(dve, start + [m], bias_row[:, lo:lo + n], bank[0:8, 0:n])
            banks.release(b, m)
        bias_out = Load(semaphore("bias_out")).start(act, [m], bias_dram[:, :], bias_row)
        stores.append(bias_out)

        def h_tile(k):
            return hT[:, k, :]

        raw_ring = Buffers([rawT[:, 0, :], rawT[:, 1, :]])

        def keep_raw(bank, m, scale=None):
            r, raw, rfree = raw_ring.take()
            return r, raw, copy(act, [m] + rfree + start, raw, bank, scale)

        def sink_kv(tile, bank, m):
            return [copy(act, [m] + start, kvT[:, tile, :], bank)]

        project(DK, h_tile, [m_h], 2, sink_kv)
        m_kv = act.mark()
        i, rs, m = sum_squares([kvT[:, j, :] for j in range(2)], [m_kv], ones, 256, EPS)
        for j in range(2):
            m = stt([m], kvT[:, j, :], kvT[:, j, :], V("kv_norm", j), rs, ALU.mult, ALU.mult)
        rs_ring.release(i, m)
        m_kv = m

        gains = room.take(P, 2)
        m_gain = ts([vec_in] + start, gains[:, 0:1], V("q_norm"), HD ** -0.5, ALU.mult)
        heads = C("heads")

        def head_norm(dst, gain):
            def sink(tile, bank, m):
                r, raw, m = keep_raw(bank, m)
                i, rs, m2 = sum_squares([raw], [m], heads, HD, EPS)
                m2 = stt([m2, m_gain], dst[:, tile, :], raw, gain, rs, ALU.mult, ALU.mult)
                rs_ring.release(i, m2)
                raw_ring.release(r, m2)
                return [m]
            return sink

        w_up, arrived = weights.next()
        for c in range(4):
            b, bank, free = banks.take()
            m = matmuls(free + [arrived, m_kv], [(w_up[:, k, c * P:(c + 1) * P], kvT[:, k, :]) for k in range(2)],
                        bank[:, :])
            banks.release(b, *head_norm(kT, V("k_norm"))(c, bank[:, :], m))
        for t in range(TT):
            b, bank, free = banks.take()
            m = matmuls(free + [arrived, m_kv], [(kvT[:, k, t * P:(t + 1) * P], w_up[:, k, 512:1024]) for k in range(2)],
                        bank[:, :])
            if t == TT - 1:
                weights.done(m)
            m = copy(act, [m] + start, v_tok[:, t, :], bank[:, :])
            banks.release(b, m)
        project(DK, h_tile, [m_h], 4, head_norm(qT, gains[:, 0:1]))
        project(DK, h_tile, [m_h], 4, lambda tile, bank, m: [copy(act, [m] + start, qiT[:, tile, :], bank, HD ** -0.5)])

        b, bank, free = banks.take()
        m = matmuls(free + [m_narrow], [(narrow[:, k, 0:P], hT[:, k, :]) for k in range(DK)], bank[:, :])
        r, raw, m = keep_raw(bank[:, :], m)
        banks.release(b, m)
        b, bank, free = banks.take()
        m = matmuls(free + [m], [(heads, raw)], bank[:, :])
        m = stt([m], raw, bank[:, :], -1.0 / HD, raw, ALU.mult, ALU.add)
        banks.release(b, m)
        i, rs, m = sum_squares([raw], [m], heads, HD, EPS)
        m = tt([m], kiT, raw, rs, ALU.mult)
        rs_ring.release(i, m)
        raw_ring.release(r, m)
        m_ki = ts([m], kiT, kiT, V("idx_k_ln_w"), ALU.mult, V("idx_k_ln_b"), ALU.add)

        b, bank, free = banks.take()
        for t in range(TT):
            m = matmuls(free + [m_narrow], [(hT[:, k, t * P:(t + 1) * P], narrow[:, k, 128:152]) for k in range(DK)],
                        bank[:, 24 * t:24 * t + 24])
        m = copy(dve, [m] + start, wi_dt.rearrange("p a b -> p (a b)"), bank[:, 0:96])
        banks.release(b, m)
        m_wi = ts([m], wi_dt[:, :, 0:8], wi_dt[:, :, 0:8], H ** -0.5, ALU.mult)
        show("qT", qT, join()); show("kT", kT, join()); show("v", v_tok, join()); show("kiT", kiT, join())
        show("qiT", qiT, join()); show("widt", wi_dt, join())
        if stop == "att_in":
            return finish(join())

        room.at = kvT_at
        bias = room.take(P, H, T)
        keep_buf = [room.take(P, T) for _ in range(2)]
        score, sel_a, sel_b = (room.take(P, T) for _ in range(3))
        best = room.take(P, 8)
        count = room.take(P, 2)
        logit_buf = Buffers([room.take(P, T) for _ in range(3)])
        prob_t_buf = Buffers([room.take(P, T) for _ in range(2)])
        stats = room.take(P, TT * H, 3)
        start = join()
        row = bias_dram[0:1, 0:1]
        bias_src = bass.AP(row.tensor, row.offset, [[1, P], [T + P, H], [1, T]])
        m_bias = Load(semaphore("bias_in")).start(act, start + [bias_out], bias, bias_src)

        pads = [dve.do(start, lambda e, v=v: e.memset(v[:, 0:3], 0.0)) for v in padded.views]

        def convolve(tile, bank, m, w_name, tiles, o):
            i, pv, pfree = padded.take()
            m = copy(act, [m, pads[i]] + pfree + start, pv[:, 3:], bank)
            bank_read = m
            m = ts([m] + start, o, pv[:, 0:T], V(w_name, tile), ALU.mult)
            for tap in range(1, 4):
                m = stt([m], o, pv[:, tap:tap + T], V(w_name, tap * tiles + tile), o, ALU.mult, ALU.add)
            padded.release(i, m)
            return bank_read, m

        def channels(tile):
            return yT[:, tile, :] if tile < 8 else bcT[:, tile - 8, :]

        def sink_conv(tile, bank, m):
            bank_read, conv_mark[tile] = convolve(tile, bank, m, "conv_w", CT, channels(tile))
            return [bank_read]

        conv_mark = {}
        convolution = project_steps(DK, h_tile, [m_h], CT, sink_conv)

        def select(after, src, width, k, cap_a, cap_b, o):
            m = None
            rounds = k // 8
            cur = src
            for r in range(rounds):
                m = dve.do((after if r == 0 else []) + [m], lambda e, cur=cur: e.max(best, cur))
                yield
                if r < rounds - 1:
                    m = dve.do([m], lambda e, cur=cur: e.match_replace(cap_a, best, cur, -3.0e38))
                    cur = cap_a
                    yield
            return threshold(after + [m], src, width, k, best[:, 7:8], cap_a, cap_b, o, count)

        def threshold(after, src, width, k, kth, cap_a, cap_b, o, count):
            m = dve.do(after, lambda e: e.tensor_scalar(o, src, kth, None, ALU.is_gt, ALU.add, accum_out=count[:, 0:1]))
            m = ts([m], count[:, 1:2], count[:, 0:1], -1.0, ALU.mult, float(k), ALU.add)
            m = ts([m], cap_a, src, kth, ALU.is_equal)
            m = dve.do([m], lambda e: e.tensor_tensor_scan(cap_b, cap_a, cap_a, 0.0, ALU.add, ALU.bypass))
            m = stt([m], cap_b, cap_b, count[:, 1:2], cap_a, ALU.is_le, ALU.mult)
            return tt([m], o, o, cap_b, ALU.add)

        def half_of(h):
            return slice((h % 2) * 64, (h % 2) * 64 + 64)

        keep_mark, keep_read = {}, {}

        def choose(t):
            width = (t + 1) * P
            keep, causal = keep_buf[t % 2][:, 0:width], C("causal", P, T - width, width)
            if t == 0:
                keep_mark[0] = copy(dve, start + [con_in], keep, causal)
                return
            sc = score[:, 0:width]
            for h in range(H):
                b, bank, free = banks.take()
                m = matmuls(free + start, [(qiT[half_of(h), h // 2, t * P:(t + 1) * P], kiT[half_of(h), 0:width])],
                            bank[:, 0:width])
                r, rv, rfree = sq_ring.take()
                m = activate([m] + rfree + start, rv[:, 0:width], bank[:, 0:width], ACT.Relu)
                banks.release(b, m)
                w = wi_dt[:, t, h:h + 1]
                if h == 0:
                    m_sc = ts([m, m_wi, keep_mark[t - 1]] + start, sc, rv[:, 0:width], w, ALU.mult)
                else:
                    m_sc = stt([m, m_sc], sc, rv[:, 0:width], w, sc, ALU.mult, ALU.add)
                sq_ring.release(r, m_sc)
                yield
            m = tt([m_sc], sc, sc, causal, ALU.add)
            m = yield from select([m, keep_read.get(t - 2)], sc, width, TOPK, sel_a[:, 0:width], sel_b[:, 0:width], keep)
            keep_mark[t] = ts([m], keep, keep, 1.0, ALU.subtract, -NEG, ALU.mult)

        run(choose(0))
        run(convolution, 8)
        for h in range(H):
            b, bank, free = banks.take()
            m = matmuls(free + [m_bias], [(C("flip"), bias[:, h, :])], bank[:, :])
            bias_in = copy((dve, act)[h % 2], [m], bias[:, h, :], bank[:, :])
            banks.release(b, bias_in)
        bias_in = [dve.mark(), act.mark()]

        exps, probs = {}, {}

        def exponentials(t, h):
            width = (t + 1) * P
            st = stats[:, t * H + h, :]
            b, bank, free = banks.take()
            m = matmuls(free + start, [(qT[half_of(h), h // 2, t * P:(t + 1) * P], kT[half_of(h), h // 2, 0:width])],
                        bank[:, 0:width])
            l, lv, lfree = logit_buf.take()
            lw, keep = lv[:, 0:width], keep_buf[t % 2][:, 0:width]
            m = tt([m] + bias_in + lfree, lw, bank[:, 0:width], bias[:, h, T - width:T], ALU.add)
            banks.release(b, m)
            m = dve.do([m, keep_mark[t]], lambda e: e.tensor_tensor_reduce(
                out=lw, in0=lw, in1=keep, scale=1.0, scalar=-3.0e38, op0=ALU.add, op1=ALU.max, accum_out=st[:, 0:1]))
            keep_read[t] = m
            m = ts([m], st[:, 0:1], st[:, 0:1], -1.0, ALU.mult)
            exps[t, h] = l, lw, activate([m], lw, lw, ACT.Exp, bias=st[:, 0:1], accum_out=st[:, 1:2])

        def probabilities(t, h):
            width = (t + 1) * P
            st = stats[:, t * H + h, :]
            l, lw, m = exps.pop((t, h))
            m = dve.do([m], lambda e: e.reciprocal(st[:, 2:3], st[:, 1:2]))
            m = ts([m], lw, lw, st[:, 2:3], ALU.mult)
            b, bank, free = banks.take()
            for s in range(t + 1):
                mt = transpose(free + [m], bank[:, s * P:(s + 1) * P], lw[:, s * P:(s + 1) * P])
            logit_buf.release(l, mt)
            q, pt, pfree = prob_t_buf.take()
            m = copy(act, [mt] + pfree + start, pt[:, 0:width], bank[:, 0:width])
            banks.release(b, m)
            probs[t, h] = q, pt, m

        def values(t, h):
            q, pt, m = probs.pop((t, h))
            if h == 0:
                out_bank[:] = held.take()
            ob, obank, ofree = out_bank
            m_o = matmuls([m] + ofree, [(v_tok[:, s, h * HD:(h + 1) * HD], pt[:, s * P:(s + 1) * P]) for s in range(t + 1)],
                          obank[half_of(h), (h // 2) * P:(h // 2 + 1) * P])
            prob_t_buf.release(q, m_o)
            if h == H - 1:
                m = copy(act, [m_o], oT[:, :, t * P:(t + 1) * P], obank[:, :].rearrange("p (a b) -> p a b", a=4))
                held.release(ob, m)

        out_bank = []
        units = [(t, h) for t in range(TT) for h in range(H)]
        for u in range(len(units) + 2):
            if u < len(units):
                t, h = units[u]
                if h == 0:
                    if t:
                        run(choosing)
                    choosing = choose(t + 1) if t + 1 < TT else iter(())
                exponentials(t, h)
            run(choosing, 3)
            if 1 <= u <= len(units):
                probabilities(*units[u - 1])
            run(convolution, 1 + u % 2)
            run(choosing, 3)
            if u >= 2:
                values(*units[u - 2])
        run(convolution)
        m_oT = act.mark()
        show("oT", oT, [m_oT])
        if stop == "att":
            return finish(join())

        room.at = after_conv
        xs_tok = room.take(P, TT, D)
        bm_tok = room.take(P, TT, 2 * SN)
        dt = room.take(P, TT, SH)
        dA = room.take(P, TT, SH)
        a_neg = room.take(P, SH)
        tmp4 = [room.take(P, TT, SH) for _ in range(4)]
        dec = room.take(P, SH)
        x_dt, x_end = room.take(P, D), room.take(P, D)
        cb = room.take(P, 2, P)
        state = room.take(P, D)
        zT = room.take(P, DK, T)
        chunk_at = room.at
        spread = room.take(P, SH, P)
        lmat = room.take(P, SH, P)
        grow = room.take(P, SH, P)
        start = join()

        for tile in range(CT):
            m = activate([conv_mark[tile], vec_in], channels(tile), channels(tile), ACT.Silu, bias=V("conv_b", tile))
        m_xbc = m

        dtb = V("dt_bias", 0, SH).unsqueeze(1).to_broadcast([P, TT, SH])
        m = tt(start + [m_wi], dt, wi_dt[:, :, 8:24], dtb, ALU.add)
        m = softplus([m], dt, dt, tmp4)
        a = activate(start, a_neg, V("a_log", 0, SH), ACT.Exp)
        m = stt([m, a], dA, dt, -1.0, a_neg.unsqueeze(1).to_broadcast([P, TT, SH]), ALU.mult, ALU.mult)
        m_dA = m

        def sink_z(tile, bank, m):
            return [copy(act, [m] + start, zT[:, tile, :], bank)]

        z_steps = project_steps(DK, h_tile, [m_h], 8, sink_z)

        for t in range(TT):
            for j in range(0, 10, 4):
                n = min(4, 10 - j)
                b, bank, free = banks.take()
                for q in range(n):
                    m = transpose(free + [m_xbc], bank[:, q * P:(q + 1) * P], channels(j + q)[:, t * P:(t + 1) * P])
                dst = xs_tok[:, t, j * P:(j + 4) * P] if j < 8 else bm_tok[:, t, :]
                m = copy((act, dve)[j == 4], [m] + start, dst, bank[:, 0:n * P])
                banks.release(b, m)
        m_tok = [act.mark(), dve.mark()]

        tri, after_mask = C("tri"), C("after")
        old = start
        for c in range(TT):
            here = slice(c * P, (c + 1) * P)
            m_spread = tt(old + [m_dA, con_in], spread, dA[:, c, :].unsqueeze(2).to_broadcast([P, SH, P]),
                          tri.unsqueeze(1).to_broadcast([P, SH, P]), ALU.mult)
            xs3 = xs_tok[:, c, :].rearrange("p (h d) -> p h d", h=SH)
            x_dt3, x_end3 = (v.rearrange("p (h d) -> p h d", h=SH) for v in (x_dt, x_end))
            m_xdt = tt(m_tok, x_dt3, xs3, dt[:, c, :].unsqueeze(2).to_broadcast([P, SH, SP_]), ALU.mult)
            b, bank, free = banks.take()
            for g in range(SG):
                m = matmuls(free + [m_xbc], [(bcT[:, g, here], bcT[:, 2 + g, here])], bank[:, g * P:(g + 1) * P])
            m_cb = tt([m] + old, cb, bank[:, 0:2 * P].rearrange("p (a b) -> p a b", a=2),
                      tri.unsqueeze(1).to_broadcast([P, SG, P]), ALU.mult)
            banks.release(b, m_cb)
            b, bank, free = banks.take()
            m = matmuls(free + [m_dA], [(after_mask, dA[:, c, :])], bank[:, 0:SH])
            m_dec = activate([m] + old, dec, bank[:, 0:SH], ACT.Exp)
            banks.release(b, m_dec)
            run(z_steps, 2)
            for lhs, dst in ((after_mask, lmat), (ones, grow)):
                for q in range(4):
                    b, bank, free = banks.take()
                    m = matmuls(free + [m_spread], [(lhs, spread[:, 4 * q:4 * q + 4, :].rearrange("p a b -> p (a b)"))],
                                bank[:, :])
                    m_grown = m
                    m = activate([m] + old, dst[:, 4 * q:4 * q + 4, :].rearrange("p a b -> p (a b)"), bank[:, :], ACT.Exp)
                    banks.release(b, m)
                if dst is lmat:
                    m_lmat = m
            m_grow = m
            m_end = tt([m_dec, m_xdt], x_end3, x_dt3, dec.unsqueeze(2).to_broadcast([P, SH, SP_]), ALU.mult)
            m_w, m_cs = [], []
            for g in range(SG):
                hs = slice(8 * g, 8 * g + 8)
                m_w.append(tt([m_lmat, m_cb], lmat[:, hs, :], lmat[:, hs, :],
                              cb[:, g, :].unsqueeze(1).to_broadcast([P, 8, P]), ALU.mult))
                if c:
                    m_cs.append(tt([m_grow, m_grown, m_xbc], spread[:, hs, :], grow[:, hs, :],
                                   bcT[:, 2 + g, here].unsqueeze(1).to_broadcast([P, 8, P]), ALU.mult))
            run(z_steps, 3)
            m_state = m_new if c else None
            for q in range(2):
                b, bank, free = banks.take()
                for pair in range(4):
                    for half in range(2):
                        h = 8 * q + 2 * pair + half
                        terms = [(x_dt[:, h * SP_:(h + 1) * SP_], lmat[:, h, :])]
                        if c:
                            terms.append((state[:, h * SP_:(h + 1) * SP_], spread[:, h, :]))
                        m = matmuls(free + [m_xdt, m_w[q], m_state] + m_cs[q:q + 1], terms,
                                    bank[half * 64:half * 64 + 64, pair * P:(pair + 1) * P])
                for pair in range(4):
                    tile = 4 * q + pair
                    my = stt([m], yT[:, tile, here], yT[:, tile, here], V("d_skip", tile),
                             bank[:, pair * P:(pair + 1) * P], ALU.mult, ALU.add)
                banks.release(b, my)
            if c < TT - 1:
                m_read = m
                for g in range(SG):
                    cols = slice(512 * g, 512 * g + 512)
                    b, bank, free = banks.take()
                    m = matmuls(free + m_tok + [m_end], [(bm_tok[:, c, g * SN:(g + 1) * SN], x_end[:, cols])], bank[:, :])
                    if c == 0:
                        m_new = copy(dve, [m] + start, state[:, cols], bank[:, :])
                    else:
                        st3 = state[:, cols].rearrange("p (h d) -> p h d", h=8)
                        m2 = tt([m_grow, m_read, m_new], st3, st3,
                                grow[:, 8 * g:8 * g + 8, P - 1:P].to_broadcast([P, 8, SP_]), ALU.mult)
                        m_new = tt([m, m2], state[:, cols], state[:, cols], bank[:, :], ALU.add)
                    banks.release(b, m_new)
            old = [m, dve.mark()]
            run(z_steps, 3)
        run(z_steps)
        m_ssd, loop_end = dve.mark(), [pe.mark(), dve.mark()]

        room.at = chunk_at
        mixedT = room.take(P, DK, T)
        gate_buf = Buffers([room.take(P, 2, T) for _ in range(2)])
        ada = xs_tok.rearrange("p a b -> p (a b)")[:, 0:2048]

        def modulations():
            yield from modulation(1, loop_end, ada)
            yield from modulation(2, list(ada_read), ada)

        modulating = modulations()
        gate = {}

        def open_gate(which):
            gi, gv, gfree = gate_buf.take()

            def sink_gate(tile, bank, m):
                return [activate([m] + gfree + loop_end, gv[:, tile, :], bank, ACT.Sigmoid)]

            project(DK, h_tile, [m_h], 2, sink_gate)
            run(modulating, 1)
            gate[which] = (gi, gv, act.mark())

        def mix(blk, which):
            gi, gv, m_gate = gate[which]

            def sink_mix(tile, bank, m):
                o = mixedT[:, 2 * blk + tile, :]
                if which == 0:
                    return [tt([m, m_gate] + loop_end, o, bank, gv[:, tile, :], ALU.mult)]
                m = tt([m, m_gate], gv[:, tile, :], bank, gv[:, tile, :], ALU.mult)
                tt([m], o, o, gv[:, tile, :], ALU.add)
                return [m]

            if which == 0:
                project(4, lambda k: oT[:, k, :], [m_oT], 2, sink_mix)
            else:
                project(DK, lambda k: yT[:, k, :], [m_yT], 2, sink_mix)
            run(modulating, 1)
            gate_buf.release(gi, dve.mark())

        for tile in range(8):
            a = activate([act.mark()], zT[:, tile, :], zT[:, tile, :], ACT.Silu)
            m = tt([a, m_ssd], yT[:, tile, :], yT[:, tile, :], zT[:, tile, :], ALU.mult)
        m_y = m
        open_gate(0)
        mix(0, 0)
        open_gate(1)
        for g in range(SG):
            i, rs, m = sum_squares([yT[:, 4 * g + j, :] for j in range(4)], [m_y], ones, 512, EPS)
            for j in range(4):
                tile = 4 * g + j
                m = stt([m], yT[:, tile, :], yT[:, tile, :], V("ssm_norm", tile), rs, ALU.mult, ALU.mult)
            rs_ring.release(i, m)
        m_yT = m
        show("yT", yT, [m_yT])
        if stop == "ssd":
            return finish(join())
        mix(0, 1)
        for blk in range(1, 4):
            for which in range(2):
                open_gate(which)
                mix(blk, which)
        run(modulating)
        m_mix = dve.mark()

        def sink_out(tile, bank, m):
            return [stt([m, mod_mark[1], m_h], xT[:, tile, :], bank, mod[:, 16 + tile:17 + tile], xT[:, tile, :],
                        ALU.mult, ALU.add)]

        project(DK, lambda k: mixedT[:, k, :], [m_mix], DK, sink_out)
        m_x = dve.mark()
        show("xT", xT[:, :, :], [m_x])
        if stop == "x1":
            return finish(join())

        room = Room(work)
        top = room.take(P, TT, E)
        gate_e = room.take(P, TT, E)
        place = room.take(P, TT, E)
        slot_of = room.take(P, TT, E)
        first = room.take(P, TT, E)
        gate_1 = room.take(P, TT, E)
        row_of = room.take(P, TT, E)
        logits = room.take(P, TT, E)
        route_a, route_b = room.take(P, E), room.take(P, E)
        best_r = room.take(P, TT, 8)
        rows_i = room.take(P, TT, 8, dt=I32)
        gates_k = room.take(P, TT, EK)
        totals = room.take(P, E)
        over = room.take(P, 2)
        tok_v = room.take(P, TT, 2, dt=BF16)
        w_router = room.take(P, DK, E)
        after_route = room.at
        h_tok = room.take(P, TT, D)
        start = join()
        router_in = Load(semaphore("router_in")).start(act, start, w_router, rows(io["w_router"][0]))
        m = ts([mod_mark[2], dve.mark()], one_plus[:, :], mod[:, 32:40], 1.0, ALU.add)
        m_h = normalise(("norm_ffn", 0), 3, [m_x, m] + start)

        for t in range(TT):
            for j in range(0, DK, 4):
                b, bank, free = banks.take()
                for q in range(4):
                    m = transpose(free + [m_h], bank[:, q * P:(q + 1) * P], hT[:, j + q, t * P:(t + 1) * P])
                m = copy(act, [m], h_tok[:, t, j * P:(j + 4) * P], bank[:, :])
                banks.release(b, m)
        h_out = Load(semaphore("h_out")).start(act, [m], h_dram.rearrange("(t p) d -> p t d", p=P), h_tok)
        stores.append(h_out)

        b, bank, free = banks.take()
        for t in range(TT):
            m = matmuls(free + [m_h, router_in], [(hT[:, k, t * P:(t + 1) * P], w_router[:, k, :]) for k in range(DK)],
                        bank[:, t * E:(t + 1) * E])
        m_log = tt([m] + start, logits, bank[:, 0:TT * E].rearrange("p (a b) -> p a b", a=TT),
                   V("b_router", 0, E).unsqueeze(1).to_broadcast([P, TT, E]), ALU.add)
        banks.release(b, m_log)
        for t in range(TT):
            lg = logits[:, t, :]
            br = best_r[:, t, :]
            m = dve.do([m_log], lambda e, br=br, lg=lg: e.max(br, lg))
            m = threshold([m], lg, E, EK, br[:, EK - 1:EK], route_a, route_b, top[:, t, :], over)
            m2 = ts([m], route_b, lg, br[:, 0:1], ALU.subtract)
            a = activate([m2], route_b, route_b, ACT.Exp)
            m = dve.do([a, m], lambda e, t=t: e.tensor_tensor_reduce(
                out=gate_e[:, t, :], in0=route_b, in1=top[:, t, :], scale=1.0, scalar=0.0, op0=ALU.mult, op1=ALU.add,
                accum_out=over[:, 0:1]))
            m = dve.do([m], lambda e: e.reciprocal(over[:, 1:2], over[:, 0:1]))
            m = ts([m], gate_e[:, t, :], gate_e[:, t, :], over[:, 1:2], ALU.mult)
        m_top = m
        b, bank, free = banks.take()
        for t in range(TT):
            m = matmuls(free + [m_top], [(C("before"), top[:, t, :])] + [(ones, top[:, s, :]) for s in range(t)],
                        bank[:, t * E:(t + 1) * E])
        m_tot = matmuls([], [(ones, top[:, s, :]) for s in range(TT)], bank[:, TT * E:(TT + 1) * E])
        flat = "p a b -> p (a b)"
        m = stt([m_tot, m_top], place.rearrange(flat), bank[:, 0:TT * E], 1.0, top.rearrange(flat), ALU.add, ALU.mult)
        m_slot = ts([m], slot_of, place, 1.0, ALU.subtract)
        m2 = stt([m], first, place, float(P), top, ALU.is_le, ALU.mult)
        m_g1 = tt([m2], gate_1, gate_e, first, ALU.mult)
        m2 = tt([m2], row_of, place, C("ebase").unsqueeze(1).to_broadcast([P, TT, E]), ALU.add)
        m_row = tt([m2, m_g1], row_of, row_of, first, ALU.mult)
        m_tot = copy(dve, [m_tot, m_slot], totals, bank[:, TT * E:(TT + 1) * E])
        m = dve.do([m_tot, m_row], lambda e, bank=bank: e.tensor_reduce(over[:, 0:1], bank[:, TT * E:(TT + 1) * E], AX.X, ALU.max))
        banks.release(b, m)
        m_over = ts([m], over_i[:, 0:1], over[:, 0:1], float(P), ALU.is_gt)
        for t in range(TT):
            m = copy(dve, [con_in], tok_v[:, t, 0:1], C("tok", P, 0, 1))
            m = ts([con_in], tok_v[:, t, 1:2], C("tok", P, 1, 1), float(t * P), ALU.mult)
        m_tokv = m
        for t in range(TT):
            br = best_r[:, t, :]
            m = dve.do([m_row], lambda e, br=br, t=t: e.max(br, row_of[:, t, :]))
            for k in range(EK):
                m2 = dve.do([m], lambda e, br=br, t=t, k=k: e.scalar_tensor_tensor(
                    out=route_a, in0=row_of[:, t, :], scalar=br[:, k:k + 1], in1=gate_1[:, t, :],
                    op0=ALU.is_equal, op1=ALU.mult, accum_out=gates_k[:, t, k:k + 1]))
                m = m2
            m_rows = ts([m], rows_i[:, t, :], br, 1.0, ALU.subtract, 0.0, ALU.max)

        room.at = after_route
        pick = Buffers([room.take(P, TT, P, dt=BF16) for _ in range(2)])
        index_sum = room.take(P, 1)
        index = Buffers([room.take(P, 1, dt=I32) for _ in range(2)])
        xe = Buffers([room.take(P, D) for _ in range(2)])
        xeT = Buffers([room.take(P, DK, P) for _ in range(2)])
        bias_rows = room.take(P, 3 * D)
        bias_all = Buffers([room.take(P, 3 * D) for _ in range(3)])
        g_act, u_act, s_act = room.take(P, D), room.take(P, D), room.take(P, D)
        acted = room.take(P, D)
        aT = room.take(P, DK, P)
        ye = Buffers([room.take(P, D) for _ in range(2)])
        moe_end = room.at
        moe_start = join() + [h_out]
        up_banks, turn_banks, down_banks = psum[0:4], Buffers(psum[4:6]), psum[6:8]
        up_free, down_free = [], []
        bias_load = [Load(semaphore(f"bias_row{j}")) for j in range(2)]
        xe_load = [Load(semaphore(f"xe_in{j}")) for j in range(2)]
        ye_store = [Load(semaphore(f"ye_out{j}")) for j in range(2)]
        bias_row_free, bias_row_turn = [None, None], [1]

        def gather_rows(after, o, table, ids, load):
            load.count += 16
            prior = pool.mark()
            pool.count += 1
            done = pool.sem
            pool.quiet(after + [prior], lambda e: e.indirect_dma_start(
                out=o, out_offset=None, in_=table, in_offset=bass.IndirectOffsetOnAxis(ap=ids, axis=0),
                engine_sem=done), load.sem, 16)
            return (load.sem, load.count)

        def gather_tokens(slots):
            i, pv, pfree = pick.take()
            for t in range(TT):
                m = ts(moe_start + pfree + slots[1], pv[:, t, :], C("slot"), slots[0](t), ALU.is_equal)
            b, bank, free = turn_banks.take()
            m = matmuls(free + moe_start + [m, m_tokv], [(pv[:, t, :], tok_v[:, t, :]) for t in range(TT)], bank[:, 0:2])
            pick.release(i, m)
            j, iv, ifree = index.take()
            m = dve.do([m] + ifree, lambda e, o=index_sum: e.tensor_reduce(o, bank[:, 0:2], AX.X, ALU.add))
            turn_banks.release(b, m)
            m = copy(dve, [m], iv, index_sum)
            j2, xv, xfree = xe.take()
            landed = gather_rows([m] + xfree, xv, h_dram, iv, xe_load[j2])
            index.release(j, landed)
            return j2, xv, landed

        def turn_tokens(j2, xv, landed):
            i, tv, tfree = xeT.take()
            for q in range(0, DK, 4):
                b, bank, free = turn_banks.take()
                for r in range(4):
                    m = transpose(free + [landed], bank[:, r * P:(r + 1) * P], xv[:, (q + r) * P:(q + r + 1) * P])
                m_t = m
                m = copy(act, [m] + tfree, tv[:, q:q + 4, :].rearrange(flat), bank[:, :])
                turn_banks.release(b, m)
            xe.release(j2, m_t)
            return i, tv, m

        def spread_bias(e_gu, e_dn, marks=()):
            held_bias, bv, bfree = bias_all.take()
            j = bias_row_turn[0] = 1 - bias_row_turn[0]
            row = bias_rows[32 * j:32 * j + 1, :]
            bias_load[j].start(act, moe_start + [bias_row_free[j]] + list(marks), row[:, 0:2 * D], e_gu)
            m = bias_load[j].start(act, [], row[:, 2 * D:3 * D], e_dn)
            m = pool.do([m, pool.mark()] + bfree + moe_start, lambda e: e.partition_broadcast(bv, row))
            bias_row_free[j] = m
            return held_bias, bv, m

        def up_part(tv, after, lo, hi):
            for k in range(lo, hi):
                w, arrived = weights.next()
                for n in range(4):
                    f = (lambda e, n=n, w=w, k=k: e.matmul(up_banks[n][:, :], tv[:, k, :], w[:, 0, n * 512:(n + 1) * 512],
                                                           start=(k == 0), stop=(k == DK - 1)))
                    m = pe.do(after + up_free + [arrived], f)
                weights.done(m)
            return m

        def gate_up(m, bv, m_bias):
            for n in range(4):
                o = (g_act if n < 2 else u_act)[:, (n % 2) * 512:(n % 2) * 512 + 512]
                r = tt([m, m_bias, act.mark()], o, up_banks[n][:, :], bv[:, n * 512:(n + 1) * 512], ALU.add)
            up_free[:] = [r]
            m = ts([r], g_act, g_act, 7.0, ALU.min)
            a = activate([m], s_act, g_act, ACT.Sigmoid, scale=1.702)
            m = ts([r], u_act, u_act, 7.0, ALU.min, -7.0, ALU.max)
            m2 = tt([a], g_act, g_act, s_act, ALU.mult)
            return stt([m, m2] + acted_free, acted, u_act, 1.0, g_act, ALU.add, ALU.mult)

        acted_free, aT_free = [], []

        def turn_acted(m_act):
            for q in range(0, DK, 4):
                b, bank, free = turn_banks.take()
                for r in range(4):
                    m = transpose(free + [m_act], bank[:, r * P:(r + 1) * P], acted[:, (q + r) * P:(q + r + 1) * P])
                m_t = m
                m = copy(act, [m] + aT_free, aT[:, q:q + 4, :].rearrange(flat), bank[:, :])
                turn_banks.release(b, m)
            acted_free[:] = [m_t]
            return m

        def down(m_aT, j, bv, m_bias, dst):
            for k in range(0, DK, 2):
                w, arrived = weights.next()
                for kk in range(2):
                    for n in range(2):
                        f = (lambda e, n=n, w=w, k=k, kk=kk, x=aT: e.matmul(
                            down_banks[n][:, :], x[:, k + kk, :], w[:, kk, n * 512:(n + 1) * 512],
                            start=(k + kk == 0), stop=(k + kk == DK - 1)))
                        m = pe.do([m_aT, arrived] + down_free, f)
                weights.done(m)
            aT_free[:] = [m]
            i, yv, yfree = ye.take()
            for n in range(2):
                r = tt([m, m_bias] + yfree, yv[:, n * 512:(n + 1) * 512], down_banks[n][:, :],
                       bv[:, 2 * D + n * 512:2 * D + (n + 1) * 512], ALU.add)
            down_free[:] = [r]
            if j is not None:
                bias_all.release(j, r)
            m = ye_store[i].start(act, [r], dst, yv)
            ye.release(i, m)
            return m

        def primary(e):
            return gather_tokens((lambda t: slot_of[:, t, e:e + 1], [m_slot]))

        def bias_of(e):
            return spread_bias(io["b_gu"][0][e:e + 1, :], io["b_dn"][0][e:e + 1, :])

        tokens = turn_tokens(*primary(0))
        ahead = primary(1)
        biases = {0: bias_of(0)}
        for e in range(E):
            i, tv, m_tv = tokens
            if e:
                m_aT = turn_acted(m_act)
            up_part(tv, [m_tv], 0, 4)
            if e + 1 < E:
                tokens = turn_tokens(*ahead)
                biases[e + 1] = bias_of(e + 1)
            if e + 2 < E:
                ahead = primary(e + 2)
            m = up_part(tv, [], 4, DK)
            xeT.release(i, m)
            m_act = gate_up(m, *biases[e][1:])
            if e:
                down(m_aT, *biases.pop(e - 1), y_dram[(e - 1) * P:e * P, :])
        down(turn_acted(m_act), *biases.pop(E - 1), y_dram[(E - 1) * P:E * P, :])
        stored = [(s.sem, s.count) for s in ye_store]
        stores.extend(stored)

        room.at = after_route
        y_tok = room.take(P, TT, D)
        after_y = room.at
        picked = Buffers([room.take(P, D) for _ in range(6)])
        picked_load = [Load(semaphore(f"picked{j}")) for j in range(6)]
        start = join() + stored
        for t in range(TT):
            for k in range(EK):
                j, pv, pfree = picked.take()
                landed = gather_rows(start + [m_rows] + pfree, pv, y_dram, rows_i[:, t, k:k + 1], picked_load[j])
                if k == 0:
                    m = ts([landed], y_tok[:, t, :], pv, gates_k[:, t, k:k + 1], ALU.mult)
                else:
                    m = stt([landed, m], y_tok[:, t, :], pv, gates_k[:, t, k:k + 1], y_tok[:, t, :], ALU.mult, ALU.add)
                picked.release(j, m)
        m_y_tok = m

        close_part(None)
        main = (pe, act, dve, pool, sp, weights, m_y_tok)
        pe, act, dve, pool, sp = (Engine(semaphore("over_" + n)) for n in ("pe", "act", "dve", "pool", "sp"))
        room.at = after_y
        over_count, incl, base, hot, hot_a = (room.take(P, E) for _ in range(5))
        over_place = room.take(P, OB, TT)
        over_e, over_b = room.take(P, OB), room.take(P, OB)
        over_e_i = room.take(P, OB, dt=I32)
        row_over, gate_over = room.take(P, TT, E), room.take(P, TT, E)
        over_ring = room.take(P, 4, SLOT)
        pick = Buffers([room.take(P, TT, P, dt=BF16)])
        index_sum = room.take(P, 1)
        index = Buffers([room.take(P, 1, dt=I32)])
        xe, xeT = Buffers([room.take(P, D)]), Buffers([room.take(P, DK, P)])
        bias_one = room.take(P, 3 * D)
        g_act, u_act, s_act, acted = (room.take(P, D) for _ in range(4))
        aT = room.take(P, DK, P)
        ye = Buffers([room.take(P, D)])
        moe_start, m_tokv = [], None
        turn_banks = Buffers(psum[4:6])
        for marks in (up_free, down_free, acted_free, aT_free):
            marks[:] = []
        xe_load, ye_store = [Load(semaphore("over_xe_in"))], [Load(semaphore("over_ye_out"))]
        over_bias = Load(semaphore("over_bias_in"))
        picked_load = [Load(semaphore("over_picked_in"))]

        m = ts([], over_count, totals, float(P), ALU.is_gt)
        for k in (2, 3):
            m = stt([m], over_count, totals, float(k * P), over_count, ALU.is_gt, ALU.add)
        m = dve.do([m], lambda e: e.tensor_tensor_scan(incl, over_count, over_count, 0.0, ALU.add, ALU.bypass))
        m = tt([m], base, incl, over_count, ALU.subtract)
        for j in range(OB):
            m = ts([m], hot_a, base, float(j), ALU.is_le)
            m = stt([m], hot, incl, float(j), hot_a, ALU.is_gt, ALU.mult)
            for dst, src in [(over_e[:, j:j + 1], C("eone")), (over_b[:, j:j + 1], base)] + [
                    (over_place[:, j, t:t + 1], place[:, t, :]) for t in range(TT)]:
                m = dve.do([m], lambda e, dst=dst, src=src: e.tensor_tensor_reduce(
                    out=hot_a, in0=hot, in1=src, scale=1.0, scalar=0.0, op0=ALU.mult, op1=ALU.add, accum_out=dst))
            m = ts([m], over_b[:, j:j + 1], over_b[:, j:j + 1], float(P), ALU.mult, -float(P * (1 + j) + 1), ALU.add)
            m = ts([m], over_place[:, j, :], over_place[:, j, :], over_b[:, j:j + 1], ALU.add)
        m_list = m
        m_e = copy(dve, [m], over_e_i, over_e)
        m = ts([m], row_over, place, float(P), ALU.is_gt)
        m_gate = tt([m], gate_over, row_over, gate_e, ALU.mult)
        m = ts([m], base, base, float(P), ALU.mult, -float(P), ALU.add)
        m = tt([m], logits, place, base.unsqueeze(1).to_broadcast([P, TT, E]), ALU.add)
        m_row = tt([m, m_gate], row_over, row_over, logits, ALU.mult)

        expert = {}

        def over_chunks(j):
            def up(k):
                return lambda: io["w_gu"][0][bass.ds(expert[j], 1), k * P:(k + 1) * P, :].rearrange("a p n -> p a n")

            def dn(k):
                return lambda: io["w_dn"][0][bass.ds(expert[j], 1), k * P:(k + 2) * P, :].rearrange(
                    "a (k p) n -> p (a k) n", p=P)
            return [(up(k), 1, 2048) for k in range(DK)] + [(dn(k), 2, 1024) for k in range(0, DK, 2)]

        def read_expert(e, j):
            expert[j] = e.value_load(over_e_i[0:1, j:j + 1], min_val=0, max_val=E - 1)

        weights = Weights("over_ring", over_ring, 4, [])
        m = None
        for j in range(OB):
            weights.plan.extend(over_chunks(j))
            sp.quiet([m_e], lambda e, j=j: read_expert(e, j))
            over_bias.start(sp, [m], bias_one[:, 0:2 * D],
                            lambda j=j: io["b_gu"][0][bass.ds(expert[j], 1), :].to_broadcast([P, 2 * D]))
            m_bias = over_bias.start(sp, [], bias_one[:, 2 * D:3 * D],
                                     lambda j=j: io["b_dn"][0][bass.ds(expert[j], 1), :].to_broadcast([P, D]))
            for _ in range(4):
                weights.start_next()
            got = gather_tokens((lambda t: over_place[:, j, t:t + 1], [m_list]))
            i, tv, m_tv = turn_tokens(*got)
            m = up_part(tv, [m_tv], 0, DK)
            xeT.release(i, m)
            m_act = gate_up(m, bias_one, m_bias)
            down(turn_acted(m_act), None, bias_one, m_bias, over_dram[j * P:(j + 1) * P, :])
            m = dve.mark()
        stored_over = (ye_store[0].sem, ye_store[0].count)
        for t in range(TT):
            br = best_r[:, t, :]
            m = dve.do([m_row], lambda e, br=br, t=t: e.max(br, row_over[:, t, :]))
            for k in range(EK):
                m = dve.do([m], lambda e, br=br, t=t, k=k: e.scalar_tensor_tensor(
                    out=hot, in0=row_over[:, t, :], scalar=br[:, k:k + 1], in1=gate_over[:, t, :],
                    op0=ALU.is_equal, op1=ALU.mult, accum_out=gates_k[:, t, k:k + 1]))
            m = ts([m], rows_i[:, t, :], br, 1.0, ALU.subtract, 0.0, ALU.max)
            for k in range(EK):
                landed = gather_rows([m, stored_over], xe.views[0], over_dram, rows_i[:, t, k:k + 1], picked_load[0])
                m = stt([landed, m], y_tok[:, t, :], xe.views[0], gates_k[:, t, k:k + 1], y_tok[:, t, :], ALU.mult, ALU.add)
        sp.quiet(join() + [stored_over] + weights.last_marks(), None)
        close_part(over_i[0:1, 0:1])
        pe, act, dve, pool, sp, weights, m_y = main

        banks = dense = Buffers(psum[:6])
        held = Buffers(psum[6:])
        for k in range(DK):
            b, bank, free = banks.take()
            for t in range(TT):
                m = transpose(free + start + [m_y], bank[:, t * P:(t + 1) * P], y_tok[:, t, k * P:(k + 1) * P])
            m = stt([m], xT[:, k, :], bank[:, :], mod[:, 40 + k:41 + k], xT[:, k, :], ALU.mult, ALU.add)
            banks.release(b, m)
        m_x = m
        show("xT2", xT[:, :, :], [m_x])
        if stop == "moe":
            return finish(join())

        room = Room(work)
        uT = room.take(P, AW // P, T)
        v_tok = room.take(P, TT, AW)
        b_s = room.take(P, 8, P)
        w_sT = room.take(P, 8, P)
        ln_row = room.take(P, AW)
        part = room.take(P, TT, 8)
        stat = room.take(P, TT, 4)
        start = join()
        w_s_load, ln_load = Load(semaphore("w_s_in")), Load(semaphore("ln_in"))
        w_s_raw = ln_row.rearrange("p (a b) -> p a b", a=16)[:, 0:8, :]
        w_s_in = w_s_load.start(act, start, w_s_raw, io["a_w_s_2"][0].rearrange("g t s -> t g s"))
        b_s_in = Load(semaphore("b_s_in")).start(
            act, start, b_s.rearrange(flat),
            io["a_b_s_2"].rearrange("a g t -> a (g t)").to_broadcast([P, 8 * P]))
        m_h = normalise(("norm_w_2", 0), None, [m_x] + start)
        for g in range(0, 8, 4):
            b, bank, free = banks.take()
            for q in range(4):
                m = transpose(free + [w_s_in], bank[:, q * P:(q + 1) * P], w_s_raw[:, g + q, :])
            m = tt([m] + start, w_sT[:, g:g + 4, :], bank[:, :].rearrange("p (a b) -> p a b", a=4),
                   C("tri").unsqueeze(1).to_broadcast([P, 4, P]), ALU.mult)
            banks.release(b, m)
        m_ws = m
        ln_in = ln_load.start(act, [pe.mark()], ln_row, io["a_ln_w_2"].to_broadcast([P, AW]))
        project(DK, h_tile, [m_h], AW // P,
                lambda tile, bank, m: [activate([m] + start, uT[:, tile, :], bank, ACT.Gelu_apprx_tanh)])
        for piece in range(8):
            w, arrived = weights.next()
            for t in range(TT):
                b, bank, free = banks.take()
                m = matmuls(free + [arrived, m_h], [(hT[:, k, t * P:(t + 1) * P], w[:, k, :]) for k in range(DK)],
                            bank[:, 0:256])
                a = activate([m] + start, v_tok[:, t, piece * 256:(piece + 1) * 256], bank[:, 0:256],
                             ACT.Gelu_apprx_tanh, accum_out=part[:, t, piece:piece + 1])
                banks.release(b, a)
            weights.done(m)
        m_v = a
        for t in range(TT):
            vt = v_tok[:, t, :]
            m = dve.do([m_v], lambda e, t=t: e.tensor_reduce(stat[:, t, 0:1], part[:, t, :], AX.X, ALU.add))
            m = ts([m], stat[:, t, 0:1], stat[:, t, 0:1], 1.0 / AW, ALU.mult)
            m = ts([m], vt, vt, stat[:, t, 0:1], ALU.subtract)
            for q in range(4):
                s, sv, sfree = sq_ring.take()
                m2 = activate([m] + sfree, sv, vt[:, q * 512:(q + 1) * 512], ACT.Square, accum_out=part[:, t, q:q + 1])
                sq_ring.release(s, m2)
            m = dve.do([m2], lambda e, t=t: e.tensor_reduce(stat[:, t, 1:2], part[:, t, 0:4], AX.X, ALU.add))
            m = ts([m], stat[:, t, 1:2], stat[:, t, 1:2], 1.0 / AW, ALU.mult, LN_EPS, ALU.add)
            a = activate([m], stat[:, t, 2:3], stat[:, t, 1:2], ACT.Sqrt)
            m = dve.do([a], lambda e, t=t: e.reciprocal(stat[:, t, 3:4], stat[:, t, 2:3]))
            m = stt([m, ln_in], vt, vt, stat[:, t, 3:4], ln_row, ALU.mult, ALU.mult)
        ln_in = ln_load.start(act, [m], ln_row, io["a_ln_b_2"].to_broadcast([P, AW]))
        for t in range(TT):
            m = tt([m, ln_in], v_tok[:, t, :], v_tok[:, t, :], ln_row, ALU.add)
        m_v = m
        s_buf = Buffers([ln_row[:, 0:T], ln_row[:, T:2 * T]])
        g_buf = Buffers([ln_row[:, 2 * T:3 * T], ln_row[:, 3 * T:4 * T]])

        def sink_spatial(tile, bank, m):
            g = tile // 2
            i, gv, gfree = g_buf.take()
            a = activate([m, m_v] + gfree, gv, bank, ACT.Silu)
            b, sbank, free = held.take()
            for t in range(TT):
                m = matmuls(free + [m_v, m_ws], [(v_tok[:, t, tile * P:(tile + 1) * P], w_sT[:, g, :])],
                            sbank[:, t * P:(t + 1) * P])
            j, sv, sfree = s_buf.take()
            m = tt([m, b_s_in, m_v] + sfree, sv.rearrange("p (a b) -> p a b", a=TT),
                   sbank[:, :].rearrange("p (a b) -> p a b", a=TT), b_s[:, g, :].unsqueeze(1).to_broadcast([P, TT, P]),
                   ALU.add)
            held.release(b, m)
            m = tt([m], sv, sv, uT[:, tile, :], ALU.mult)
            m = tt([m, a], uT[:, tile, :], sv, gv, ALU.mult)
            s_buf.release(j, m)
            g_buf.release(i, m)
            return [a]

        project(DK, h_tile, [m_h], AW // P, sink_spatial)
        m_y = dve.mark()

        def sink_add(tile, bank, m):
            return [tt([m], xT[:, tile, :], xT[:, tile, :], bank, ALU.add)]

        project(AW // P, lambda k: uT[:, k, :], [m_y], DK, sink_add)
        m_x = dve.mark()
        show("xT3", xT[:, :, :], [m_x])
        if stop == "a":
            return finish(join())

        room = Room(work)
        yT = room.take(P, BT, T)
        gate_w = room.take(P, 2, BT, P)
        padded = Buffers([room.take(P, T + 8)[:, 0:T + 3] for _ in range(2)])
        conv_buf = Buffers([room.take(P, T) for _ in range(4)])
        tmp = Buffers([room.take(P, 5, T) for _ in range(2)])
        lam = room.take(P, BT)
        tmp4 = [room.take(P, BT) for _ in range(4)]
        start = join()
        gate_load = Load(semaphore("gate_w_in"))
        for j, name in enumerate(("b_gate_a_w_2", "b_gate_x_w_2")):
            gate_in = gate_load.start(act, start, gate_w[:, j, :, :], io[name][0].rearrange("h i j -> i h j"))
        m = ts([vec_in] + start, lam, V("b_lambda_2", 0, BT), -1.0, ALU.mult)
        m = softplus([m], lam, lam, tmp4)
        m_lam = ts([m], lam, lam, 8.0, ALU.mult)
        m_h = normalise(("norm_w_2", 8), None, [m_x] + start)
        pads = [dve.do(start, lambda e, v=v: e.memset(v[:, 0:3], 0.0)) for v in padded.views]
        convolved = {}

        def sink_branch(tile, bank, m):
            i, cv, cfree = conv_buf.take()
            dve.quiet(cfree, None)
            bank_read, m = convolve(tile, bank, m, "b_conv_w_2", BT, cv)
            m = ts([m], cv, cv, V("b_conv_b_2", tile), ALU.add)
            convolved[tile] = (i, cv, m)
            return [bank_read]

        def sink_rglru(tile, bank, m):
            i, cv, m_c = convolved.pop(tile)
            k, tv, tfree = tmp.take()
            r, inp, a_, gz, tau = (tv[:, j, :] for j in range(5))
            m_gz = activate([m] + tfree + start, gz, bank, ACT.Silu)
            for j, (o, name) in enumerate(((r, "b_gate_a_b_2"), (inp, "b_gate_x_b_2"))):
                b, gbank, free = held.take()
                m = matmuls(free + [m_c, gate_in], [(gate_w[:, j, tile, :], cv)], gbank[:, :])
                m = activate([m], o, gbank[:, :], ACT.Sigmoid, bias=V(name, tile))
                held.release(b, m)
            m = ts([m, m_lam], r, r, lam[:, tile:tile + 1], ALU.mult)
            m_a = activate([m], a_, r, ACT.Exp, scale=-1.0)
            m = activate([m], tau, r, ACT.Tanh)
            m2 = tt([m], inp, inp, cv, ALU.mult)
            conv_buf.release(i, m2)
            m = ts([m], r, tau, 1.0, ALU.add)
            m = dve.do([m], lambda e: e.reciprocal(r, r))
            m = stt([m], tau, tau, 2.0, r, ALU.mult, ALU.mult)
            m = activate([m], tau, tau, ACT.Sqrt)
            m = tt([m, m2], inp, inp, tau, ALU.mult)
            m = dve.do([m, m_a], lambda e: e.tensor_tensor_scan(r, a_, inp, 0.0, ALU.mult, ALU.add))
            m = tt([m, m_gz], yT[:, tile, :], r, gz, ALU.mult)
            tmp.release(k, m)
            return [m_gz]

        for blk in range(BT // 2):
            project(DK, h_tile, [m_h], 2, lambda tile, bank, m: sink_branch(2 * blk + tile, bank, m))
            project(DK, h_tile, [m_h], 2, lambda tile, bank, m: sink_rglru(2 * blk + tile, bank, m))
        m_y = dve.mark()
        project(BT, lambda k: yT[:, k, :], [m_y], DK, sink_add)
        m_x = dve.mark()

        m_h = normalise(("norm_f_w_2", 0), None, [m_x, pe.mark()])
        room = Room(work)
        o_buf = [room.take(P, D) for _ in range(TT)]
        start = join()
        out_store = Load(semaphore("out_store"))
        for t in range(TT):
            for j in range(0, DK, 4):
                b, bank, free = banks.take()
                for q in range(4):
                    m = transpose(free + [m_h], bank[:, q * P:(q + 1) * P], hT[:, j + q, t * P:(t + 1) * P])
                m = copy((act, dve)[j // 4], [m] + start, o_buf[t][:, j * P:(j + 4) * P], bank[:, :])
                banks.release(b, m)
            stored = out_store.start(act, [m, act.mark()], out[0][t * P:(t + 1) * P, :], o_buf[t])
        stores.append(stored)
        finish(join())


def packed_vectors(i):
    out = np.zeros((P, NVEC), np.float32)

    def put(name, value):
        a, n = VEC[name]
        out[:, a:a + n] = value

    for name in ("c", "b_ada", "norm_mix", "norm_ffn", "kv_norm", "conv_w", "conv_b", "ssm_norm", "norm_w_2",
                 "b_conv_w_2", "b_conv_b_2", "b_gate_a_b_2", "b_gate_x_b_2", "b_lambda_2", "norm_f_w_2"):
        put(name, np.asarray(i[name]).reshape(-1, P).T)
    for name in ("q_norm", "k_norm", "idx_k_ln_w", "idx_k_ln_b"):
        put(name, np.tile(np.asarray(i[name]).reshape(-1), 2)[:, None])
    put("d_skip", np.repeat(np.asarray(i["d_skip"]).reshape(-1), SP_).reshape(-1, P).T)
    for name in ("dt_bias", "a_log", "b_router"):
        put(name, np.broadcast_to(np.asarray(i[name]).reshape(1, -1), (P, VEC[name][1])))
    return out


_WEIGHTS = ["x", "rel_bias", "w_ada", "w_in", "w_kv_up", "w_attn_o", "w_ssm_o", "w_out", "w_router", "w_gu", "b_gu",
            "w_dn", "b_dn", "a_w_in_2", "a_ln_w_2", "a_ln_b_2", "a_w_s_2", "a_b_s_2", "a_w_out_2", "b_w_in_2",
            "b_gate_a_w_2", "b_gate_x_w_2", "b_w_out_2"]


def make(nc, inputs, debug=None, stop=None):
    arrays = {name: np.ascontiguousarray(inputs[name]) for name in _WEIGHTS}
    arrays["vec"] = packed_vectors(inputs)
    arrays["con"] = shape_constants()
    io = {n: nc.dram_tensor(f"in_{n}", a.shape, F32, kind="ExternalInput").ap() for n, a in arrays.items()}
    out = nc.dram_tensor("out_x", (1, T, D), F32, kind="ExternalOutput").ap()
    dbg = {n: nc.dram_tensor(f"dbg_{n}", s, F32, kind="ExternalOutput").ap() for n, s in (debug or {}).items()}
    build(nc, io, out, dbg, stop)
    return {f"in_{n}": a for n, a in arrays.items()}


def kernel(**inputs):
    import concourse.bacc as bacc
    from concourse.bass_utils import run_bass_kernel_spmd
    nc = bacc.Bacc("TRN2", target_bir_lowering=False, num_devices=1, dynamic_dma_scratch_size=8192)
    arrays = make(nc, inputs)
    return run_bass_kernel_spmd(nc, [arrays], core_ids=[0]).results[0]["out_x"]
```

```python
import math
from contextlib import ExitStack

import numpy as np

import concourse.bass as bass
from concourse import mybir
from concourse.alu_op_type import AluOpType as ALU

F32, F32R, I32, BF16 = mybir.dt.float32, mybir.dt.float32r, mybir.dt.int32, mybir.dt.bfloat16
ACT, AX = mybir.ActivationFunctionType, mybir.AxisListType

P = 128
T = 512
TT = T // P
D = 1024
DK = D // P
H, HD = 8, 64
TOPK = 128
NB, MAXD = 32, 128
SH, SP_ = 16, 64
SG, SN = 2, 128
CT = 12
E, EK = 32, 4
OB = T * EK // P
AW = 2048
BW = 1536
BT = BW // P
EPS, LN_EPS = 1e-6, 1e-5
NEG = -1.0e30
C_Q, C_KV, C_QI, C_KI, C_WI, C_Z, C_X, C_DT, C_G = 0, 512, 768, 1280, 1344, 1352, 2376, 3912, 3928
SLOT = 2048
RING = 4
HALF = 1024
SPLIT = 4
ROOM = 32896

VEC = {}
for _name, _n in [("c", 8), ("b_ada", 48), ("norm_mix", 8), ("norm_ffn", 8), ("kv_norm", 2), ("conv_w", 48),
                  ("conv_b", 12), ("ssm_norm", 8), ("norm_w_2", 16), ("b_conv_w_2", 48), ("b_conv_b_2", 12),
                  ("b_gate_a_b_2", 12), ("b_gate_x_b_2", 12), ("b_lambda_2", 12), ("norm_f_w_2", 8),
                  ("q_norm", 1), ("k_norm", 1), ("idx_k_ln_w", 1), ("idx_k_ln_b", 1), ("d_skip", 8),
                  ("dt_bias", 16), ("a_log", 16), ("b_router", 32)]:
    VEC[_name] = (sum(n for _, n in VEC.values()), _n)
NVEC = sum(n for _, n in VEC.values())

CON = {}
for _name, _n in [("ident", P), ("ones", P), ("heads", P), ("tri", P), ("after", P), ("before", P),
                  ("causal", T), ("slot", P), ("flip", P), ("ebase", E), ("eone", E), ("tok", 2), ("bucket", T + P)]:
    CON[_name] = (sum(n for _, n in CON.values()), _n)
NCON = sum(n for _, n in CON.values())


def shape_constants():
    k = np.arange(P)
    out = np.zeros((P, NCON), np.float32)

    def put(name, value):
        a, n = CON[name]
        out[:value.shape[0], a:a + n] = value

    put("ident", np.eye(P))
    put("ones", np.ones((P, P)))
    put("heads", (k[:, None] // HD == k[None] // HD) * 1.0)
    put("tri", (k[:, None] <= k[None]) * 1.0)
    put("after", (k[:, None] > k[None]) * 1.0)
    put("before", (k[:, None] < k[None]) * 1.0)
    put("causal", np.where(np.arange(T)[None] <= k[:, None] + T - P, 0.0, NEG))
    put("slot", np.broadcast_to(k[None] * 1.0, (P, P)))
    put("flip", np.eye(P)[::-1])
    put("ebase", np.broadcast_to(np.arange(E)[None] * float(P), (P, E)))
    put("eone", np.broadcast_to(np.arange(E)[None] * 1.0, (P, E)))
    put("tok", np.stack([k * 1.0, np.ones(P)], 1))
    dist = np.maximum(T - 1 - np.arange(T + P), 0)
    nf = np.maximum(dist, 1).astype(np.float32)
    far = NB // 2 + (np.log(nf / (NB // 2)) / math.log(MAXD / (NB // 2)) * (NB - NB // 2)).astype(np.int32)
    bucket = np.where(dist < NB // 2, dist, np.minimum(far, NB - 1))
    put("bucket", (bucket[None] == np.arange(NB)[:, None]) * 1.0)
    return out


class Engine:

    def __init__(self, sem):
        self.sem, self.count, self.queue, self.seen = sem, 0, [], {}

    def do(self, after, issue):
        self.quiet(after, issue, self.sem)
        self.count += 1
        return (self.sem, self.count)

    def quiet(self, after, issue, sem=None, step=1):
        self.queue.append(([m for m in after if m], issue, sem, step))

    def mark(self):
        return (self.sem, self.count) if self.count else None

    def emit(self, eng, queue):
        seen = self.seen
        for marks, issue, sem, step in queue:
            for s, value in marks:
                if seen.get(s.name, 0) < value:
                    eng.wait_ge(s, value)
                    seen[s.name] = value
            if issue is not None:
                ins = issue(eng)
                if ins is not None and sem is not None:
                    ins.then_inc(sem, step)


class Buffers:

    def __init__(self, views):
        self.views, self.free, self.at = views, [[] for _ in views], -1

    def take(self):
        self.at = (self.at + 1) % len(self.views)
        return self.at, self.views[self.at], self.free[self.at]

    def release(self, i, *marks):
        self.free[i] = list(marks)


class Room:

    def __init__(self, view):
        self.view, self.at, self.words = view, 0, view.shape[1]

    def take(self, *shape, dt=None):
        n = int(np.prod(shape[1:]))
        words = n if dt is not BF16 else (n + 1) // 2
        v = self.view[0:shape[0], self.at:self.at + words]
        self.at += (words + 7) // 8 * 8
        assert self.at <= self.words, self.at
        if dt is not None:
            v = v.bitcast(dt)
        if len(shape) == 3:
            v = v.rearrange("p (a b) -> p a b", a=shape[1])
        elif len(shape) == 4:
            v = v.rearrange("p (a b c) -> p a b c", a=shape[1], b=shape[2])
        return v


class Load:

    def __init__(self, sem):
        self.sem, self.count = sem, 0

    def start(self, queue, after, out, in_, parts=1):
        self.count += 16
        queue.quiet(after, lambda e: e.dma_start(out, in_() if callable(in_) else in_), self.sem, 16)
        return (self.sem, self.count)


def build(nc, io, out):
    stack = ExitStack()
    with stack:
        def sb(name, shape, dt=F32, where=stack):
            return where.enter_context(nc.sbuf_tensor(name, shape, dt))

        def semaphore(name):
            return stack.enter_context(nc.semaphore(name))

        pe, act, dve, pool, sp = (Engine(semaphore(n)) for n in
                                  ("pe_done", "act_done", "dve_done", "pool_done", "sp_done"))

        vec = sb("vec", [P, NVEC])
        con = sb("con", [P, NCON])
        xT = sb("xT", [P, DK, T])
        ring = sb("ring", [P, RING, SLOT])
        mod = sb("mod", [P, 48])
        rs_v, rs_t = sb("rs_v", [P, T]), sb("rs_t", [P, T])
        rs_y = sb("rs_y", [P, 2, T])
        sq = sb("sq", [P, 2, T])
        cond, one_plus = sb("cond", [P, DK]), sb("one_plus", [P, DK])
        over_i = sb("over_i", [P, 8], I32)
        layer = ExitStack()
        phase = ExitStack()
        hT = sb("hT", [P, DK, T], where=phase)
        work = sb("work", [P, ROOM], where=phase)
        psum = [stack.enter_context(nc.psum_tensor(f"bank{i}", [P, 512], F32)) for i in range(8)]
        banks = Buffers(psum[:5])
        held = Buffers(psum[5:6])
        dense = Buffers(psum[6:])

        def V(name, j=0, n=None):
            a, w = VEC[name]
            return vec[:, a + j:a + j + (n or 1)] if n is not None or w > 1 else vec[:, a:a + 1]

        def C(name, rows=P, lo=0, n=None):
            a, w = CON[name]
            return con[0:rows, a + lo:a + lo + (n or w)]

        ident, ones = C("ident"), C("ones")

        bias_dram = nc.dram_tensor("bias_rows", (H, T + P), F32).ap()
        h_dram = nc.dram_tensor("h_rows", (T, D), F32).ap()
        y_dram = nc.dram_tensor("expert_rows", (E * P, D), F32).ap()
        over_dram = nc.dram_tensor("overflow_rows", (OB * P, D), F32).ap()

        vec_in = Load(semaphore("vec_in")).start(act, [], vec[:, :], io["vec"])
        con_in = Load(semaphore("con_in")).start(act, [], con[:, :], io["con"])

        chunks = []

        def plan(src, k, n):
            chunks.append((src, k, n))

        class Weights:

            def __init__(self, name, view, slots, plan, start=()):
                self.view, self.slots, self.plan = view, slots, plan
                self.started = self.used = self.released = 0
                self.sems = [semaphore(f"{name}{i}") for i in range(slots)]
                self.free = [list(start) for _ in range(slots)]

            def start_next(self):
                if self.started < len(self.plan):
                    i, (src, k, n) = self.started, self.plan[self.started]
                    slot = i % self.slots
                    dst = self.view[:, slot, 0:k * n].rearrange("p (k n) -> p k n", k=k)
                    sp.quiet(self.free[slot], lambda e: e.dma_start(dst, src() if callable(src) else src),
                             self.sems[slot], 16)
                    self.started += 1

            def next(self):
                i = self.used
                _, k, n = self.plan[i]
                self.used += 1
                slot = i % self.slots
                return (self.view[:, slot, 0:k * n].rearrange("p (k n) -> p k n", k=k),
                        (self.sems[slot], 16 * (i // self.slots + 1)))

            def done(self, mark):
                self.free[self.released % self.slots] = [mark]
                self.released += 1
                self.start_next()

            def last_marks(self):
                return [(self.sems[i % self.slots], 16 * (i // self.slots + 1)) for i in range(self.started)][-self.slots:]

        weights = Weights("ring", ring, RING, chunks)

        def rows(w, cols=None):
            w = w if cols is None else w[:, cols[0]:cols[1]]
            return w.rearrange("(k p) n -> p k n", p=P)

        def plan_columns(w, lo, hi, step):
            for a in range(lo, hi, step):
                plan(rows(w, (a, a + step)), w.shape[0] // P, step)

        w_ada, w_in = io["w_ada"][0], io["w_in"][0]
        for k in range(DK):
            plan(w_ada[k * P:(k + 1) * P, 0:2048].unsqueeze(1), 1, 2048)
        plan_columns(w_in, C_KV, C_KV + 256, 256)
        plan_columns(w_in, C_Q, C_Q + 512, 256)
        plan(rows(io["w_kv_up"][0]), 2, 1024)
        plan_columns(w_in, C_QI, C_QI + 512, 256)
        plan_columns(w_in, C_X, C_X + 1536, 256)
        plan_columns(w_in, C_Z, C_Z + 1024, 256)
        for b in range(4):
            for i, (w, lo) in enumerate(((w_in, C_G), (io["w_attn_o"][0], 0), (w_in, C_G + 1024), (io["w_ssm_o"][0], 0))):
                plan_columns(w, lo + 256 * b, lo + 256 * b + 256, 256)
                half, k = divmod(4 * b + i, DK)
                a = 2048 + 2048 * half
                plan(w_ada[k * P:(k + 1) * P, a:a + 2048].unsqueeze(1), 1, 2048)
        plan_columns(io["w_out"][0], 0, D, 256)

        def plan_up(e):
            for k in range(DK):
                plan(io["w_gu"][0][e][k * P:(k + 1) * P, :].unsqueeze(1), 1, 2048)

        def plan_down(e):
            for k in range(0, DK, 2):
                plan(rows(io["w_dn"][0][e][k * P:(k + 2) * P, :]), 2, 1024)

        plan_up(0)
        for e in range(1, E):
            plan_up(e)
            plan_down(e - 1)
        plan_down(E - 1)
        for piece in (1, 0, 2):
            plan_columns(io["a_w_in_2"][0], piece * AW, (piece + 1) * AW, 256)
        plan_columns(io["a_w_out_2"][0], 0, D, 128)
        for b in range(BW // 256):
            plan_columns(io["b_w_in_2"][0], 256 * b, 256 * b + 256, 256)
            plan_columns(io["b_w_in_2"][0], BW + 256 * b, BW + 256 * b + 256, 256)
        plan_columns(io["b_w_out_2"][0], 0, D, 128)
        for _ in range(RING):
            weights.start_next()

        def matmuls(after, pairs, o, start=True, stop=True):
            for i, (lhsT, rhs) in enumerate(pairs):
                last = i == len(pairs) - 1
                f = (lambda e, l=lhsT, r=rhs, s=(start and i == 0), t=(stop and last):
                     e.matmul(o, l, r, start=s, stop=t))
                if last:
                    return pe.do(after if i == 0 else [], f)
                pe.quiet(after if i == 0 else [], f)

        def transpose(after, o, in_):
            return pe.do(after, lambda e: e.transpose(o, in_, ident))

        def copy(eng, after, o, in_, scale=None):
            if eng is act:
                return act.do(after, lambda e: e.activation(o, in_, ACT.Copy, scale=1.0 if scale is None else scale))
            return eng.do(after, lambda e: e.tensor_copy(o, in_) if scale is None else
                          e.tensor_scalar(o, in_, scale, None, ALU.mult))

        def activate(after, o, in_, f, **kw):
            return act.do(after, lambda e: e.activation(o, in_, f, **kw))

        def tt(after, o, a, b, op, eng=None):
            return (eng or dve).do(after, lambda e: e.tensor_tensor(o, a, b, op))

        def ts(after, o, a, s1, op0, s2=None, op1=None, eng=None):
            if op1 is None:
                return (eng or dve).do(after, lambda e: e.tensor_scalar(o, a, s1, None, op0))
            return (eng or dve).do(after, lambda e: e.tensor_scalar(o, a, s1, s2, op0, op1))

        def stt(after, o, a, s, b, op0, op1):
            return dve.do(after, lambda e: e.scalar_tensor_tensor(out=o, in0=a, scalar=s, in1=b, op0=op0, op1=op1))

        rs_ring = Buffers([0, 1])
        sq_ring = Buffers([sq[:, 0, :], sq[:, 1, :]])

        def rsqrt(after, total, n, eps):
            i, j, free = rs_ring.take()
            v, y, t = rs_v[:, :], rs_y[:, j, :], rs_t[:, :]
            m = ts(after + free, v, total, 1.0 / n, ALU.mult, eps, ALU.add)
            a = activate([m] + free, y, v, ACT.Ln)
            a = activate([a], y, y, ACT.Exp, scale=-0.5)
            m = tt([a], t, y, y, ALU.mult)
            m = tt([m], t, t, v, ALU.mult)
            m = ts([m], t, t, -0.5, ALU.mult, 1.5, ALU.add)
            m = tt([m], y, y, t, ALU.mult)
            return i, y, m

        class SquaresOfX:

            def __init__(self):
                self.b, self.bank, self.free = held.take()
                self.waiting, self.n = [], 0

            def add(self, tile, after):
                s, sv, sfree = sq_ring.take()
                a = activate(after + sfree, sv, xT[:, tile, :], ACT.Square)
                self.multiply()
                self.waiting.append((s, sv, a))

            def multiply(self):
                for s, sv, a in self.waiting:
                    first, last = self.n == 0, self.n == DK - 1
                    self.m = pe.do([a] + self.free if first else [a], lambda e, sv=sv, first=first, last=last: e.matmul(
                        self.bank[:, :], ones, sv, start=first, stop=last))
                    sq_ring.release(s, self.m)
                    self.n += 1
                self.waiting.clear()

            def rsqrt(self):
                self.multiply()
                i, y, m = rsqrt([self.m], self.bank[:, :], D, EPS)
                held.release(self.b, m)
                return i, y, m

        def project_steps(ktiles, source, after, n_tiles, sink, step=2):
            tile = 0
            while tile < n_tiles:
                w, arrived = weights.next()
                for c in range(w.shape[2] // P):
                    b, bank, free = dense.take()
                    for k in range(0, ktiles, step):
                        ready = [after[kk] for kk in range(k, k + step)] if isinstance(after, dict) else after
                        m = matmuls(ready + free + [arrived],
                                    [(w[:, kk, c * P:(c + 1) * P], source(kk)) for kk in range(k, k + step)],
                                    bank[:, :], start=(k == 0), stop=(k + step == ktiles))
                        if k + step < ktiles:
                            yield
                    last = m
                    dense.release(b, *sink(tile, bank[:, :], m))
                    tile += 1
                    yield
                weights.done(last)

        def project(ktiles, source, after, n_tiles, sink):
            run(project_steps(ktiles, source, after, n_tiles, sink, 1 if isinstance(after, dict) else ktiles))

        def run(steps, n=None):
            while n is None or n > 0:
                if next(steps, run) is run:
                    return
                n = n if n is None else n - 1

        def join():
            return [e.mark() for e in (pe, act, dve, pool)]

        def softplus(after, o, x, tmp):
            ax, u, s, z = tmp
            m = activate(after, ax, x, ACT.Abs)
            a = activate([m], u, ax, ACT.Exp, scale=-1.0)
            m = ts([a], ax, u, 2.0, ALU.add)
            m = dve.do([m], lambda e: e.reciprocal(ax, ax))
            m = tt([m], s, u, ax, ALU.mult)
            m = tt([m], z, s, s, ALU.mult)
            m = ts([m], u, z, 1.0 / 17, ALU.mult)
            for d in (15, 13, 11, 9, 7, 5, 3):
                m = stt([m], u, u, 1.0 / d, z, ALU.add, ALU.mult)
            m = stt([m], u, u, 1.0, s, ALU.add, ALU.mult)
            m = ts([m], ax, x, 0.0, ALU.max)
            return stt([m], o, u, 2.0, ax, ALU.mult, ALU.add)

        stores = []

        def finish(after):
            sp.quiet(after + stores + weights.last_marks(), None)
            layer.close()
            phase.close()
            close_part(None)
            for engines, flag in parts:
                if flag is None:
                    emit_part(engines)
                else:
                    taken = nc.values_load(flag, min_val=0, max_val=1)
                    with nc.If(taken > 0):
                        emit_part(engines)

        parts = []

        def close_part(flag):
            engines = (pe, act, dve, pool, sp)
            parts.append(([(e, e.queue) for e in engines], flag))
            for e in engines:
                e.queue = []

        def emit_part(engines):
            with nc.Block() as block:
                for (engine, queue), on in zip(engines, (block.tensor, block.scalar, block.vector, block.gpsimd, block.sync)):
                    on(lambda e, engine=engine, queue=queue: engine.emit(e, queue))

        room = Room(work)
        room.at = ROOM - TT * D - 2048
        x_tok = room.take(P, TT, D)
        x_in = Load(semaphore("x_in")).start(act, [], x_tok[:, :, :], io["x"][0].rearrange("(t p) d -> p t d", p=P))
        m_cond = activate([vec_in], cond[:, :], V("c", 0, 8), ACT.Silu)

        mod_mark = {}

        def modulation(block, after, ada):
            m = None
            for k in range(DK):
                w, arrived = weights.next()
                if k == 0:
                    m = ts([arrived, m_cond] + after, ada[:, :], w[:, 0, :], cond[:, k:k + 1], ALU.mult)
                else:
                    m = stt([arrived, m], ada[:, :], w[:, 0, :], cond[:, k:k + 1], ada[:, :], ALU.mult, ALU.add)
                weights.done(m)
                if k < DK - 1:
                    yield
            b, bank, free = banks.take()
            for j in range(16):
                p_ = pe.do([m, con_in] + free, lambda e, j=j: e.matmul(bank[:, j:j + 1], ada[:, j * P:(j + 1) * P],
                                                             ones[:, 0:1], start=True, stop=True))
            ada_read[:] = [p_]
            m = tt([p_, vec_in], mod[:, 16 * block:16 * block + 16], bank[:, 0:16], V("b_ada", 16 * block, 16), ALU.add)
            banks.release(b, m)
            mod_mark[block] = m
            yield

        ada_read = []
        squares = SquaresOfX()
        for k in range(DK):
            b, bank, free = banks.take()
            for t in range(TT):
                m = transpose([x_in, con_in] + free, bank[:, t * P:(t + 1) * P], x_tok[:, t, k * P:(k + 1) * P])
            m = copy(act, [m], xT[:, k, :], bank[:, :])
            banks.release(b, m)
            squares.add(k, [m])
        squares.multiply()
        modulating = modulation(0, [], room.take(P, 2048))
        run(modulating, DK - 1)
        rs_x = squares.rsqrt()
        run(modulating)
        m_mod = mod_mark[0]

        def normalise(gain, shift_block, rs_x, after):
            i, rs, m_rs = rs_x
            for k in range(DK):
                m = stt([m_rs] + after, hT[:, k, :], xT[:, k, :], V(gain[0], gain[1] + k), rs, ALU.mult, ALU.mult)
                h_mark[k] = m
                if shift_block is not None:
                    h_mark[k] = activate([m], hT[:, k, :], hT[:, k, :], ACT.Identity, scale=one_plus[:, k:k + 1],
                                         bias=mod[:, shift_block * 8 + k:shift_block * 8 + k + 1])
            rs_ring.release(i, m)
            return h_mark[DK - 1]

        h_mark = {}
        m_op = ts([m_mod], one_plus[:, :], mod[:, 8:16], 1.0, ALU.add)
        m_h = normalise(("norm_mix", 0), 0, rs_x, [m_op])

        room = Room(work)
        oT = room.take(P, 4, T)
        yT = room.take(P, 8, T)
        wi_dt = room.take(P, TT, 24)
        bcT = room.take(P, 4, T)
        padded = Buffers([room.take(P, T + 8)[:, 0:T + 3] for _ in range(2)])
        after_conv = room.at
        qT, kT, qiT = (room.take(P, 4, T) for _ in range(3))
        kiT = room.take(P, T)
        v_tok = room.take(P, TT, T)
        kvT_at = room.at
        kvT = room.take(P, 2, T)
        rawT = room.take(P, 3, T)
        start = []

        narrow = room.take(P, DK, 152)
        narrow_in = Load(semaphore("narrow_in"))
        for dst, lo, n in ((0, C_KI, 64), (64, C_KI, 64), (128, C_WI, 8), (136, C_DT, 16)):
            m_narrow = narrow_in.start(act, start, narrow[:, :, dst:dst + n], rows(w_in, (lo, lo + n)))

        bias_row = room.take(8, T + P)
        rel = room.take(NB, 8)
        rel_in = Load(semaphore("rel_in")).start(act, start, rel, io["rel_bias"])
        for lo, n in ((0, T), (T, P)):
            b, bank, free = banks.take()
            m = matmuls(free + [rel_in, con_in], [(rel, C("bucket", NB, lo, n))], bank[0:8, 0:n])
            m = copy(dve, start + [m], bias_row[:, lo:lo + n], bank[0:8, 0:n])
            banks.release(b, m)
        bias_out = Load(semaphore("bias_out")).start(act, [m], bias_dram[:, :], bias_row)
        stores.append(bias_out)

        def h_tile(k):
            return hT[:, k, :]

        raw_ring = Buffers([rawT[:, j, :] for j in range(3)])

        def keep_raw(bank, m, scale=None):
            r, raw, rfree = raw_ring.take()
            return r, raw, copy(act, [m] + rfree + start, raw, bank, scale)

        def sink_kv(tile, bank, m):
            return [copy(act, [m] + start, kvT[:, tile, :], bank)]

        gains = room.take(P, 2)
        m_gain = ts([vec_in] + start, gains[:, 0:1], V("q_norm"), HD ** -0.5, ALU.mult)
        heads = C("heads")

        tasks = []

        def advance():
            for task in list(tasks):
                if next(task, run) is run:
                    tasks.remove(task)

        def square(x, after):
            s, sv, sfree = sq_ring.take()
            return s, sv, activate(after + sfree, sv, x, ACT.Square)

        def mean_rsqrt(squared, lhs, n):
            b, bank, free = banks.take()
            for j, (s, sv, a) in enumerate(squared):
                m = pe.do([a] + free, lambda e, sv=sv, j=j: e.matmul(
                    bank[:, :], lhs, sv, start=(j == 0), stop=(j == len(squared) - 1)))
                sq_ring.release(s, m)
            i, y, m = rsqrt([m], bank[:, :], n, EPS)
            banks.release(b, m)
            return i, y, m

        def kv_norm(after):
            squared = [square(kvT[:, j, :], after) for j in range(2)]
            yield
            i, rs, m = mean_rsqrt(squared, ones, 256)
            for j in range(2):
                m = stt([m], kvT[:, j, :], kvT[:, j, :], V("kv_norm", j), rs, ALU.mult, ALU.mult)
            rs_ring.release(i, m)
            kv_mark[0] = m

        def query_norm(tile, r, raw, m):
            squared = [square(raw, [m])]
            yield
            i, rs, m = mean_rsqrt(squared, heads, HD)
            m = stt([m, m_gain], qT[:, tile, :], raw, gains[:, 0:1], rs, ALU.mult, ALU.mult)
            rs_ring.release(i, m)
            raw_ring.release(r, m)

        def key_norms():
            squared = [square(kT[:, 0, :], [m_k])]
            yield
            for tile in range(4):
                if tile < 3:
                    squared.append(square(kT[:, tile + 1, :], [m_k]))
                i, rs, m = mean_rsqrt([squared.pop(0)], heads, HD)
                m = stt([m], kT[:, tile, :], kT[:, tile, :], V("k_norm"), rs, ALU.mult, ALU.mult)
                rs_ring.release(i, m)
                yield

        def index_key_norm(r, raw, m):
            yield
            b, bank, free = banks.take()
            m = matmuls(free + [m], [(heads, raw)], bank[:, :])
            m = stt([m], raw, bank[:, :], -1.0 / HD, raw, ALU.mult, ALU.add)
            banks.release(b, m)
            squared = [square(raw, [m])]
            yield
            i, rs, m = mean_rsqrt(squared, heads, HD)
            m = tt([m], kiT, raw, rs, ALU.mult)
            rs_ring.release(i, m)
            raw_ring.release(r, m)
            ts([m], kiT, kiT, V("idx_k_ln_w"), ALU.mult, V("idx_k_ln_b"), ALU.add)

        kv_mark = {}
        project(DK, h_tile, h_mark, 2, sink_kv)
        tasks.append(kv_norm([act.mark()]))
        advance()

        def sink_q(tile, bank, m):
            r, raw, m = keep_raw(bank, m)
            advance()
            tasks.append(query_norm(tile, r, raw, m))
            next(tasks[-1])
            return [m]

        project(DK, h_tile, [m_h], 4, sink_q)
        b, bank, free = banks.take()
        m = matmuls(free + [m_narrow], [(narrow[:, k, 0:P], hT[:, k, :]) for k in range(DK)], bank[:, :])
        r, raw, m = keep_raw(bank[:, :], m)
        banks.release(b, m)
        advance()
        tasks.append(index_key_norm(r, raw, m))
        advance()
        m_kv = kv_mark[0]
        w_up, arrived = weights.next()
        for c in range(4):
            b, bank, free = banks.take()
            m = matmuls(free + [arrived, m_kv], [(w_up[:, k, c * P:(c + 1) * P], kvT[:, k, :]) for k in range(2)],
                        bank[:, :])
            m_k = copy(act, [m] + start, kT[:, c, :], bank[:, :])
            banks.release(b, m_k)
        tasks.append(key_norms())
        for t in range(TT):
            b, bank, free = banks.take()
            m = matmuls(free + [arrived, m_kv], [(kvT[:, k, t * P:(t + 1) * P], w_up[:, k, 512:1024]) for k in range(2)],
                        bank[:, :])
            if t == TT - 1:
                weights.done(m)
            m = copy(dve, [m] + start, v_tok[:, t, :], bank[:, :])
            banks.release(b, m)
        advance()

        def sink_qi(tile, bank, m):
            m = copy(act, [m] + start, qiT[:, tile, :], bank, HD ** -0.5)
            advance()
            return [m]

        project(DK, h_tile, [m_h], 4, sink_qi)
        while tasks:
            advance()

        b, bank, free = banks.take()
        for t in range(TT):
            m = matmuls(free + [m_narrow], [(hT[:, k, t * P:(t + 1) * P], narrow[:, k, 128:152]) for k in range(DK)],
                        bank[:, 24 * t:24 * t + 24])
        m = copy(dve, [m] + start, wi_dt.rearrange("p a b -> p (a b)"), bank[:, 0:96])
        banks.release(b, m)
        m_wi = ts([m], wi_dt[:, :, 0:8], wi_dt[:, :, 0:8], H ** -0.5, ALU.mult)

        room.at = kvT_at
        bias = room.take(P, H, T)
        keep_buf = [room.take(P, T) for _ in range(2)]
        score, sel_a, sel_b = (room.take(P, T) for _ in range(3))
        best = room.take(P, 8)
        count = room.take(P, 2)
        logit_buf = Buffers([room.take(P, T) for _ in range(3)])
        prob_t_buf = Buffers([room.take(P, T) for _ in range(2)])
        stats = room.take(P, TT * H, 3)
        start = join() + [bias_out]
        row = bias_dram[0:1, 0:1]
        bias_src = bass.AP(row.tensor, row.offset, [[1, P], [T + P, H], [1, T]])
        m_bias = Load(semaphore("bias_in")).start(act, start, bias, bias_src)

        pads = [dve.do(start, lambda e, v=v: e.memset(v[:, 0:3], 0.0)) for v in padded.views]

        def pad(bank, m):
            i, pv, pfree = padded.take()
            return i, pv, copy(act, [m, pads[i]] + pfree + start, pv[:, 3:], bank)

        def convolve(i, pv, m, tile, w_name, tiles, o):
            m = ts([m] + start, o, pv[:, 0:T], V(w_name, tile), ALU.mult)
            for tap in range(1, 4):
                m = stt([m], o, pv[:, tap:tap + T], V(w_name, tap * tiles + tile), o, ALU.mult, ALU.add)
            padded.release(i, m)
            return m

        def channels(tile):
            return yT[:, tile, :] if tile < 8 else bcT[:, tile - 8, :]

        def sink_conv(tile, bank, m):
            i, pv, m = pad(bank, m)
            to_convolve.append((tile, i, pv, m))
            return [m]

        def convolve_pending():
            for tile, i, pv, m in to_convolve:
                conv_mark[tile] = convolve(i, pv, m, tile, "conv_w", CT, channels(tile))
            to_convolve.clear()

        conv_mark, to_convolve = {}, []
        convolution = project_steps(DK, h_tile, [m_h], CT, sink_conv)

        def select(after, src, width, k, cap_a, cap_b, o):
            m = None
            rounds = k // 8
            cur = src
            for r in range(rounds):
                m = dve.do((after if r == 0 else []) + [m], lambda e, cur=cur: e.max(best, cur))
                yield
                if r < rounds - 1:
                    m = dve.do([m], lambda e, cur=cur: e.match_replace(cap_a, best, cur, -3.0e38))
                    cur = cap_a
                    yield
            return threshold(after + [m], src, width, k, best[:, 7:8], cap_a, cap_b, o, count)

        def threshold(after, src, width, k, kth, cap_a, cap_b, o, count):
            m = dve.do(after, lambda e: e.tensor_scalar(o, src, kth, None, ALU.is_gt, ALU.add, accum_out=count[:, 0:1]))
            m = ts([m], count[:, 1:2], count[:, 0:1], -1.0, ALU.mult, float(k), ALU.add)
            m = ts([m], cap_a, src, kth, ALU.is_equal)
            m = dve.do([m], lambda e: e.tensor_tensor_scan(cap_b, cap_a, cap_a, 0.0, ALU.add, ALU.bypass))
            m = stt([m], cap_b, cap_b, count[:, 1:2], cap_a, ALU.is_le, ALU.mult)
            return tt([m], o, o, cap_b, ALU.add)

        def half_of(h):
            return slice((h % 2) * 64, (h % 2) * 64 + 64)

        keep_mark, keep_read = {}, {}

        def choose(t):
            width = (t + 1) * P
            keep, causal = keep_buf[t % 2][:, 0:width], C("causal", P, T - width, width)
            if t == 0:
                keep_mark[0] = copy(dve, start + [con_in], keep, causal)
                return
            sc = score[:, 0:width]
            ahead = []
            for h in range(H + 1):
                if h < H:
                    b, bank, free = banks.take()
                    m = matmuls(free + start, [(qiT[half_of(h), h // 2, t * P:(t + 1) * P], kiT[half_of(h), 0:width])],
                                bank[:, 0:width])
                    r, rv, rfree = sq_ring.take()
                    m = activate([m] + rfree + start, rv[:, 0:width], bank[:, 0:width], ACT.Relu)
                    banks.release(b, m)
                    ahead.append((r, rv, m))
                    yield
                if h == 0:
                    continue
                h, (r, rv, m) = h - 1, ahead.pop(0)
                w = wi_dt[:, t, h:h + 1]
                if h == 0:
                    m_sc = ts([m, m_wi, keep_mark[t - 1]] + start, sc, rv[:, 0:width], w, ALU.mult)
                else:
                    m_sc = stt([m, m_sc], sc, rv[:, 0:width], w, sc, ALU.mult, ALU.add)
                sq_ring.release(r, m_sc)
                yield
            m = tt([m_sc], sc, sc, causal, ALU.add)
            m = yield from select([m, keep_read.get(t - 2)], sc, width, TOPK, sel_a[:, 0:width], sel_b[:, 0:width], keep)
            keep_mark[t] = ts([m], keep, keep, 1.0, ALU.subtract, -NEG, ALU.mult)

        run(choose(0))
        for _ in range(2):
            run(convolution, 4)
            convolve_pending()
        for h in range(H):
            b, bank, free = banks.take()
            m = matmuls(free + [m_bias], [(C("flip"), bias[:, h, :])], bank[:, :])
            bias_in = copy((dve, act)[h % 2], [m], bias[:, h, :], bank[:, :])
            banks.release(b, bias_in)
        bias_in = [dve.mark(), act.mark()]

        banks, qk_banks = Buffers(psum[0:3]), Buffers(psum[3:5])
        start = join()
        logits, exps, scaled, probs = {}, {}, {}, {}

        def query_key(t, h):
            width = (t + 1) * P
            b, bank, free = qk_banks.take()
            logits[t, h] = b, bank, matmuls(
                free + start, [(qT[half_of(h), h // 2, t * P:(t + 1) * P], kT[half_of(h), h // 2, 0:width])], bank[:, 0:width])

        def exponentials(t, h):
            width = (t + 1) * P
            st = stats[:, t * H + h, :]
            b, bank, m = logits.pop((t, h))
            l, lv, lfree = logit_buf.take()
            lw, keep = lv[:, 0:width], keep_buf[t % 2][:, 0:width]
            m = tt([m] + bias_in + lfree, lw, bank[:, 0:width], bias[:, h, T - width:T], ALU.add)
            qk_banks.release(b, m)
            m = dve.do([m, keep_mark[t]], lambda e: e.tensor_tensor_reduce(
                out=lw, in0=lw, in1=keep, scale=1.0, scalar=-3.0e38, op0=ALU.add, op1=ALU.max, accum_out=st[:, 0:1]))
            keep_read[t] = m
            m = ts([m], st[:, 0:1], st[:, 0:1], -1.0, ALU.mult)
            exps[t, h] = l, lw, activate([m], lw, lw, ACT.Exp, bias=st[:, 0:1], accum_out=st[:, 1:2])

        def scale(t, h):
            st = stats[:, t * H + h, :]
            l, lw, m = exps.pop((t, h))
            m = dve.do([m], lambda e: e.reciprocal(st[:, 2:3], st[:, 1:2]))
            scaled[t, h] = l, lw, ts([m], lw, lw, st[:, 2:3], ALU.mult)

        def turn(t, h):
            width = (t + 1) * P
            l, lw, m = scaled.pop((t, h))
            b, bank, free = banks.take()
            for s in range(t + 1):
                mt = transpose(free + [m], bank[:, s * P:(s + 1) * P], lw[:, s * P:(s + 1) * P])
            logit_buf.release(l, mt)
            q, pt, pfree = prob_t_buf.take()
            m = copy(act, [mt] + pfree + start, pt[:, 0:width], bank[:, 0:width])
            banks.release(b, m)
            probs[t, h] = q, pt, m

        def values(t, h):
            q, pt, m = probs.pop((t, h))
            if h == 0:
                out_bank[:] = held.take()
            ob, obank, ofree = out_bank
            m_o = matmuls([m] + ofree, [(v_tok[:, s, h * HD:(h + 1) * HD], pt[:, s * P:(s + 1) * P]) for s in range(t + 1)],
                          obank[half_of(h), (h // 2) * P:(h // 2 + 1) * P])
            prob_t_buf.release(q, m_o)
            if h == H - 1:
                m = copy(act, [m_o], oT[:, :, t * P:(t + 1) * P], obank[:, :].rearrange("p (a b) -> p a b", a=4))
                held.release(ob, m)

        out_bank = []
        units = [(t, h) for t in range(TT) for h in range(H)]

        def step(work_of, u):
            if 0 <= u < len(units):
                work_of(*units[u])

        step(query_key, 0)
        for u in range(len(units) + 2):
            step(query_key, u + 1)
            step(values, u - 2)
            run(convolution, 1 + u % 2)
            if u < len(units) and units[u][1] == 0:
                t = units[u][0]
                if t:
                    run(choosing)
                choosing = choose(t + 1) if t + 1 < TT else iter(())
            step(exponentials, u)
            run(choosing, 3)
            step(scale, u - 1)
            convolve_pending()
            run(choosing, 4)
            step(turn, u - 1)
        run(convolution)
        convolve_pending()
        banks = Buffers(psum[:5])
        m_oT = act.mark()

        room.at = after_conv
        xs_tok = room.take(P, TT, D)
        bm_tok = room.take(P, TT, 2 * SN)
        dt = room.take(P, TT, SH)
        dA = room.take(P, TT, SH)
        a_neg = room.take(P, SH)
        tmp4 = [room.take(P, TT, SH) for _ in range(4)]
        dec = room.take(P, SH)
        x_dt, x_end = room.take(P, D), room.take(P, D)
        cb = room.take(P, 2, P)
        state = room.take(P, D)
        zT = room.take(P, DK, T)
        chunk_at = room.at
        spread = room.take(P, SH, P)
        lmat = room.take(P, SH, P)
        grow = room.take(P, SH, P)
        start = join()

        m_silu = [activate([conv_mark[tile], vec_in], channels(tile), channels(tile), ACT.Silu, bias=V("conv_b", tile))
                  for tile in range(CT)]
        m_xbc = m_silu[-1]

        dtb = V("dt_bias", 0, SH).unsqueeze(1).to_broadcast([P, TT, SH])
        m = tt(start + [m_wi], dt, wi_dt[:, :, 8:24], dtb, ALU.add)
        m = softplus([m], dt, dt, tmp4)
        a = activate(start, a_neg, V("a_log", 0, SH), ACT.Exp)
        m = stt([m, a], dA, dt, -1.0, a_neg.unsqueeze(1).to_broadcast([P, TT, SH]), ALU.mult, ALU.mult)
        m_dA = m

        def sink_z(tile, bank, m):
            return [copy(act, [m] + start, zT[:, tile, :], bank)]

        z_steps = project_steps(DK, h_tile, [m_h], 8, sink_z)

        for t in range(TT):
            for j in range(0, 10, 4):
                n = min(4, 10 - j)
                b, bank, free = banks.take()
                for q in range(n):
                    m = transpose(free + [m_silu[j + q]], bank[:, q * P:(q + 1) * P], channels(j + q)[:, t * P:(t + 1) * P])
                dst = xs_tok[:, t, j * P:(j + 4) * P] if j < 8 else bm_tok[:, t, :]
                m = copy((act, dve)[j == 4], [m] + start, dst, bank[:, 0:n * P])
                banks.release(b, m)
        m_tok = [act.mark(), dve.mark()]

        tri, after_mask = C("tri"), C("after")
        old = start
        for c in range(TT):
            here = slice(c * P, (c + 1) * P)
            m_spread = tt(old + [m_dA, con_in], spread, dA[:, c, :].unsqueeze(2).to_broadcast([P, SH, P]),
                          tri.unsqueeze(1).to_broadcast([P, SH, P]), ALU.mult)
            xs3 = xs_tok[:, c, :].rearrange("p (h d) -> p h d", h=SH)
            x_dt3, x_end3 = (v.rearrange("p (h d) -> p h d", h=SH) for v in (x_dt, x_end))
            m_xdt = tt(m_tok, x_dt3, xs3, dt[:, c, :].unsqueeze(2).to_broadcast([P, SH, SP_]), ALU.mult)
            b, bank, free = banks.take()
            for g in range(SG):
                m = matmuls(free + [m_xbc], [(bcT[:, g, here], bcT[:, 2 + g, here])], bank[:, g * P:(g + 1) * P])
            m_cb = tt([m] + old, cb, bank[:, 0:2 * P].rearrange("p (a b) -> p a b", a=2),
                      tri.unsqueeze(1).to_broadcast([P, SG, P]), ALU.mult)
            banks.release(b, m_cb)
            b, bank, free = banks.take()
            m = matmuls(free + [m_dA], [(after_mask, dA[:, c, :])], bank[:, 0:SH])
            m_dec = activate([m] + old, dec, bank[:, 0:SH], ACT.Exp)
            banks.release(b, m_dec)
            run(z_steps, 2)
            for lhs, dst in ((after_mask, lmat), (ones, grow)):
                for q in range(4):
                    b, bank, free = banks.take()
                    m = matmuls(free + [m_spread], [(lhs, spread[:, 4 * q:4 * q + 4, :].rearrange("p a b -> p (a b)"))],
                                bank[:, :])
                    m_grown = m
                    m = activate([m] + old, dst[:, 4 * q:4 * q + 4, :].rearrange("p a b -> p (a b)"), bank[:, :], ACT.Exp)
                    banks.release(b, m)
                if dst is lmat:
                    m_lmat = m
            m_grow = m
            m_end = tt([m_dec, m_xdt], x_end3, x_dt3, dec.unsqueeze(2).to_broadcast([P, SH, SP_]), ALU.mult)
            m_w, m_cs = [], []
            for g in range(SG):
                hs = slice(8 * g, 8 * g + 8)
                m_w.append(tt([m_lmat, m_cb], lmat[:, hs, :], lmat[:, hs, :],
                              cb[:, g, :].unsqueeze(1).to_broadcast([P, 8, P]), ALU.mult))
                if c:
                    m_cs.append(tt([m_grow, m_grown, m_xbc], spread[:, hs, :], grow[:, hs, :],
                                   bcT[:, 2 + g, here].unsqueeze(1).to_broadcast([P, 8, P]), ALU.mult))
            run(z_steps, 3)
            m_state = m_new if c else None
            for q in range(2):
                b, bank, free = banks.take()
                for pair in range(4):
                    for half in range(2):
                        h = 8 * q + 2 * pair + half
                        terms = [(x_dt[:, h * SP_:(h + 1) * SP_], lmat[:, h, :])]
                        if c:
                            terms.append((state[:, h * SP_:(h + 1) * SP_], spread[:, h, :]))
                        m = matmuls(free + [m_xdt, m_w[q], m_state] + m_cs[q:q + 1], terms,
                                    bank[half * 64:half * 64 + 64, pair * P:(pair + 1) * P])
                for pair in range(4):
                    tile = 4 * q + pair
                    my = stt([m], yT[:, tile, here], yT[:, tile, here], V("d_skip", tile),
                             bank[:, pair * P:(pair + 1) * P], ALU.mult, ALU.add)
                banks.release(b, my)
            if c < TT - 1:
                m_read = m
                for g in range(SG):
                    cols = slice(512 * g, 512 * g + 512)
                    b, bank, free = banks.take()
                    m = matmuls(free + m_tok + [m_end], [(bm_tok[:, c, g * SN:(g + 1) * SN], x_end[:, cols])], bank[:, :])
                    if c == 0:
                        m_new = copy(dve, [m] + start, state[:, cols], bank[:, :])
                    else:
                        st3 = state[:, cols].rearrange("p (h d) -> p h d", h=8)
                        m2 = tt([m_grow, m_read, m_new], st3, st3,
                                grow[:, 8 * g:8 * g + 8, P - 1:P].to_broadcast([P, 8, SP_]), ALU.mult)
                        m_new = tt([m, m2], state[:, cols], state[:, cols], bank[:, :], ALU.add)
                    banks.release(b, m_new)
            old = [m, dve.mark()]
            run(z_steps, 3)
        run(z_steps)
        m_ssd, loop_end = dve.mark(), [pe.mark(), dve.mark()]

        room.at = chunk_at
        mixedT = room.take(P, DK, T)
        gate_buf = Buffers([room.take(P, 2, T) for _ in range(2)])
        ada = xs_tok.rearrange("p a b -> p (a b)")[:, 0:2048]

        def modulations():
            yield from modulation(1, loop_end, ada)
            yield from modulation(2, list(ada_read), ada)

        modulating = modulations()
        gate = {}

        def open_gate(which):
            gi, gv, gfree = gate_buf.take()

            def sink_gate(tile, bank, m):
                return [activate([m] + gfree + loop_end, gv[:, tile, :], bank, ACT.Sigmoid)]

            project(DK, h_tile, [m_h], 2, sink_gate)
            run(modulating, 1)
            gate[which] = (gi, gv, act.mark())

        def mix(blk, which):
            gi, gv, m_gate = gate[which]

            def sink_mix(tile, bank, m):
                o = mixedT[:, 2 * blk + tile, :]
                if which == 0:
                    return [tt([m, m_gate] + loop_end, o, bank, gv[:, tile, :], ALU.mult)]
                m = tt([m, m_gate], gv[:, tile, :], bank, gv[:, tile, :], ALU.mult)
                tt([m], o, o, gv[:, tile, :], ALU.add)
                return [m]

            if which == 0:
                project(4, lambda k: oT[:, k, :], [m_oT], 2, sink_mix)
            else:
                project(DK, lambda k: yT[:, k, :], [m_yT], 2, sink_mix)
            run(modulating, 1)
            gate_buf.release(gi, dve.mark())

        for tile in range(8):
            a = activate([act.mark()], zT[:, tile, :], zT[:, tile, :], ACT.Silu)
            m = tt([a, m_ssd], yT[:, tile, :], yT[:, tile, :], zT[:, tile, :], ALU.mult)
        m_y = m
        open_gate(0)
        mix(0, 0)
        open_gate(1)
        for g in range(SG):
            b, bank, free = banks.take()
            for j in range(4):
                s, sv, a = square(yT[:, 4 * g + j, :], [m_y])
                m = pe.do([a] + free, lambda e, sv=sv, j=j, bank=bank: e.matmul(
                    bank[:, :], ones, sv, start=(j == 0), stop=(j == 3)))
                sq_ring.release(s, m)
            i, rs, m = rsqrt([m], bank[:, :], 512, EPS)
            banks.release(b, m)
            for j in range(4):
                tile = 4 * g + j
                m = stt([m], yT[:, tile, :], yT[:, tile, :], V("ssm_norm", tile), rs, ALU.mult, ALU.mult)
            rs_ring.release(i, m)
        m_yT = m
        mix(0, 1)
        for blk in range(1, 4):
            for which in range(2):
                open_gate(which)
                mix(blk, which)
        run(modulating)
        m_mix = dve.mark()

        squares = SquaresOfX()

        def sink_out(tile, bank, m):
            m = stt([m, mod_mark[1], m_h], xT[:, tile, :], bank, mod[:, 16 + tile:17 + tile], xT[:, tile, :],
                    ALU.mult, ALU.add)
            squares.add(tile, [m])
            return [m]

        project(DK, lambda k: mixedT[:, k, :], [m_mix], DK, sink_out)
        m_x = dve.mark()

        room = Room(work)
        top = room.take(P, TT, E)
        gate_e = room.take(P, TT, E)
        place = room.take(P, TT, E)
        slot_of = room.take(P, TT, E)
        first = room.take(P, TT, E)
        gate_1 = room.take(P, TT, E)
        row_of = room.take(P, TT, E)
        logits = room.take(P, TT, E)
        route_a, route_b = room.take(P, E), room.take(P, E)
        best_r = room.take(P, TT, 8)
        rows_i = room.take(P, TT, 8, dt=I32)
        gates_k = room.take(P, TT, EK)
        totals = room.take(P, E)
        over = room.take(P, 2)
        tok_v = room.take(P, TT, 2, dt=BF16)
        w_router = room.take(P, DK, E)
        after_route = room.at
        h_tok = room.take(P, TT, D)
        start = join()
        router_in = Load(semaphore("router_in")).start(act, start, w_router, rows(io["w_router"][0]))
        m = ts([mod_mark[2], dve.mark()], one_plus[:, :], mod[:, 32:40], 1.0, ALU.add)
        m_h = normalise(("norm_ffn", 0), 3, squares.rsqrt(), [m] + start)

        b, bank, free = banks.take()
        for t in range(TT):
            m = matmuls(free + [m_h, router_in], [(hT[:, k, t * P:(t + 1) * P], w_router[:, k, :]) for k in range(DK)],
                        bank[:, t * E:(t + 1) * E])
        m_log = tt([m] + start, logits, bank[:, 0:TT * E].rearrange("p (a b) -> p a b", a=TT),
                   V("b_router", 0, E).unsqueeze(1).to_broadcast([P, TT, E]), ALU.add)
        banks.release(b, m_log)
        for t in range(TT):
            for j in range(0, DK, 4):
                b, bank, free = banks.take()
                for q in range(4):
                    m = transpose(free + [m_h], bank[:, q * P:(q + 1) * P], hT[:, j + q, t * P:(t + 1) * P])
                m = copy(act, [m], h_tok[:, t, j * P:(j + 4) * P], bank[:, :])
                banks.release(b, m)
        h_out = Load(semaphore("h_out")).start(act, [m], h_dram.rearrange("(t p) d -> p t d", p=P), h_tok)
        stores.append(h_out)

        for t in range(TT):
            lg = logits[:, t, :]
            br = best_r[:, t, :]
            m = dve.do([m_log], lambda e, br=br, lg=lg: e.max(br, lg))
            m = threshold([m], lg, E, EK, br[:, EK - 1:EK], route_a, route_b, top[:, t, :], over)
            m2 = ts([m], route_b, lg, br[:, 0:1], ALU.subtract)
            a = activate([m2], route_b, route_b, ACT.Exp)
            m = dve.do([a, m], lambda e, t=t: e.tensor_tensor_reduce(
                out=gate_e[:, t, :], in0=route_b, in1=top[:, t, :], scale=1.0, scalar=0.0, op0=ALU.mult, op1=ALU.add,
                accum_out=over[:, 0:1]))
            m = dve.do([m], lambda e: e.reciprocal(over[:, 1:2], over[:, 0:1]))
            m = ts([m], gate_e[:, t, :], gate_e[:, t, :], over[:, 1:2], ALU.mult)
        m_top = m
        b, bank, free = banks.take()
        for t in range(TT):
            m = matmuls(free + [m_top], [(C("before"), top[:, t, :])] + [(ones, top[:, s, :]) for s in range(t)],
                        bank[:, t * E:(t + 1) * E])
        m_tot = matmuls([], [(ones, top[:, s, :]) for s in range(TT)], bank[:, TT * E:(TT + 1) * E])
        flat = "p a b -> p (a b)"
        m = stt([m_tot, m_top], place.rearrange(flat), bank[:, 0:TT * E], 1.0, top.rearrange(flat), ALU.add, ALU.mult)
        m_slot = ts([m], slot_of, place, 1.0, ALU.subtract)
        m2 = stt([m], first, place, float(P), top, ALU.is_le, ALU.mult)
        m_g1 = tt([m2], gate_1, gate_e, first, ALU.mult)
        m2 = tt([m2], row_of, place, C("ebase").unsqueeze(1).to_broadcast([P, TT, E]), ALU.add)
        m_row = tt([m2, m_g1], row_of, row_of, first, ALU.mult)
        m_tot = copy(dve, [m_tot, m_slot], totals, bank[:, TT * E:(TT + 1) * E])
        m = dve.do([m_tot, m_row], lambda e, bank=bank: e.tensor_reduce(over[:, 0:1], bank[:, TT * E:(TT + 1) * E], AX.X, ALU.max))
        banks.release(b, m)
        m_over = ts([m], over_i[:, 0:1], over[:, 0:1], float(P), ALU.is_gt)
        for t in range(TT):
            m = copy(dve, [con_in], tok_v[:, t, 0:1], C("tok", P, 0, 1))
            m = ts([con_in], tok_v[:, t, 1:2], C("tok", P, 1, 1), float(t * P), ALU.mult)
        m_tokv = m
        room.at = after_route
        y_tok = room.take(P, TT, D)
        after_y = room.at
        picked_room = room.take(P, 2, D)
        pick = Buffers([room.take(P, TT, P, dt=BF16) for _ in range(2)])
        index_sum = room.take(P, 1)
        index = Buffers([room.take(P, 1, dt=I32) for _ in range(2)])
        xe = Buffers([room.take(P, D) for _ in range(2)])
        xeT = Buffers([room.take(P, DK, P) for _ in range(2)])
        bias_rows = room.take(P, 3 * D)
        bias_all = Buffers([room.take(P, 3 * D) for _ in range(3)])
        g_act, u_act, s_act = room.take(P, D), room.take(P, D), room.take(P, D)
        acted = room.take(P, D)
        aT = room.take(P, DK, P)
        ye = Buffers([room.take(P, D) for _ in range(2)])
        moe_end = room.at
        moe_start = join() + [h_out]
        up_banks, turn_banks, down_banks = psum[0:4], Buffers(psum[4:6]), psum[6:8]
        up_free, down_free = [], []
        bias_load = [Load(semaphore(f"bias_row{j}")) for j in range(2)]
        xe_load = [Load(semaphore(f"xe_in{j}")) for j in range(2)]
        ye_store = [Load(semaphore(f"ye_out{j}")) for j in range(2)]
        bias_row_free, bias_row_turn = [None, None], [1]

        def gather_rows(after, o, table, ids, load):
            load.count += 16
            prior = pool.mark()
            pool.count += 1
            done = pool.sem
            pool.quiet(after + [prior], lambda e: e.indirect_dma_start(
                out=o, out_offset=None, in_=table, in_offset=bass.IndirectOffsetOnAxis(ap=ids, axis=0),
                engine_sem=done), load.sem, 16)
            return (load.sem, load.count)

        def gather_tokens(slots):
            i, pv, pfree = pick.take()
            for t in range(TT):
                m = ts(moe_start + pfree + slots[1], pv[:, t, :], C("slot"), slots[0](t), ALU.is_equal)
            b, bank, free = turn_banks.take()
            m = matmuls(free + moe_start + [m, m_tokv], [(pv[:, t, :], tok_v[:, t, :]) for t in range(TT)], bank[:, 0:2])
            pick.release(i, m)
            j, iv, ifree = index.take()
            m = dve.do([m] + ifree, lambda e, o=index_sum: e.tensor_reduce(o, bank[:, 0:2], AX.X, ALU.add))
            turn_banks.release(b, m)
            m = copy(dve, [m], iv, index_sum)
            j2, xv, xfree = xe.take()
            landed = gather_rows([m] + xfree, xv, h_dram, iv, xe_load[j2])
            index.release(j, landed)
            return j2, xv, landed

        def turn_tokens(j2, xv, landed):
            i, tv, tfree = xeT.take()
            for q in range(0, DK, 4):
                b, bank, free = turn_banks.take()
                for r in range(4):
                    m = transpose(free + [landed], bank[:, r * P:(r + 1) * P], xv[:, (q + r) * P:(q + r + 1) * P])
                m_t = m
                m = copy(act, [m] + tfree, tv[:, q:q + 4, :].rearrange(flat), bank[:, :])
                turn_banks.release(b, m)
            xe.release(j2, m_t)
            return i, tv, m

        gathered = []

        def spread_bias(e_gu, e_dn, marks=()):
            held_bias, bv, bfree = bias_all.take()
            j = bias_row_turn[0] = 1 - bias_row_turn[0]
            row = bias_rows[32 * j:32 * j + 1, :]
            bias_load[j].start(act, moe_start + [bias_row_free[j]] + list(marks), row[:, 0:2 * D], e_gu)
            m = bias_load[j].start(act, [], row[:, 2 * D:3 * D], e_dn)
            m = pool.do([m, pool.mark()] + gathered + bfree + moe_start, lambda e: e.partition_broadcast(bv, row))
            bias_row_free[j] = m
            return held_bias, bv, m

        def up_part(tv, after, lo, hi):
            for k in range(lo, hi):
                w, arrived = weights.next()
                for n in range(4):
                    f = (lambda e, n=n, w=w, k=k: e.matmul(up_banks[n][:, :], tv[:, k, :], w[:, 0, n * 512:(n + 1) * 512],
                                                           start=(k == 0), stop=(k == DK - 1)))
                    m = pe.do(after + up_free + [arrived], f)
                weights.done(m)
            return m

        def gate_up(m, bv, m_bias):
            for n in range(4):
                o = (g_act if n < 2 else u_act)[:, (n % 2) * 512:(n % 2) * 512 + 512]
                r = tt([m, m_bias, act.mark()], o, up_banks[n][:, :], bv[:, n * 512:(n + 1) * 512], ALU.add)
            up_free[:] = [r]
            m = ts([r], g_act, g_act, 7.0, ALU.min)
            a = activate([m], s_act, g_act, ACT.Sigmoid, scale=1.702)
            m = ts([r], u_act, u_act, 7.0, ALU.min, -7.0, ALU.max)
            m2 = tt([a], g_act, g_act, s_act, ALU.mult)
            return stt([m, m2] + acted_free, acted, u_act, 1.0, g_act, ALU.add, ALU.mult)

        acted_free, aT_free = [], []

        def turn_acted(m_act):
            for q in range(0, DK, 4):
                b, bank, free = turn_banks.take()
                for r in range(4):
                    m = transpose(free + [m_act], bank[:, r * P:(r + 1) * P], acted[:, (q + r) * P:(q + r + 1) * P])
                m_t = m
                m = copy(act, [m] + aT_free, aT[:, q:q + 4, :].rearrange(flat), bank[:, :])
                turn_banks.release(b, m)
            acted_free[:] = [m_t]
            return m

        def down(m_aT, j, bv, m_bias, dst):
            for k in range(0, DK, 2):
                w, arrived = weights.next()
                for kk in range(2):
                    for n in range(2):
                        f = (lambda e, n=n, w=w, k=k, kk=kk, x=aT: e.matmul(
                            down_banks[n][:, :], x[:, k + kk, :], w[:, kk, n * 512:(n + 1) * 512],
                            start=(k + kk == 0), stop=(k + kk == DK - 1)))
                        m = pe.do([m_aT, arrived] + down_free, f)
                weights.done(m)
            aT_free[:] = [m]
            i, yv, yfree = ye.take()
            for n in range(2):
                r = tt([m, m_bias] + yfree, yv[:, n * 512:(n + 1) * 512], down_banks[n][:, :],
                       bv[:, 2 * D + n * 512:2 * D + (n + 1) * 512], ALU.add)
            down_free[:] = [r]
            if j is not None:
                bias_all.release(j, r)
            m = ye_store[i].start(act, [r], dst, yv)
            ye.release(i, m)
            return m

        def primary(e):
            return gather_tokens((lambda t: slot_of[:, t, e:e + 1], [m_slot]))

        def bias_of(e):
            return spread_bias(io["b_gu"][0][e:e + 1, :], io["b_dn"][0][e:e + 1, :])

        picked = Buffers([picked_room[:, 0, :], picked_room[:, 1, :], *xe.views])
        picked_load = [Load(semaphore(f"picked{j}")) for j in range(4)]
        y_load = Load(semaphore("y_tok_in"))
        to_add = []

        def add_picked():
            for t, k, j, pv, landed in to_add:
                if k == EK - 1:
                    m_y[t] = ts([landed], y_tok[:, t, :], y_tok[:, t, :], gates_k[:, t, k:k + 1], ALU.mult)
                else:
                    m_y[t] = stt([landed, m_y[t]], y_tok[:, t, :], pv, gates_k[:, t, k:k + 1], y_tok[:, t, :],
                                 ALU.mult, ALU.add)
                    picked.release(j, m_y[t])
            to_add.clear()

        m_y = {}

        def pick_rows(k):
            add_picked()
            if k == EK - 2:
                for j in (2, 3):
                    picked.release(j, pe.mark())
            table = y_dram[0:(E - k) * P, :]
            wait = moe_start + [(s.sem, s.count) for s in ye_store] + [m_rows]
            gathered.clear()
            for t in range(TT):
                ids = rows_i[:, t, k:k + 1]
                if k == EK - 1:
                    landed = gather_rows(wait, y_tok[:, t, :], table, ids, y_load)
                else:
                    j, pv, pfree = picked.take()
                    landed = gather_rows(wait + pfree, pv, table, ids, picked_load[j])
                    to_add.append((t, k, j, pv, landed))
                    gathered.append(landed)
            if k == EK - 1:
                to_add.extend((t, k, None, None, landed) for t in range(TT))
                gathered.append(landed)

        tokens = turn_tokens(*primary(0))
        for t in range(TT):
            br = best_r[:, t, :]
            m = dve.do([m_row], lambda e, br=br, t=t: e.max(br, row_of[:, t, :]))
            for k in range(EK):
                m2 = dve.do([m], lambda e, br=br, t=t, k=k: e.scalar_tensor_tensor(
                    out=route_a, in0=row_of[:, t, :], scalar=br[:, k:k + 1], in1=gate_1[:, t, :],
                    op0=ALU.is_equal, op1=ALU.mult, accum_out=gates_k[:, t, k:k + 1]))
                m = m2
            m_rows = ts([m], rows_i[:, t, :], br, 1.0, ALU.subtract, 0.0, ALU.max)
        ahead = primary(1)
        biases = {0: bias_of(0)}
        for e in range(E):
            i, tv, m_tv = tokens
            if e:
                m_aT = turn_acted(m_act)
            up_part(tv, [m_tv], 0, 4)
            if e + 1 < E:
                tokens = turn_tokens(*ahead)
                biases[e + 1] = bias_of(e + 1)
            if e + 2 < E:
                ahead = primary(e + 2)
            m = up_part(tv, [], 4, DK)
            xeT.release(i, m)
            m_act = gate_up(m, *biases[e][1:])
            if e:
                down(m_aT, *biases.pop(e - 1), y_dram[(e - 1) * P:e * P, :])
            if e >= E - EK + 1:
                pick_rows(E - e)
        down(turn_acted(m_act), *biases.pop(E - 1), y_dram[(E - 1) * P:E * P, :])
        stored = [(s.sem, s.count) for s in ye_store]
        stores.extend(stored)

        pick_rows(0)
        add_picked()
        m_y_tok = m_y[TT - 1]

        close_part(None)
        main = (pe, act, dve, pool, sp, weights, m_y_tok)
        pe, act, dve, pool, sp = (Engine(semaphore("over_" + n)) for n in ("pe", "act", "dve", "pool", "sp"))
        room.at = after_y
        over_count, incl, base, hot, hot_a = (room.take(P, E) for _ in range(5))
        over_place = room.take(P, OB, TT)
        over_e, over_b = room.take(P, OB), room.take(P, OB)
        over_e_i = room.take(P, OB, dt=I32)
        row_over, gate_over = room.take(P, TT, E), room.take(P, TT, E)
        over_ring = room.take(P, 4, SLOT)
        pick = Buffers([room.take(P, TT, P, dt=BF16)])
        index_sum = room.take(P, 1)
        index = Buffers([room.take(P, 1, dt=I32)])
        xe, xeT = Buffers([room.take(P, D)]), Buffers([room.take(P, DK, P)])
        bias_one = room.take(P, 3 * D)
        g_act, u_act, s_act, acted = (room.take(P, D) for _ in range(4))
        aT = room.take(P, DK, P)
        ye = Buffers([room.take(P, D)])
        moe_start, m_tokv = [], None
        turn_banks = Buffers(psum[4:6])
        for marks in (up_free, down_free, acted_free, aT_free):
            marks[:] = []
        xe_load, ye_store = [Load(semaphore("over_xe_in"))], [Load(semaphore("over_ye_out"))]
        over_bias = Load(semaphore("over_bias_in"))
        picked_load = [Load(semaphore("over_picked_in"))]

        m = ts([], over_count, totals, float(P), ALU.is_gt)
        for k in (2, 3):
            m = stt([m], over_count, totals, float(k * P), over_count, ALU.is_gt, ALU.add)
        m = dve.do([m], lambda e: e.tensor_tensor_scan(incl, over_count, over_count, 0.0, ALU.add, ALU.bypass))
        m = tt([m], base, incl, over_count, ALU.subtract)
        for j in range(OB):
            m = ts([m], hot_a, base, float(j), ALU.is_le)
            m = stt([m], hot, incl, float(j), hot_a, ALU.is_gt, ALU.mult)
            for dst, src in [(over_e[:, j:j + 1], C("eone")), (over_b[:, j:j + 1], base)] + [
                    (over_place[:, j, t:t + 1], place[:, t, :]) for t in range(TT)]:
                m = dve.do([m], lambda e, dst=dst, src=src: e.tensor_tensor_reduce(
                    out=hot_a, in0=hot, in1=src, scale=1.0, scalar=0.0, op0=ALU.mult, op1=ALU.add, accum_out=dst))
            m = ts([m], over_b[:, j:j + 1], over_b[:, j:j + 1], float(P), ALU.mult, -float(P * (1 + j) + 1), ALU.add)
            m = ts([m], over_place[:, j, :], over_place[:, j, :], over_b[:, j:j + 1], ALU.add)
        m_list = m
        m_e = copy(dve, [m], over_e_i, over_e)
        m = ts([m], row_over, place, float(P), ALU.is_gt)
        m_gate = tt([m], gate_over, row_over, gate_e, ALU.mult)
        m = ts([m], base, base, float(P), ALU.mult, -float(P), ALU.add)
        m = tt([m], logits, place, base.unsqueeze(1).to_broadcast([P, TT, E]), ALU.add)
        m_row = tt([m, m_gate], row_over, row_over, logits, ALU.mult)

        expert = {}

        def over_chunks(j):
            def up(k):
                return lambda: io["w_gu"][0][bass.ds(expert[j], 1), k * P:(k + 1) * P, :].rearrange("a p n -> p a n")

            def dn(k):
                return lambda: io["w_dn"][0][bass.ds(expert[j], 1), k * P:(k + 2) * P, :].rearrange(
                    "a (k p) n -> p (a k) n", p=P)
            return [(up(k), 1, 2048) for k in range(DK)] + [(dn(k), 2, 1024) for k in range(0, DK, 2)]

        def read_expert(e, j):
            expert[j] = e.value_load(over_e_i[0:1, j:j + 1], min_val=0, max_val=E - 1)

        weights = Weights("over_ring", over_ring, 4, [])
        m = None
        for j in range(OB):
            weights.plan.extend(over_chunks(j))
            sp.quiet([m_e], lambda e, j=j: read_expert(e, j))
            over_bias.start(sp, [m], bias_one[:, 0:2 * D],
                            lambda j=j: io["b_gu"][0][bass.ds(expert[j], 1), :].to_broadcast([P, 2 * D]))
            m_bias = over_bias.start(sp, [], bias_one[:, 2 * D:3 * D],
                                     lambda j=j: io["b_dn"][0][bass.ds(expert[j], 1), :].to_broadcast([P, D]))
            for _ in range(4):
                weights.start_next()
            got = gather_tokens((lambda t: over_place[:, j, t:t + 1], [m_list]))
            i, tv, m_tv = turn_tokens(*got)
            m = up_part(tv, [m_tv], 0, DK)
            xeT.release(i, m)
            m_act = gate_up(m, bias_one, m_bias)
            down(turn_acted(m_act), None, bias_one, m_bias, over_dram[j * P:(j + 1) * P, :])
            m = dve.mark()
        stored_over = (ye_store[0].sem, ye_store[0].count)
        for t in range(TT):
            br = best_r[:, t, :]
            m = dve.do([m_row], lambda e, br=br, t=t: e.max(br, row_over[:, t, :]))
            for k in range(EK):
                m = dve.do([m], lambda e, br=br, t=t, k=k: e.scalar_tensor_tensor(
                    out=hot, in0=row_over[:, t, :], scalar=br[:, k:k + 1], in1=gate_over[:, t, :],
                    op0=ALU.is_equal, op1=ALU.mult, accum_out=gates_k[:, t, k:k + 1]))
            m = ts([m], rows_i[:, t, :], br, 1.0, ALU.subtract, 0.0, ALU.max)
            for k in range(EK):
                landed = gather_rows([m, stored_over], xe.views[0], over_dram, rows_i[:, t, k:k + 1], picked_load[0])
                m = stt([landed, m], y_tok[:, t, :], xe.views[0], gates_k[:, t, k:k + 1], y_tok[:, t, :], ALU.mult, ALU.add)
        sp.quiet(join() + [stored_over] + weights.last_marks(), None)
        close_part(over_i[0:1, 0:1])
        pe, act, dve, pool, sp, weights, m_y = main

        banks = dense = Buffers(psum[:6])
        held = Buffers(psum[6:])
        squares = SquaresOfX()
        for k in range(DK):
            b, bank, free = banks.take()
            for t in range(TT):
                m = transpose(free + start + [m_y], bank[:, t * P:(t + 1) * P], y_tok[:, t, k * P:(k + 1) * P])
            m = stt([m], xT[:, k, :], bank[:, :], mod[:, 40 + k:41 + k], xT[:, k, :], ALU.mult, ALU.add)
            banks.release(b, m)
            squares.add(k, [m])
        m_x = m
        rs_x = squares.rsqrt()

        phase.close()
        phase = ExitStack()
        h_hi, h_lo = (sb(n, [P, DK, T], F32R, where=phase) for n in ("h_hi", "h_lo"))
        w_hi, w_lo = (sb(n, [P, SPLIT, HALF], F32R, where=phase) for n in ("w_hi", "w_lo"))
        late_words = ROOM + DK * T - 2 * DK * T - 2 * SPLIT * HALF
        uT = sb("uT", [P, AW // P, T], where=phase)
        layer = ExitStack()
        work = sb("work_gmlp", [P, late_words - AW // P * T], where=layer)
        split_slots = Buffers([(w_hi[:, j, :], w_lo[:, j, :]) for j in range(SPLIT)])
        passes = ((0, 0), (0, 1), (1, 0))

        def split(after, hi, lo, x):
            a = activate(after, hi, x, ACT.Copy)
            return tt([a], lo, x, hi.bitcast(F32), ALU.subtract)

        def normalise_split(gain, rs_x, after):
            i, rs, m_rs = rs_x
            for k in range(DK):
                s, sv, sfree = sq_ring.take()
                m = stt([m_rs] + sfree + after, sv, xT[:, k, :], V(gain[0], gain[1] + k), rs, ALU.mult, ALU.mult)
                m = split([m], h_hi[:, k, :], h_lo[:, k, :], sv)
                sq_ring.release(s, m)
                m_hk[k] = m
            rs_ring.release(i, m)

        m_hk = {}
        prepared = []

        def prepare_chunk():
            w, arrived = weights.next()
            halves = []
            kh, n = w.shape[1] // 2, w.shape[2]
            for half in range(2):
                i, views, free = split_slots.take()
                hi, lo = (v[:, 0:kh * n] for v in views)
                m = split([arrived] + free + start, hi, lo, w[:, kh * half:kh * half + kh, :].rearrange(flat))
                halves.append((i, [v.rearrange("p (k n) -> p k n", k=kh) for v in (hi, lo)], m))
            weights.done(m)
            prepared.append(halves)

        def split_chunk():
            while len(prepared) < 2 and weights.used < split_until:
                prepare_chunk()
            return prepared.pop(0)

        def release_chunk(halves, m):
            for i, _, _ in halves:
                split_slots.release(i, m)

        def h_parts(k):
            return h_hi[:, k, :], h_lo[:, k, :]

        def project_split(n_tiles, sink, ktiles=DK, source=h_parts, ready=None):
            for tile in range(n_tiles):
                if not in_use:
                    in_use[:] = [0, split_chunk()]
                c, halves = in_use
                b, bank, free = banks.take()
                for k in range(ktiles):
                    _, w, m_w = halves[k // (ktiles // 2)]
                    x = source(k)
                    m = matmuls(free + [m_w, (ready or m_hk)[k]],
                                [(w[j][:, k % (ktiles // 2), c * P:(c + 1) * P], x[i]) for i, j in passes],
                                bank[:, :], start=(k == 0), stop=(k == ktiles - 1))
                in_use[0] = c + 1
                if (c + 1) * P == w[0].shape[2]:
                    release_chunk(halves, m)
                    in_use.clear()
                banks.release(b, *sink(tile, bank[:, :], m))

        def project_out(xT_, ktiles, lo):
            done = [pe.mark(), dve.mark()]

            def source(k):
                return (h_hi[:, k, :] if k < DK else h_lo[:, k - DK, :]), lo[:, k, :]

            ready = {k: split(done, *source(k), xT_[:, k, :]) for k in range(ktiles)}
            project_split(DK, sink_add, ktiles, source, ready)

        in_use = []
        room = Room(work)
        v_tok = room.take(P, TT, AW)
        b_s = room.take(P, 8, P)
        w_sT = room.take(P, 8, P)
        ln_row = room.take(P, AW)
        part = room.take(P, TT, 8)
        stat = room.take(P, TT, 4)
        start = join()
        w_s_load, ln_load = Load(semaphore("w_s_in")), Load(semaphore("ln_in"))
        w_s_raw = ln_row.rearrange("p (a b) -> p a b", a=16)[:, 0:8, :]
        w_s_in = w_s_load.start(act, start, w_s_raw, io["a_w_s_2"][0].rearrange("g t s -> t g s"))
        b_s_in = Load(semaphore("b_s_in")).start(
            act, start, b_s.rearrange(flat),
            io["a_b_s_2"].rearrange("a g t -> a (g t)").to_broadcast([P, 8 * P]))
        split_until = weights.used + 3 * AW // 256 + DK
        prepare_chunk()
        normalise_split(("norm_w_2", 0), rs_x, start)
        for piece in range(8):
            halves = split_chunk()
            for t in range(TT):
                b, bank, free = banks.take()
                for k in range(DK):
                    _, w, m_w = halves[k // 4]
                    m = matmuls(free + [m_w, m_hk[k]],
                                [((h_hi, h_lo)[i][:, k, t * P:(t + 1) * P], w[j][:, k % 4, :]) for i, j in passes],
                                bank[:, 0:256], start=(k == 0), stop=(k == DK - 1))
                a = activate([m] + start, v_tok[:, t, piece * 256:(piece + 1) * 256], bank[:, 0:256],
                             ACT.Gelu_apprx_tanh, accum_out=part[:, t, piece:piece + 1])
                banks.release(b, a)
            release_chunk(halves, m)
        m_v = a
        for g in range(0, 8, 4):
            b, bank, free = banks.take()
            for q in range(4):
                m = transpose(free + [w_s_in], bank[:, q * P:(q + 1) * P], w_s_raw[:, g + q, :])
            m = tt([m] + start, w_sT[:, g:g + 4, :], bank[:, :].rearrange("p (a b) -> p a b", a=4),
                   C("tri").unsqueeze(1).to_broadcast([P, 4, P]), ALU.mult)
            banks.release(b, m)
        m_ws = m
        ln_in = ln_load.start(act, [pe.mark()], ln_row, io["a_ln_w_2"].to_broadcast([P, AW]))

        def layer_norm():
            for t in range(TT):
                vt = v_tok[:, t, :]
                m = dve.do([m_v], lambda e, t=t: e.tensor_reduce(stat[:, t, 0:1], part[:, t, :], AX.X, ALU.add))
                m = ts([m], stat[:, t, 0:1], stat[:, t, 0:1], 1.0 / AW, ALU.mult)
                m = ts([m], vt, vt, stat[:, t, 0:1], ALU.subtract)
                for q in range(4):
                    s, sv, sfree = sq_ring.take()
                    m2 = activate([m] + sfree, sv, vt[:, q * 512:(q + 1) * 512], ACT.Square, accum_out=part[:, t, q:q + 1])
                    sq_ring.release(s, m2)
                yield
                m = dve.do([m2], lambda e, t=t: e.tensor_reduce(stat[:, t, 1:2], part[:, t, 0:4], AX.X, ALU.add))
                m = ts([m], stat[:, t, 1:2], stat[:, t, 1:2], 1.0 / AW, ALU.mult, LN_EPS, ALU.add)
                a = activate([m], stat[:, t, 2:3], stat[:, t, 1:2], ACT.Sqrt)
                m = dve.do([a], lambda e, t=t: e.reciprocal(stat[:, t, 3:4], stat[:, t, 2:3]))
                m = stt([m, ln_in], vt, vt, stat[:, t, 3:4], ln_row, ALU.mult, ALU.mult)
                yield
            bias_in = ln_load.start(act, [m], ln_row, io["a_ln_b_2"].to_broadcast([P, AW]))
            for t in range(TT):
                norm_mark[0] = tt([m, bias_in], v_tok[:, t, :], v_tok[:, t, :], ln_row, ALU.add)
                yield

        norm_mark, norming = {}, layer_norm()

        def sink_u(tile, bank, m):
            m = activate([m] + start, uT[:, tile, :], bank, ACT.Gelu_apprx_tanh)
            run(norming, 1)
            return [m]

        project_split(AW // P, sink_u)
        run(norming)
        m_v = norm_mark[0]
        s_buf = Buffers([ln_row[:, 0:T], ln_row[:, T:2 * T]])
        g_buf = Buffers([ln_row[:, 2 * T:3 * T], ln_row[:, 3 * T:4 * T]])

        def sink_spatial(tile, bank, m):
            g = tile // 2
            i, gv, gfree = g_buf.take()
            a = activate([m, m_v] + gfree, gv, bank, ACT.Silu)
            b, sbank, free = held.take()
            for t in range(TT):
                m = matmuls(free + [m_v, m_ws], [(v_tok[:, t, tile * P:(tile + 1) * P], w_sT[:, g, :])],
                            sbank[:, t * P:(t + 1) * P])
            j, sv, sfree = s_buf.take()
            m = tt([m, b_s_in, m_v] + sfree, sv.rearrange("p (a b) -> p a b", a=TT),
                   sbank[:, :].rearrange("p (a b) -> p a b", a=TT), b_s[:, g, :].unsqueeze(1).to_broadcast([P, TT, P]),
                   ALU.add)
            held.release(b, m)
            m = tt([m], sv, sv, uT[:, tile, :], ALU.mult)
            m = tt([m, a], uT[:, tile, :], sv, gv, ALU.mult)
            s_buf.release(j, m)
            g_buf.release(i, m)
            return [a]

        project_split(AW // P, sink_spatial)
        m_y = dve.mark()

        def sink_add(tile, bank, m):
            m = tt([m], xT[:, tile, :], xT[:, tile, :], bank, ALU.add)
            squares.add(tile, [m])
            return [m]

        squares = SquaresOfX()
        layer.close()
        layer = ExitStack()
        start = []
        project_out(uT, AW // P, sb("u_lo", [P, AW // P, T], F32R, where=layer))
        m_x = dve.mark()
        rs_x = squares.rsqrt()

        layer.close()
        layer = ExitStack()
        work = sb("work_rglru", [P, late_words - AW // P * T], where=layer)
        room = Room(work)
        yT = uT[:, 0:BT, :]
        gate_w = room.take(P, 2, BT, P)
        padded = Buffers([room.take(P, T + 8)[:, 0:T + 3] for _ in range(2)])
        conv_buf = Buffers([room.take(P, T) for _ in range(4)])
        silu_buf = Buffers([room.take(P, T) for _ in range(4)])
        tmp = Buffers([room.take(P, 4, T) for _ in range(2)])
        lam, minus_lam = room.take(P, BT), room.take(P, BT)
        tmp4 = [room.take(P, BT) for _ in range(4)]
        start = join()
        gate_load = Load(semaphore("gate_w_in"))
        for j, name in enumerate(("b_gate_a_w_2", "b_gate_x_w_2")):
            gate_in = gate_load.start(act, start, gate_w[:, j, :, :], io[name][0].rearrange("h i j -> i h j"))
        split_until = weights.used + 2 * BW // 256 + DK
        prepare_chunk()
        normalise_split(("norm_w_2", 8), rs_x, start)
        m = ts([vec_in] + start, lam, V("b_lambda_2", 0, BT), -1.0, ALU.mult)
        m = softplus([m], lam, lam, tmp4)
        m = ts([m], lam, lam, 8.0, ALU.mult)
        m_lam = ts([m], minus_lam, lam, -1.0, ALU.mult)
        pads = [dve.do(start, lambda e, v=v: e.memset(v[:, 0:3], 0.0)) for v in padded.views]
        convolved, silus = {}, {}

        def sink_branch(tile, bank, m):
            i, cv, cfree = conv_buf.take()
            p_, pv, bank_read = pad(bank, m)
            dve.quiet(cfree, None)
            m = convolve(p_, pv, bank_read, tile, "b_conv_w_2", BT, cv)
            convolved[tile] = (i, cv, ts([m], cv, cv, V("b_conv_b_2", tile), ALU.add))
            return [bank_read]

        def sink_silu(tile, bank, m):
            i, gz, free = silu_buf.take()
            m = activate([m] + free + start, gz, bank, ACT.Silu)
            silus[tile] = (i, gz, m)
            return [m]

        def recurrence(tiles):
            ctx = []
            for tile in tiles:
                k, tv, tfree = tmp.take()
                ctx.append((tile, *(tv[:, j, :] for j in range(4)), convolved.pop(tile), silus.pop(tile), k, tfree))
            gates = {}
            for j, name in enumerate(("b_gate_a_b_2", "b_gate_x_b_2")):
                for tile, r, inp, a_, tau, (_, cv, m_c), _, _, tfree in ctx:
                    b, gbank, free = held.take()
                    m = matmuls(free + [m_c, gate_in], [(gate_w[:, j, tile, :], cv)], gbank[:, :])
                    gates[j, tile] = activate([m] + tfree, (r, inp)[j], gbank[:, :], ACT.Sigmoid, bias=V(name, tile))
                    held.release(b, gates[j, tile])
            yield
            m_a, m_t, m_i = {}, {}, {}
            for tile, r, inp, a_, tau, *_ in ctx:
                m_t[tile] = activate([gates[0, tile], m_lam], tau, r, ACT.Tanh, scale=lam[:, tile:tile + 1])
            for tile, r, inp, a_, tau, *_ in ctx:
                m_a[tile] = activate([m_lam], a_, r, ACT.Exp, scale=minus_lam[:, tile:tile + 1])
            for tile, r, inp, a_, tau, (i, cv, _), *_ in ctx:
                m_i[tile] = tt([gates[1, tile]], inp, inp, cv, ALU.mult)
                conv_buf.release(i, m_i[tile])
            yield
            for tile, r, inp, a_, tau, *_ in ctx:
                m = activate([m_a[tile]], r, a_, ACT.Square)
                m_t[tile] = stt([m, m_t[tile]], tau, r, 1.0, tau, ALU.add, ALU.mult)
            for tile, r, inp, a_, tau, *_ in ctx:
                m_t[tile] = activate([m_t[tile]], tau, tau, ACT.Sqrt)
            yield
            for tile, r, inp, a_, tau, *_ in ctx:
                m_t[tile] = tt([m_t[tile], m_i[tile]], inp, inp, tau, ALU.mult)
            for tile, r, inp, a_, tau, *_ in ctx:
                m_t[tile] = dve.do([m_t[tile], m_a[tile]], lambda e, r=r, a_=a_, inp=inp: e.tensor_tensor_scan(
                    r, a_, inp, 0.0, ALU.mult, ALU.add))
            for tile, r, inp, a_, tau, _, (i, gz, m_gz), k, _ in ctx:
                m = tt([m_t[tile], m_gz], yT[:, tile, :], r, gz, ALU.mult)
                tmp.release(k, m)
                silu_buf.release(i, m)

        steps = iter(())
        for blk in range(BT // 2):
            run(steps, 1)
            project_split(1, lambda tile, bank, m: sink_branch(2 * blk, bank, m))
            run(steps, 1)
            project_split(1, lambda tile, bank, m: sink_branch(2 * blk + 1, bank, m))
            run(steps, 1)
            project_split(1, lambda tile, bank, m: sink_silu(2 * blk, bank, m))
            run(steps)
            project_split(1, lambda tile, bank, m: sink_silu(2 * blk + 1, bank, m))
            steps = recurrence((2 * blk, 2 * blk + 1))
        run(steps)
        m_y = dve.mark()
        squares = SquaresOfX()
        layer.close()
        layer = ExitStack()
        start = []
        project_out(yT, BT, sb("y_lo", [P, BT, T], F32R, where=layer))
        rs_x = squares.rsqrt()

        layer.close()
        room = Room(uT[:, :, :].rearrange("p a b -> p (a b)"))
        hT = room.take(P, DK, T)
        o_buf = [room.take(P, D) for _ in range(TT)]
        start = join()
        m_h = normalise(("norm_f_w_2", 0), None, rs_x, start)
        out_store = Load(semaphore("out_store"))
        for t in range(TT):
            for j in range(0, DK, 4):
                b, bank, free = banks.take()
                for q in range(4):
                    m = transpose(free + [m_h], bank[:, q * P:(q + 1) * P], hT[:, j + q, t * P:(t + 1) * P])
                m = copy((act, dve)[j // 4], [m] + start, o_buf[t][:, j * P:(j + 4) * P], bank[:, :])
                banks.release(b, m)
            stored = out_store.start(act, [m, act.mark()], out[0][t * P:(t + 1) * P, :], o_buf[t])
        stores.append(stored)
        finish(join())


def packed_vectors(i):
    out = np.zeros((P, NVEC), np.float32)

    def put(name, value):
        a, n = VEC[name]
        out[:, a:a + n] = value

    for name in ("c", "b_ada", "norm_mix", "norm_ffn", "kv_norm", "conv_w", "conv_b", "ssm_norm", "norm_w_2",
                 "b_conv_w_2", "b_conv_b_2", "b_gate_a_b_2", "b_gate_x_b_2", "b_lambda_2", "norm_f_w_2"):
        put(name, np.asarray(i[name]).reshape(-1, P).T)
    for name in ("q_norm", "k_norm", "idx_k_ln_w", "idx_k_ln_b"):
        put(name, np.tile(np.asarray(i[name]).reshape(-1), 2)[:, None])
    put("d_skip", np.repeat(np.asarray(i["d_skip"]).reshape(-1), SP_).reshape(-1, P).T)
    for name in ("dt_bias", "a_log", "b_router"):
        put(name, np.broadcast_to(np.asarray(i[name]).reshape(1, -1), (P, VEC[name][1])))
    return out


_WEIGHTS = ["x", "rel_bias", "w_ada", "w_in", "w_kv_up", "w_attn_o", "w_ssm_o", "w_out", "w_router", "w_gu", "b_gu",
            "w_dn", "b_dn", "a_w_in_2", "a_ln_w_2", "a_ln_b_2", "a_w_s_2", "a_b_s_2", "a_w_out_2", "b_w_in_2",
            "b_gate_a_w_2", "b_gate_x_w_2", "b_w_out_2"]


def make(nc, inputs):
    arrays = {name: np.ascontiguousarray(inputs[name]) for name in _WEIGHTS}
    arrays["vec"] = packed_vectors(inputs)
    arrays["con"] = shape_constants()
    io = {n: nc.dram_tensor(f"in_{n}", a.shape, F32, kind="ExternalInput").ap() for n, a in arrays.items()}
    out = nc.dram_tensor("out_x", (1, T, D), F32, kind="ExternalOutput").ap()
    build(nc, io, out)
    return {f"in_{n}": a for n, a in arrays.items()}


def kernel(**inputs):
    import concourse.bacc as bacc
    from concourse.bass_utils import run_bass_kernel_spmd
    nc = bacc.Bacc("TRN2", target_bir_lowering=False, num_devices=1, dynamic_dma_scratch_size=8192)
    arrays = make(nc, inputs)
    return run_bass_kernel_spmd(nc, [arrays], core_ids=[0]).results[0]["out_x"]
```
